# Optimizing a Trainium2 kernel written in Bass

```python
import math
import jax, jax.numpy as jnp
from jax import lax
import numpy as np

D_MODEL = 2048
BATCH = 1
SEQ = 256
DEPTH = 1

CHUNK = 64
GDN_HEAD_DIM = 128
GDN_WIDTH = D_MODEL // 2
GDN_HEADS = GDN_WIDTH // GDN_HEAD_DIM
SC_WIDTH = D_MODEL - GDN_WIDTH
GDN_CONV = 4
SC_CONV = 3
FFN_CONV = 3
N_MEM = 256
XATTN_HEADS = 4
XATTN_HEAD_DIM = D_MODEL // XATTN_HEADS
D_FF = ((8 * D_MODEL // 3 + 255) // 256) * 256
N_MIX_IN = 4 * GDN_WIDTH + 2 * GDN_HEADS + 3 * SC_WIDTH
EPS = 1e-6


def rmsnorm(x, w):
    xf = x.astype(jnp.float32)
    y = xf * lax.rsqrt(jnp.mean(xf * xf, axis=-1, keepdims=True) + EPS)
    return (y * w.astype(jnp.float32)).astype(x.dtype)

def l2norm(x):
    return x * lax.rsqrt(jnp.sum(x * x, axis=-1, keepdims=True) + EPS)

def causal_dwconv(x, w):
    K = w.shape[0]
    S = x.shape[1]
    w = w.astype(x.dtype)
    xp = jnp.pad(x, ((0, 0), (K - 1, 0), (0, 0)))
    y = xp[:, 0:S] * w[0]
    for j in range(1, K):
        y = y + xp[:, j:j + S] * w[j]
    return y

def gated_delta_rule(q, k, v, g, beta):
    Bsz, S, H, DK = q.shape
    DV = v.shape[-1]
    N = S // CHUNK

    def to_chunks(t):
        t = t.reshape((Bsz, N, CHUNK, H) + t.shape[3:])
        return jnp.moveaxis(t, 3, 1)

    q, k, v, g, beta = (to_chunks(t) for t in (q, k, v, g, beta))
    q = q * (DK ** -0.5)
    g = jnp.cumsum(g, axis=-1)
    causal = jnp.tril(jnp.ones((CHUNK, CHUNK), dtype=bool))
    strict = jnp.tril(jnp.ones((CHUNK, CHUNK), dtype=bool), k=-1)
    decay = jnp.exp(jnp.where(causal, g[..., :, None] - g[..., None, :], -jnp.inf))
    k_beta = k * beta[..., None]
    a_strict = jnp.where(strict, jnp.einsum('bhncd,bhnmd->bhncm', k_beta, k) * decay, 0.0)
    eye = jnp.eye(CHUNK, dtype=jnp.float32)
    rhs = jnp.concatenate([v * beta[..., None], k_beta * jnp.exp(g)[..., None]], axis=-1)
    sol = lax.linalg.triangular_solve(eye + a_strict, rhs, left_side=True, lower=True,
                                      unit_diagonal=True)
    u, w = sol[..., :DV], sol[..., DV:]
    attn = jnp.einsum('bhncd,bhnmd->bhncm', q, k) * decay
    q_dec = q * jnp.exp(g)[..., None]
    g_last = g[..., -1]
    k_dec = k * jnp.exp(g_last[..., None] - g)[..., None]

    def step(state, xs):
        q_i, k_i, u_i, w_i, attn_i, gl_i = xs
        v_new = u_i - jnp.einsum('bhcd,bhde->bhce', w_i, state)
        o_i = (jnp.einsum('bhcd,bhde->bhce', q_i, state)
               + jnp.einsum('bhcm,bhme->bhce', attn_i, v_new))
        state = (state * jnp.exp(gl_i)[..., None, None]
                 + jnp.einsum('bhcd,bhce->bhde', k_i, v_new))
        return state, o_i

    xs = tuple(jnp.moveaxis(t, 2, 0) for t in (q_dec, k_dec, u, w, attn, g_last))
    state0 = jnp.zeros((Bsz, H, DK, DV), jnp.float32)
    _, o = lax.scan(step, state0, xs)
    return jnp.transpose(o, (1, 0, 3, 2, 4)).reshape(Bsz, S, H, DV)

def gdn_group(proj, conv_w, a_log, dt_bias, out_gain):
    Bsz, S, _ = proj.shape
    W, H, Dh = GDN_WIDTH, GDN_HEADS, GDN_HEAD_DIM
    qkv = jax.nn.silu(causal_dwconv(proj[..., :3 * W], conv_w)).astype(jnp.float32)
    q = l2norm(qkv[..., :W].reshape(Bsz, S, H, Dh))
    k = l2norm(qkv[..., W:2 * W].reshape(Bsz, S, H, Dh))
    v = qkv[..., 2 * W:].reshape(Bsz, S, H, Dh)
    z = proj[..., 3 * W:4 * W].reshape(Bsz, S, H, Dh)
    b_raw = proj[..., 4 * W:4 * W + H].astype(jnp.float32)
    a_raw = proj[..., 4 * W + H:4 * W + 2 * H].astype(jnp.float32)
    beta = jax.nn.sigmoid(b_raw)
    g = -jnp.exp(a_log.astype(jnp.float32)) * jax.nn.softplus(a_raw + dt_bias.astype(jnp.float32))
    o = gated_delta_rule(q, k, v, g, beta)
    o = rmsnorm(o, out_gain).astype(proj.dtype) * jax.nn.silu(z)
    return o.reshape(Bsz, S, W)

def shortconv_group(proj, conv_w):
    off = 4 * GDN_WIDTH + 2 * GDN_HEADS
    b_gate = proj[..., off:off + SC_WIDTH]
    c_gate = proj[..., off + SC_WIDTH:off + 2 * SC_WIDTH]
    h = proj[..., off + 2 * SC_WIDTH:off + 3 * SC_WIDTH]
    return b_gate * causal_dwconv(c_gate * h, conv_w)

def memory_xattn(h, mem_n, w_q, w_k, w_v, w_o):
    Bsz, S, _ = h.shape
    q = (h @ w_q).reshape(Bsz, S, XATTN_HEADS, XATTN_HEAD_DIM)
    k = (mem_n @ w_k).reshape(Bsz, N_MEM, XATTN_HEADS, XATTN_HEAD_DIM)
    v = (mem_n @ w_v).reshape(Bsz, N_MEM, XATTN_HEADS, XATTN_HEAD_DIM)
    s = jnp.einsum('bshd,bmhd->bhsm', q, k).astype(jnp.float32) * (XATTN_HEAD_DIM ** -0.5)
    p = jax.nn.softmax(s, axis=-1).astype(v.dtype)
    o = jnp.einsum('bhsm,bmhd->bshd', p, v).reshape(Bsz, S, D_MODEL)
    return o @ w_o

def conv_ffn(h, w_up, conv_w, w_down):
    u = causal_dwconv(h @ w_up, conv_w)
    gate, up = u[..., :D_FF], u[..., D_FF:]
    return (jax.nn.silu(gate) * up) @ w_down

def first_inputs(seed: int = 0) -> dict:
    key = jax.random.key(seed)
    ks = jax.random.split(key, 24)
    L, D = DEPTH, D_MODEL
    out_scale = (3 * DEPTH) ** -0.5

    def normal(k, shape, std):
        return jax.random.normal(k, shape, jnp.float32) * std

    def gain(k, shape):
        return 1.0 + normal(k, shape, 0.02)

    dt = jnp.exp(jax.random.uniform(ks[6], (L, GDN_HEADS), jnp.float32,
                                    math.log(1e-3), math.log(1e-1)))
    return {
        'x': normal(ks[0], (BATCH, SEQ, D), 1.0),
        'mem': normal(ks[1], (BATCH, N_MEM, D), 1.0),
        'mix_norm': gain(ks[2], (L, D)),
        'w_mix_in': normal(ks[3], (L, D, N_MIX_IN), D ** -0.5),
        'gdn_conv': normal(ks[4], (L, GDN_CONV, 3 * GDN_WIDTH), GDN_CONV ** -0.5),
        'gdn_a_log': jnp.log(jax.random.uniform(ks[5], (L, GDN_HEADS), jnp.float32, 1.0, 16.0)),
        'gdn_dt_bias': dt + jnp.log(-jnp.expm1(-dt)),
        'gdn_out_norm': gain(ks[7], (L, GDN_HEAD_DIM)),
        'sc_conv': normal(ks[8], (L, SC_CONV, SC_WIDTH), SC_CONV ** -0.5),
        'w_mix_out': normal(ks[9], (L, D, D), D ** -0.5 * out_scale),
        'xattn_norm': gain(ks[10], (L, D)),
        'mem_norm': gain(ks[11], (L, D)),
        'w_xq': normal(ks[12], (L, D, D), D ** -0.5),
        'w_xk': normal(ks[13], (L, D, D), D ** -0.5),
        'w_xv': normal(ks[14], (L, D, D), D ** -0.5),
        'w_xo': normal(ks[15], (L, D, D), D ** -0.5 * out_scale),
        'ffn_norm': gain(ks[16], (L, D)),
        'w_ffn_up': normal(ks[17], (L, D, 2 * D_FF), D ** -0.5),
        'ffn_conv': normal(ks[18], (L, FFN_CONV, 2 * D_FF), FFN_CONV ** -0.5),
        'w_ffn_down': normal(ks[19], (L, D_FF, D), D_FF ** -0.5 * out_scale),
        'final_norm': gain(ks[20], (D,)),
    }

def first_block(x, mem, mix_norm, w_mix_in, gdn_conv, gdn_a_log, gdn_dt_bias, gdn_out_norm,
              sc_conv, w_mix_out, xattn_norm, mem_norm, w_xq, w_xk, w_xv, w_xo,
              ffn_norm, w_ffn_up, ffn_conv, w_ffn_down, final_norm):
    for l in range(DEPTH):
        h = rmsnorm(x, mix_norm[l])
        proj = h @ w_mix_in[l]
        y_gdn = gdn_group(proj, gdn_conv[l], gdn_a_log[l], gdn_dt_bias[l], gdn_out_norm[l])
        y_sc = shortconv_group(proj, sc_conv[l])
        x = x + jnp.concatenate([y_gdn, y_sc], axis=-1) @ w_mix_out[l]
        h = rmsnorm(x, xattn_norm[l])
        mem_n = rmsnorm(mem, mem_norm[l])
        x = x + memory_xattn(h, mem_n, w_xq[l], w_xk[l], w_xv[l], w_xo[l])
        h = rmsnorm(x, ffn_norm[l])
        x = x + conv_ffn(h, w_ffn_up[l], ffn_conv[l], w_ffn_down[l])
    return rmsnorm(x, final_norm)


Q_BLOCK = 128
HEAD_WIDTH = 128
MLA_HEADS = (D_MODEL // 2) // HEAD_WIDTH
MLA_NOPE_DIM = 128
MLA_ROPE_DIM = 64
MLA_V_DIM = 128
MLA_QK_DIM = MLA_NOPE_DIM + MLA_ROPE_DIM
MLA_Q_RANK = 768
MLA_KV_RANK = 512
MLA_WIDTH = MLA_HEADS * MLA_V_DIM
FOX_HEADS = (D_MODEL // 2) // HEAD_WIDTH
FOX_HEAD_DIM = HEAD_WIDTH
FOX_WIDTH = FOX_HEADS * FOX_HEAD_DIM
D_MIX = MLA_WIDTH + FOX_WIDTH
ROPE_THETA = 10000.0
NORM_EPS = 1e-6
IN_SPLITS = (MLA_Q_RANK, MLA_KV_RANK, MLA_ROPE_DIM, MLA_WIDTH,
             FOX_WIDTH, FOX_WIDTH, FOX_WIDTH, FOX_HEADS, FOX_WIDTH)
D_IN = (MLA_Q_RANK + MLA_KV_RANK + MLA_ROPE_DIM + MLA_WIDTH
        + 4 * FOX_WIDTH + FOX_HEADS)


def _rms_norm(x, g):
    xf = x.astype(jnp.float32)
    y = xf * lax.rsqrt(jnp.mean(xf * xf, axis=-1, keepdims=True) + NORM_EPS)
    return (y * g.astype(jnp.float32)).astype(x.dtype)

def _rope_angles(positions, dim):
    inv_freq = ROPE_THETA ** (-jnp.arange(0, dim, 2, dtype=jnp.float32) / dim)
    ang = positions.astype(jnp.float32)[..., None] * inv_freq
    return jnp.cos(ang), jnp.sin(ang)

def _apply_rope(x, cos, sin):
    xf = x.astype(jnp.float32)
    half = xf.shape[-1] // 2
    x1, x2 = xf[..., :half], xf[..., half:]
    out = jnp.concatenate([x1 * cos - x2 * sin, x2 * cos + x1 * sin], axis=-1)
    return out.astype(x.dtype)

def _causal_block_sweep(score_fn, v):
    b, seq = v.shape[0], v.shape[1]
    n_blocks = seq // Q_BLOCK
    key_pos = jnp.arange(seq)

    def one_block(i):
        start = i * Q_BLOCK
        logits = score_fn(start)
        q_pos = start + jnp.arange(Q_BLOCK)
        logits = jnp.where(key_pos[None, :] <= q_pos[:, None], logits, -jnp.inf)
        p = jax.nn.softmax(logits, axis=-1).astype(v.dtype)
        return jnp.einsum('bhqs,bshd->bqhd', p, v)

    out = lax.map(one_block, jnp.arange(n_blocks))
    return out.transpose(1, 0, 2, 3, 4).reshape(b, seq, -1)

def _mla_branch(q_lat, kv_lat, k_rope_raw, g_q, w_uq, g_kv, w_ukv, cos, sin):
    b, s, _ = q_lat.shape
    q = (_rms_norm(q_lat, g_q) @ w_uq).reshape(b, s, MLA_HEADS, MLA_QK_DIM)
    q_nope = q[..., :MLA_NOPE_DIM]
    q_rope = _apply_rope(q[..., MLA_NOPE_DIM:], cos[:, :, None, :], sin[:, :, None, :])
    kv = (_rms_norm(kv_lat, g_kv) @ w_ukv).reshape(b, s, MLA_HEADS, MLA_NOPE_DIM + MLA_V_DIM)
    k_nope, v = kv[..., :MLA_NOPE_DIM], kv[..., MLA_NOPE_DIM:]
    k_rope = _apply_rope(k_rope_raw, cos, sin)
    scale = MLA_QK_DIM ** -0.5

    def score(start):
        qn = lax.dynamic_slice_in_dim(q_nope, start, Q_BLOCK, axis=1)
        qr = lax.dynamic_slice_in_dim(q_rope, start, Q_BLOCK, axis=1)
        s_nope = jnp.einsum('bqhd,bshd->bhqs', qn, k_nope, preferred_element_type=jnp.float32)
        s_rope = jnp.einsum('bqhr,bsr->bhqs', qr, k_rope, preferred_element_type=jnp.float32)
        return (s_nope + s_rope) * scale

    return _causal_block_sweep(score, v)

def _fox_branch(q, k, v, f_logit, b_forget):
    b, s, _ = q.shape
    q = q.reshape(b, s, FOX_HEADS, FOX_HEAD_DIM)
    k = k.reshape(b, s, FOX_HEADS, FOX_HEAD_DIM)
    v = v.reshape(b, s, FOX_HEADS, FOX_HEAD_DIM)
    log_f = jax.nn.log_sigmoid(f_logit.astype(jnp.float32) + b_forget.astype(jnp.float32))
    c = jnp.cumsum(log_f, axis=1).transpose(0, 2, 1)
    scale = FOX_HEAD_DIM ** -0.5

    def score(start):
        qb = lax.dynamic_slice_in_dim(q, start, Q_BLOCK, axis=1)
        cq = lax.dynamic_slice_in_dim(c, start, Q_BLOCK, axis=2)
        logits = jnp.einsum('bqhd,bshd->bhqs', qb, k, preferred_element_type=jnp.float32) * scale
        return logits + cq[:, :, :, None] - c[:, :, None, :]

    return _causal_block_sweep(score, v)

def _hybrid_layer(x, cos, sin, g_pre, w_in, g_q, w_uq, g_kv, w_ukv, b_forget, w_out, g_post):
    h = _rms_norm(x, g_pre)
    proj = h @ w_in
    split_points = np.cumsum(IN_SPLITS)[:-1].tolist()
    (q_lat, kv_lat, k_rope_raw, gate_mla,
     fq, fk, fv, f_logit, gate_fox) = jnp.split(proj, split_points, axis=-1)
    o_mla = _mla_branch(q_lat, kv_lat, k_rope_raw, g_q, w_uq, g_kv, w_ukv, cos, sin) * jax.nn.silu(gate_mla)
    o_fox = _fox_branch(fq, fk, fv, f_logit, b_forget) * jax.nn.silu(gate_fox)
    o = jnp.concatenate([o_mla, o_fox], axis=-1) @ w_out
    return x + _rms_norm(o, g_post)

def second_inputs(seed: int = 0) -> dict:
    key = jax.random.key(seed)
    ks = jax.random.split(key, 12)
    f32 = jnp.float32
    x = jax.random.normal(ks[0], (BATCH, SEQ, D_MODEL), f32)
    offsets = jax.random.randint(ks[1], (BATCH, 1), 0, 1024, dtype=jnp.int32)
    positions = jnp.arange(SEQ, dtype=jnp.int32)[None, :] + offsets
    g_pre = 1.0 + 0.02 * jax.random.normal(ks[2], (DEPTH, D_MODEL), f32)
    w_in = jax.random.normal(ks[3], (DEPTH, D_MODEL, D_IN), f32) * D_MODEL ** -0.5
    g_q_latent = 1.0 + 0.02 * jax.random.normal(ks[4], (DEPTH, MLA_Q_RANK), f32)
    w_uq = jax.random.normal(ks[5], (DEPTH, MLA_Q_RANK, MLA_HEADS * MLA_QK_DIM), f32) * MLA_Q_RANK ** -0.5
    g_kv_latent = 1.0 + 0.02 * jax.random.normal(ks[6], (DEPTH, MLA_KV_RANK), f32)
    w_ukv = jax.random.normal(ks[7], (DEPTH, MLA_KV_RANK, MLA_HEADS * (MLA_NOPE_DIM + MLA_V_DIM)), f32) * MLA_KV_RANK ** -0.5
    b_forget = 3.0 + 0.1 * jax.random.normal(ks[8], (DEPTH, FOX_HEADS), f32)
    w_out = jax.random.normal(ks[9], (DEPTH, D_MIX, D_MODEL), f32) * D_MIX ** -0.5
    g_post = 1.0 + 0.02 * jax.random.normal(ks[10], (DEPTH, D_MODEL), f32)
    return {"x": x, "positions": positions, "g_pre": g_pre, "w_in": w_in,
            "g_q_latent": g_q_latent, "w_uq": w_uq, "g_kv_latent": g_kv_latent,
            "w_ukv": w_ukv, "b_forget": b_forget, "w_out": w_out, "g_post": g_post}

def second_block(x, positions, g_pre, w_in, g_q_latent, w_uq, g_kv_latent, w_ukv, b_forget, w_out, g_post):
    cos, sin = _rope_angles(positions, MLA_ROPE_DIM)
    for l in range(DEPTH):
        x = _hybrid_layer(x, cos, sin, g_pre[l], w_in[l], g_q_latent[l], w_uq[l],
                          g_kv_latent[l], w_ukv[l], b_forget[l], w_out[l], g_post[l])
    return x


def setup_inputs(seed=0):
    out = dict(first_inputs(seed))
    for name, value in second_inputs(seed + 1).items():
        if name != "x":
            out[name + "_2"] = value
    return out


def reference(
    x, mem, mix_norm, w_mix_in, gdn_conv, gdn_a_log, gdn_dt_bias, gdn_out_norm, sc_conv,
    w_mix_out, xattn_norm, mem_norm, w_xq, w_xk, w_xv, w_xo, ffn_norm, w_ffn_up, ffn_conv,
    w_ffn_down, final_norm, positions_2, g_pre_2, w_in_2, g_q_latent_2, w_uq_2, g_kv_latent_2,
    w_ukv_2, b_forget_2, w_out_2, g_post_2,
):
    x = first_block(
        x, mem, mix_norm, w_mix_in, gdn_conv, gdn_a_log, gdn_dt_bias, gdn_out_norm, sc_conv,
        w_mix_out, xattn_norm, mem_norm, w_xq, w_xk, w_xv, w_xo, ffn_norm, w_ffn_up, ffn_conv,
        w_ffn_down, final_norm,
    )
    return second_block(
        x, positions_2, g_pre_2, w_in_2, g_q_latent_2, w_uq_2, g_kv_latent_2, w_ukv_2,
        b_forget_2, w_out_2, g_post_2,
    )


_drawn_inputs = setup_inputs


def setup_inputs(seed=0):
    import zlib

    import numpy as np

    out = dict(_drawn_inputs(seed))
    spreads = {}
    factors = {'gdn_out_norm': 7.736,
     'xattn_norm': 8.0,
     'mem_norm': 8.0,
     'ffn_norm': 4.529,
     'g_q_latent_2': 8.0,
     'g_kv_latent_2': 6.037,
     'g_post_2': 30.931,
     'b_forget_2': 64.0}
    for name, (base, spread) in spreads.items():
        noise = np.random.default_rng([zlib.crc32(name.encode()), seed]).standard_normal(out[name].shape)
        drawn = base * np.exp(spread * noise) if base else spread * noise
        out[name] = __import__('jax').numpy.asarray(drawn.astype(out[name].dtype))
    for name, factor in factors.items():
        out[name] = (out[name] * factor).astype(out[name].dtype)
    return out
```

```python
import concourse.bass as bass
from concourse import mybir
from contextlib import ExitStack
import numpy as np

F32 = mybir.dt.float32
F32R = mybir.dt.float32r
I32 = mybir.dt.int32
ALU = mybir.AluOpType
ACT = mybir.ActivationFunctionType
AX = mybir.AxisListType

P = 128
S = 256
D = 2048
KT = D // P
CHUNK = 128
NLEV = 7
GH = 8
XH = 4
FT = 5632 // P
SEGS = [16, 16, 12]
SLOTS = 4
BLK = 4
BW = 256
EPS = 1e-6
NEG = -1e30
MAGIC = 1.5 * 2.0 ** 23
TWO_PI = (6.28125, 0.0019350051879882812, 3.019916050561733e-07)


STREAM = ([("xk", 8, KT), ("xv", 8, KT), ("ba", 1, 8), ("qkv", 12, KT), ("gdn", 16, KT),
           ("mixo", 8, KT), ("xq", 8, KT), ("xo", 8, KT)]
          + [x for i, n in enumerate(SEGS) for x in ((f"up{i}", n, KT), (f"down{i}", 8, n))]
          + [("lat", 6, KT), ("gm", 4, KT), ("fox", 16, KT), ("uq", 6, 6), ("ukv", 8, 4),
             ("out", 8, KT)])
UNIT0, CHUNK0 = {}, {}
_u = _b = 0
for _name, _n, _k in STREAM:
    UNIT0[_name], CHUNK0[_name] = _u, _b // BLK
    _u += _n
    _b += _n * _k
N_CHUNKS = _b // BLK
assert _b % BLK == 0

COLS, _at = {}, 0
for _name, _n in (("mix", KT), ("xa", KT), ("mem", KT), ("ffn", KT), ("fin", KT), ("pre", KT),
                  ("post", KT), ("gq", 6), ("gkv", 4), ("ogain", 1), ("gconv", 24 * 4),
                  ("sconv", 8 * 3), ("fconv", 88 * 3), ("alog", 1), ("dtb", 1), ("bfor", 1)):
    COLS[_name] = _at
    _at += _n
N_COLS = _at
CST, _at = {}, 0
for _name, _n in (("ident", P), ("ones", P), ("causT", P), ("levT", NLEV * P), ("cmask", 2 * S),
                  ("head0", 1), ("head1", 1), ("eps", 1), ("invf", 1), ("sgn", 1), ("hpi", 1)):
    CST[_name] = _at
    _at += _n
N_CST = _at



HFILL, _h = {}, 0
for _name, _n in (("mem", KT), ("mix", KT), ("y", KT), ("xa", KT), ("o", KT), ("ffn", KT),
                  ("pre", KT), ("lat", 10), ("o2", KT)):
    HFILL[_name] = _h
    _h += _n
HFILL["gq"], HFILL["gkv"] = HFILL["lat"], HFILL["lat"] + 6
NORM, SQ0, TN0, _s, _t = {}, {}, {}, 0, 0
for _i, (_name, _n) in enumerate((("mem", 8), ("mix", 8), ("xa", 8), ("ffn", 8), ("fin", 8), ("pre", 8),
                                  ("gq", 3), ("gkv", 2), ("post", 8))):
    NORM[_name], SQ0[_name], TN0[_name] = _i + 1, _s, _t
    _s += 2 * _n - 1
    _t += 2 * _n if _name not in ("fin", "post") else 0
G_COL, B_COL, EG_COL, NBEG_COL, KD_ARG, KD_COL, EA_COL = 0, 16, 32, 40, 48, 50, 52
NMAX, RSUM, RINV, C_COL = 60, 64, 68, 72


def sl(start, n):
    return slice(start, start + n) if isinstance(start, int) else bass.ds(start, n)


def build_program(nc, wst, xT, memT, cols_d, cst_d, pos_d, out_d):
    ctx = ExitStack()
    with ctx:
        def at(name, kb, shape, dt=F32):
            return nc.alloc_sbuf_tensor_at(name, [P] + list(shape), dt, offset=16512 + int(kb * 1024))

        raw = at("raw", 0, [SLOTS, BLK * BW])
        w_hi = at("w_hi", 16, [SLOTS, BLK * BW], F32R)
        w_lo = at("w_lo", 32, [SLOTS, BLK * BW], F32R)
        h_hi = at("h_hi", 48, [KT, S], F32R)
        h_lo = at("h_lo", 64, [KT, S], F32R)
        x = at("x", 80, [KT, S])
        kx = at("kx", 96, [KT, S])
        vx = at("vx", 112, [2, D])
        qkv = at("qkv", 128, [24, S])
        y = at("y", 160, [KT, S])
        cst = at("cst", 176, [N_CST])
        cols = at("cols", 183.5, [N_COLS])
        tn = at("tn", 186, [4, S])
        rr = at("rr", 190, [S])
        sq = at("sq", 191, [2, S])
        acc = at("acc", 193, [2, S])
        cy = at("cy", 195, [2, S])
        cz = at("cz", 197, [2, S])
        cw = at("cw", 199, [2, S])
        cv = at("cv", 201, [2, S])
        rows = at("rows", 203, [4, S])
        sm = at("sm", 207, [160])
        qn, kn = at("qn", 80, [2, S]), at("kn", 82, [2, S])
        dec, aT, attT = at("dec", 84, [4, P]), at("aT", 86, [4, P]), at("attT", 88, [4, P])
        inv, invT, lv = at("inv", 90, [4, P]), at("invT", 92, [4, P]), at("lv", 94, [4, P])
        vs, zs, vb = at("vs", 152, [2, S]), at("zs", 154, [2, S]), at("vb", 156, [4, P])
        kd, qd = at("kd", 158, [2, P]), at("qd", 159, [2, P])
        vn, s1, r1 = at("vn", 186, [4, P]), at("s1", 188, [2, P]), at("r1", 189, [2, P])
        lp, osq = at("lp", 190, [4, P]), at("osq", 192, [2, S])
        xq = at("xq", 128, [4, S])
        vh = at("vh", 132, [2, 512])
        pr = at("pr", 136, [4, S])
        pT = at("pT", 140, [4, S])
        db = at("db", 144, [4, S])
        g_hi = at("g_hi", 96, [KT, S], F32R)
        g_lo = at("g_lo", 112, [KT, S], F32R)
        lat = at("lat", 96, [12, S])
        gmla = at("gmla", 108, [8, S])
        kr = at("kr", 116, [S])
        fq, fk = at("fq", 117, [2, S]), at("fk", 119, [2, S])
        fg, fv = at("fg", 121, [2, S]), at("fv", 123, [2, S])
        qnope, qrope = at("qnope", 148, [8, S]), at("qrope", 156, [4, S])
        knope, vm = at("knope", 125, [8, S]), at("vm", 117, [2, 1024])
        qmask = at("qmask", 197, [2, S])
        pos = at("pos", 137, [S], I32)
        cosr, sinr = at("cosr", 133, [S]), at("sinr", 134, [S])
        qm = at("qm", 135, [S])

        ident = cst[:, CST["ident"]:CST["ident"] + P]
        ones = cst[:, CST["ones"]:CST["ones"] + P]
        causT = cst[:, CST["causT"]:CST["causT"] + P]
        levT = cst[:, CST["levT"]:CST["levT"] + NLEV * P].rearrange("p (l m) -> p l m", l=NLEV)
        cmask = cst[:, CST["cmask"]:CST["cmask"] + 2 * S].rearrange("p (t m) -> p t m", t=2)

        def c1(name, parts=slice(0, P)):
            return cst[parts, CST[name]:CST[name] + 1]

        def col(name, i=0, parts=slice(0, P)):
            return cols[parts, sl(COLS[name] + i, 1)]

        bank = [ctx.enter_context(nc.psum_tensor(f"unit{i}", [P, 2, S], F32)) for i in range(2)]
        pb = [ctx.enter_context(nc.psum_tensor(f"pb{i}", [P, 2, S], F32)) for i in range(6)]
        pb4 = [b[:, :, :].rearrange("p a (b c) -> p (a b) c", b=2) for b in pb]

        sems = {}

        def sem(name):
            if name not in sems:
                sems[name] = ctx.enter_context(nc.semaphore(name))
            return sems[name]

        raw_ready = [sem(f"raw_ready{i}") for i in range(SLOTS)]
        hi_ready, lo_ready, w_used = sem("hi_ready"), sem("lo_ready"), sem("w_used")
        evacuated = sem("evacuated")
        h_ready = sem("h_ready")

        def loop(eng, n, body, first=False):
            if first:
                body(0)
            with eng.Fori(1 if first else 0, n) as it:
                body(it)

        block = ctx.enter_context(nc.Block())

        @block.sync
        def _(sp):
            sp.dma_start(x[:, :, :], memT).then_inc(sem("mem_in"), 16)
            for s in range(SLOTS):
                sp.dma_start(raw[:, s], wst[s]).then_inc(raw_ready[s], 16)
            with sp.Fori(1, N_CHUNKS // SLOTS) as it:
                for s in range(SLOTS):
                    sp.wait_ge(lo_ready, SLOTS * it + (s - SLOTS + 1))
                    sp.dma_start(raw[:, s], wst[SLOTS * it + s]).then_inc(raw_ready[s], 16)
            for c in range(N_CHUNKS // SLOTS * SLOTS, N_CHUNKS):
                sp.wait_ge(lo_ready, c - SLOTS + 1)
                sp.dma_start(raw[:, c % SLOTS], wst[c]).then_inc(raw_ready[c % SLOTS], 16)
            sp.wait_ge(sem("out_ready"), KT)
            sp.dma_start(out_d, x[:, :, :]).then_inc(sem("stored"), 16)
            sp.wait_ge(sem("stored"), 16)

        @block.gpsimd
        def _(pool):
            pool.dma_start(cst[:, :], cst_d).then_inc(sem("cst_in"), 16)
            pool.dma_start(cols[:, :], cols_d).then_inc(sem("cols_in"), 16)

            def sum_squares(name, src, ready, nt=8):
                done, s0 = sem("squares"), SQ0[name]
                ready(0)
                nc.gpsimd.tensor_tensor(acc[:, :, :], src(0), src(0), ALU.mult).then_inc(done, 1)
                with pool.Fori(1, nt) as j:
                    ready(j)
                    nc.gpsimd.tensor_tensor(sq[:, :, :], src(j), src(j), ALU.mult).then_inc(done, 1)
                    pool.wait_ge(done, 2 * j + s0)
                    nc.gpsimd.tensor_tensor(acc[:, :, :], acc[:, :, :], sq[:, :, :], ALU.add)\
                        .then_inc(done, 1)
                    pool.wait_ge(done, 2 * j + (s0 + 1))

            def pair(t, first=0):
                return lambda j: t[:, sl(2 * j + first, 2), :]

            sum_squares("mem", pair(x), lambda j: pool.wait_ge(sem("mem_in"), 16))
            pool.wait_ge(h_ready, HFILL["mem"] + KT)
            pool.dma_start(x[:, :, :], xT).then_inc(sem("x_in"), 16)
            sum_squares("mix", pair(x), lambda j: pool.wait_ge(sem("x_in"), 16))

            pool.wait_ge(sem("qkv_ready"), 12)
            def copy_v(it):
                if not isinstance(it, int):
                    pool.wait_ge(sem("kv_token_major"), it)
                nc.gpsimd.tensor_copy(vs[:, :, :], qkv[:, sl(2 * it + 16, 2), :]).then_inc(sem("vs_ready"), 1)
            loop(pool, 4, copy_v, first=True)

            pool.wait_ge(sem("gdn_y"), 8)
            pool.dma_start(x[:, :, :], xT).then_inc(sem("x_again"), 16)
            sum_squares("xa", pair(x), lambda j: pool.wait_ge(evacuated, j + (UNIT0["mixo"] + 1)))

            def copy_vh(h):
                if not isinstance(h, int):
                    pool.wait_ge(sem("xa_pv"), h)
                nc.gpsimd.tensor_copy(vh[:, :, :], vx[:, :, sl(512 * h, 512)]).then_inc(sem("vh_ready"), 1)
            loop(pool, XH, copy_vh, first=True)
            sum_squares("ffn", pair(x), lambda j: pool.wait_ge(evacuated, j + (UNIT0["xo"] + 1)))
            pool.wait_ge(sem("xa_o"), 2 * XH)
            pool.dma_start(pos[:, :], pos_d.partition_broadcast(P)).then_inc(sem("pos_in"), 16)
            sum_squares("fin", pair(x), lambda j: pool.wait_ge(evacuated, j + (UNIT0["down2"] + 1)))
            sum_squares("pre", pair(x), lambda j: pool.wait_ge(sem("x_final"), 2 * j + 2))
            sum_squares("gq", pair(lat), lambda j: pool.wait_ge(evacuated, j + (UNIT0["lat"] + 1)), nt=3)
            pool.wait_ge(sem("rsqrt_ready"), NORM["gq"])
            sum_squares("gkv", pair(lat, 6), lambda j: pool.wait_ge(evacuated, j + (UNIT0["lat"] + 4)), nt=2)
            sum_squares("post", pair(y), lambda j: pool.wait_ge(evacuated, j + (UNIT0["out"] + 1)))

        @block.tensor
        def _(pe):
            def mm(out, lhsT, rhs, start=True, stop=True):
                return nc.tensor.matmul(out, lhsT, rhs, start=start, stop=stop, skip_group_check=True)

            def turn(out, in_, idn):
                return nc.tensor.transpose(out, in_, idn)

            def unit(name, it, n, j, K=KT, tokens=False, src=None, hwait=None, step=None,
                     narrow=False, hoff=0):
                hi, lo = src or (h_hi, h_lo)
                u = UNIT0[name] + j
                blk0 = j * K if isinstance(it, int) and it == 0 else j * K
                if isinstance(it, int):
                    blk0 += it * n * K
                    if UNIT0[name] + n * it + j >= 2:
                        pe.wait_ge(evacuated, UNIT0[name] + n * it + j - 1)
                else:
                    pe.wait_ge(evacuated, n * it + (u - 1))
                per = 0 if isinstance(it, int) else n * K // BLK
                for k in range(K):
                    blk = blk0 + (k // 2 if narrow else k)
                    half = (k % 2) * P if narrow else 0
                    c, sub = CHUNK0[name] + blk // BLK, blk % BLK
                    w0 = sub * BW + half
                    slot = c % SLOTS
                    if (sub == 0 or k == 0) and half == 0:
                        pe.wait_ge(lo_ready, per * it + (c + 1))
                    if hwait is not None:
                        pe.wait_ge(h_ready, hwait + k + 1)
                    for t in range(1 if narrow else 2):
                        o = bank[(UNIT0[name] + j + (n * it if isinstance(it, int) else 0)) % 2][:, t, :]
                        if tokens:
                            wh, wl = w_hi[:, slot, w0:w0 + BW], w_lo[:, slot, w0:w0 + BW]
                            ah = hi[:, hoff + k, t * P:(t + 1) * P]
                            al = lo[:, hoff + k, t * P:(t + 1) * P]
                            mm(o, ah, wh, k == 0 and t == 0, False)
                            mm(o, al, wh, False, False)
                            last = mm(o, ah, wl, False, k == K - 1)
                        else:
                            wh = w_hi[:, slot, w0 + t * P:w0 + (t + 1) * P]
                            wl = w_lo[:, slot, w0 + t * P:w0 + (t + 1) * P]
                            mm(o, wh, hi[:, hoff + k, :], k == 0 and t == 0, False)
                            mm(o, wh, lo[:, hoff + k, :], False, False)
                            last = mm(o, wl, hi[:, hoff + k, :], False, k == K - 1)
                    if sub == BLK - 1 and (not narrow or half):
                        last.then_inc(w_used, 1)
                    elif k == K - 1:
                        last.then_inc(sem("mid_chunk"), 1)
                    if step is not None and sub % 2 == 1:
                        step(K // BLK * 2 * j + k // 2)

            def norm_sum(name, nt=8):
                pe.wait_ge(sem("squares"), SQ0[name] + 2 * nt - 1)
                if NORM[name] > 1:
                    pe.wait_ge(sem("rms_ready"), NORM[name] - 1)
                mm(pb[5][:, 0, :], ones, acc[:, 0, :], True, False)
                mm(pb[5][:, 0, :], ones, acc[:, 1, :], False, True).then_inc(sem("norm_sum"), 1)

            def gdn(g, it):
                if g == 0:
                    pe.wait_ge(sem("qk_squares"), 2 * it + 2)
                    mm(pb4[0], ones, dec[:, :, :])
                    mm(pb4[1], ones, aT[:, :, :]).then_inc(sem("qk_sums"), 1)
                elif g == 1:
                    pe.wait_ge(sem("qk_normed"), 2 * it + 2)
                    for b in range(4):
                        kb = kn[:, b // 2, (b % 2) * P:(b % 2 + 1) * P]
                        mm(pb4[0][:, b], kb, kb)
                    for b in range(4):
                        kb, qb = (t[:, b // 2, (b % 2) * P:(b % 2 + 1) * P] for t in (kn, qn))
                        last = mm(pb4[1][:, b], kb, qb)
                    last.then_inc(sem("grams"), 1)
                elif g == 2:
                    pe.wait_ge(sem("head_rows"), 4 * it + 4)
                    mm(pb4[2], ones[0:8, :], rows[0:8, 2:4, :].rearrange("p a b -> p (a b)"))
                    mm(pb4[3], ones[32:40, :], rows[32:40, 2:4, :].rearrange("p a b -> p (a b)"))\
                        .then_inc(sem("rows_spread"), 1)
                    for i in range(2):
                        turn(pb4[4][:, i], kn[:, i, 0:P], ident)
                    pe.wait_ge(sem("vs_ready"), it + 1)
                    for b in range(4):
                        last = turn(pb4[5][:, b], vs[:, b // 2, (b % 2) * P:(b % 2 + 1) * P], ident)
                    last.then_inc(sem("kv_token_major"), 1)
                elif g == 3:
                    pe.wait_ge(sem("inv0_ready"), it + 1)
                    for b in range(4):
                        last = turn(pb4[0][:, b], invT[:, b], ident)
                    last.then_inc(sem("inv0_turned"), 1)
                elif g < 16 and g % 2 == 0:
                    l = (g - 4) // 2
                    pe.wait_ge(sem("level_part"), 6 * it + (l + 1))
                    if l == 0:
                        pe.wait_ge(sem("inv0_copied"), it + 1)
                    else:
                        pe.wait_ge(sem("inv_updated"), 11 * it + 2 * l)
                    for b in range(4):
                        last = mm(pb4[1][:, b], lv[:, b], inv[:, b])
                    last.then_inc(sem("level_product"), 1)
                elif g < 16:
                    l = (g - 5) // 2
                    pe.wait_ge(sem("level_copied"), 6 * it + (l + 1))
                    if l < 5:
                        for b in range(4):
                            mm(pb4[2][:, b], invT[:, b], lp[:, b])
                    for b in range(4):
                        last = mm(pb4[3][:, b], lp[:, b], invT[:, b])
                    last.then_inc(sem("level_update"), 1)
                elif g == 16:
                    pe.wait_ge(sem("inv_updated"), 11 * it + 11)
                    pe.wait_ge(sem("kv_scaled"), 6 * it + 6)
                    for i in range(2):
                        last = mm(pb4[0][:, i], invT[:, 2 * i], vb[:, 2 * i])
                    last.then_inc(sem("new0"), 1)
                elif g == 17:
                    pe.wait_ge(sem("new_copied"), 2 * it + 1)
                    for i in range(2):
                        last = mm(pb4[1][:, i], kd[:, i], vn[:, 2 * i])
                    last.then_inc(sem("state"), 1)
                elif g == 18:
                    pe.wait_ge(sem("state_copied"), it + 1)
                    for i in range(2):
                        last = mm(pb4[2][:, i], kn[:, i, P:2 * P], s1[:, i])
                    last.then_inc(sem("k_state"), 1)
                elif g == 19:
                    pe.wait_ge(sem("rest_ready"), 2 * it + 2)
                    for i in range(2):
                        last = mm(pb4[3][:, i], invT[:, 2 * i + 1], r1[:, i])
                    last.then_inc(sem("new1"), 1)
                elif g == 20:
                    pe.wait_ge(sem("new_copied"), 2 * it + 2)
                    pe.wait_ge(sem("att_ready"), 3 * it + 3)
                    for b in range(4):
                        last = mm(pb4[4][:, b], vn[:, b], attT[:, b], True, b % 2 == 0)
                        if b % 2:
                            last = mm(pb4[4][:, b], s1[:, b // 2], qd[:, b // 2], False, True)
                    last.then_inc(sem("gdn_out"), 1)
                elif g == 21:
                    pe.wait_ge(sem("out_squares"), it + 1)
                    mm(pb[5][:, :, :], ones, osq[:, :, :]).then_inc(sem("out_sums"), 1)

            def xa(a, h):
                if a == 0:
                    pe.wait_ge(evacuated, 2 * h + (UNIT0["xq"] + 2))
                    for t in range(2):
                        for kk in range(4):
                            last = mm(pb[0][:, t, :], xq[:, kk, t * P:(t + 1) * P],
                                      kx[:, sl(4 * h + kk, 1), :], kk == 0, kk == 3)
                    last.then_inc(sem("xa_scores"), 1)
                elif a == 1:
                    pe.wait_ge(sem("xa_prob"), 2 * h + 2)
                    for t in range(2):
                        for m in range(2):
                            last = turn(pb[1][:, m, t * P:(t + 1) * P], pr[:, t, m * P:(m + 1) * P], ident)
                    last.then_inc(sem("xa_turned"), 1)
                else:
                    pe.wait_ge(sem("xa_prob_copied"), h + 1)
                    pe.wait_ge(sem("vh_ready"), h + 1)
                    for jj in range(4):
                        for m in range(2):
                            last = mm(pb[2 + jj // 2][:, jj % 2, :], vh[:, m, jj * P:(jj + 1) * P],
                                      pT[:, m, :], m == 0, m == 1)
                    last.then_inc(sem("xa_pv"), 1)

            def ca(a, n, p=None):
                if a == 0:
                    if p is None:
                        pe.wait_ge(sem("forget_rows"), 2 * n + 2)
                        mm(pb4[2], ones[0:8, :], rows[0:8, 2:4, :].rearrange("p a b -> p (a b)"))
                        for i in range(2):
                            for t in range(2):
                                last = mm(pb[i][:, t, :], fq[:, i, t * P:(t + 1) * P], fk[:, i, :])
                    else:
                        pe.wait_ge(sem("mla_q_masked"), 2 * p + 2)
                        for i in range(2):
                            for t in range(2):
                                q = slice(t * P, (t + 1) * P)
                                mm(pb[i][:, t, :], qnope[:, 2 * p + i, q], knope[:, 2 * p + i, :], True, False)
                                last = mm(pb[i][:, t, :], qmask[:, i, q], kr[:, :], False, True)
                    last.then_inc(sem("ca_scores"), 1)
                elif a == 1:
                    pe.wait_ge(sem("ca_prob"), 4 * n + 4)
                    for i in range(2):
                        for t in range(2):
                            for m in range(2):
                                last = turn(pb[3 + i][:, m, t * P:(t + 1) * P],
                                            pr[:, 2 * i + t, m * P:(m + 1) * P], ident)
                    last.then_inc(sem("ca_turned"), 1)
                else:
                    pe.wait_ge(sem("ca_prob_copied"), 2 * n + 2)
                    for i in range(2):
                        for m in range(2):
                            v = fv[:, m, i * P:(i + 1) * P] if p is None else \
                                vm[:, m, (2 * p + i) * P:(2 * p + i + 1) * P]
                            last = mm(pb[5][:, i, :], v, pT[:, 2 * i + m, :], m == 0, m == 1)
                    last.then_inc(sem("ca_pv"), 1)

            pe.wait_ge(sem("cst_in"), 16)
            norm_sum("mem")

            def xk(it):
                for j in range(2):
                    unit("xk", it, 2, j, hwait=HFILL["mem"] if j == 0 else None)
            xk(0)
            with pe.Fori(1, 4) as it:
                xk(it)

            with pe.Fori(0, 4) as it:
                for j in range(2):
                    unit("xv", it, 2, j, tokens=True)

            norm_sum("mix")
            unit("ba", 0, 1, 0, K=KT, narrow=True, hwait=HFILL["mix"])
            with pe.Fori(0, 6) as it:
                for j in range(2):
                    unit("qkv", it, 2, j)
            pe.wait_ge(sem("ba_dve"), 6)
            pe.wait_ge(sem("ba_act"), 4)
            for n in range(2):
                g_last = turn(pb[5][:, 0, 8 * n:8 * n + 8], rows[0:8, 0, n * P:(n + 1) * P], ident[0:8, 0:8])
            g_last.then_inc(sem("ba_cols"), 1)
            for n in range(2):
                last = turn(pb[4][:, 0, 8 * n:8 * n + 8], rows[32:40, 0, n * P:(n + 1) * P],
                            ident[32:40, 32:40])
            last.then_inc(sem("ba_cols"), 1)
            with pe.Fori(0, 4) as it:
                for j in range(4):
                    def step(s):
                        if s < 22:
                            gdn(s, it)
                    unit("gdn", it, 4, j, step=step)

            with pe.Fori(0, 4) as it:
                for j in range(2):
                    unit("mixo", it, 2, j, hwait=HFILL["y"] if j == 0 else None)
            norm_sum("xa")

            def xq_units(it):
                def step(s):
                    if isinstance(it, int):
                        return
                    if s == 0:
                        xa(0, it - 1)
                    elif s == 5:
                        xa(1, it - 1)
                    elif s == 9:
                        xa(2, it - 1)
                for j in range(2):
                    unit("xq", it, 2, j, hwait=HFILL["xa"] if j == 0 else None, step=step)
            xq_units(0)
            with pe.Fori(1, 4) as it:
                xq_units(it)
            for a in range(3):
                xa(a, XH - 1)

            with pe.Fori(0, 4) as it:
                for j in range(2):
                    unit("xo", it, 2, j, hwait=HFILL["o"] if j == 0 else None)
            norm_sum("ffn")
            for s, nt in enumerate(SEGS):
                with pe.Fori(0, nt // 2) as it:
                    for j in range(2):
                        unit(f"up{s}", it, 2, j, hwait=HFILL["ffn"] if j == 0 and s == 0 else None)
                pe.wait_ge(sem("g_ready"), sum(SEGS[:s + 1]) // 2)
                with pe.Fori(0, 2) as it:
                    for j in range(4):
                        unit(f"down{s}", it, 4, j, K=nt, src=(g_hi, g_lo))
            norm_sum("fin")
            norm_sum("pre")
            with pe.Fori(0, 3) as it:
                for j in range(2):
                    unit("lat", it, 2, j, hwait=HFILL["pre"] if j == 0 else None)
            with pe.Fori(0, 2) as it:
                for j in range(2):
                    unit("gm", it, 2, j)
            pe.wait_ge(sem("forget_dve"), 6)
            for n in range(2):
                last = turn(pb[5][:, 0, 8 * n:8 * n + 8], rows[0:8, 0, n * P:(n + 1) * P], ident[0:8, 0:8])
            last.then_inc(sem("forget_cols"), 1)

            def fox(it):
                def step(s):
                    if isinstance(it, int):
                        return
                    if s == 1:
                        ca(0, it - 1)
                    elif s == 9:
                        ca(1, it - 1)
                    elif s == 14:
                        ca(2, it - 1)
                for j in range(4):
                    unit("fox", it, 4, j, tokens=j == 3, step=step)
            fox(0)
            with pe.Fori(1, 4) as it:
                fox(it)
            for a in range(3):
                ca(a, 3)
            pe.wait_ge(sem("ca_o"), 4)
            norm_sum("gq", 3)
            norm_sum("gkv", 2)
            for u in range(6):
                unit("uq", 0, 6, u, K=6, hwait=HFILL["lat"] if u == 0 else None)
            for u in range(8):
                unit("ukv", 0, 8, u, K=4, tokens=u >= 4, hoff=6,
                     hwait=HFILL["lat"] + 6 if u == 0 else None)
            for p in range(4):
                for a in range(3):
                    ca(a, 4 + p, p)
            with pe.Fori(0, 4) as it:
                for j in range(2):
                    unit("out", it, 2, j, hwait=HFILL["o2"] if j == 0 else None)
            norm_sum("post")

        pair4 = "p (a b) c -> p a (b c)"

        def smc(c, n=1):
            return sm[:, sl(c, n)]

        @block.scalar
        def _(act):
            def A(out, in_, func, bias=0.0, scale=1.0, **kw):
                return nc.scalar.activation(out, in_, func, bias=bias, scale=scale, **kw)

            def split(c, per=0, it=0):
                if isinstance(it, int):
                    c, it, per = c + per * it, 0, 0
                    if c >= N_CHUNKS:
                        return
                s = c % SLOTS
                act.wait_ge(raw_ready[s], 16 * per // SLOTS * it + 16 * (c // SLOTS + 1))
                if c >= SLOTS:
                    act.wait_ge(w_used, per * it + (c - SLOTS + 1))
                A(w_hi[:, s], raw[:, s], ACT.Copy).then_inc(hi_ready, 1)

            def units(name, it, n, evac=None, react=None, K=KT, j0=0):
                m = n * K // BLK
                for j in range(j0, n):
                    for i in range(K // BLK):
                        if react is not None:
                            react(j, i)
                        if i == K // BLK - 1 and evac is not None:
                            evac(j)
                        split(CHUNK0[name] + j * K // BLK + i + SLOTS, m, it)

            def done(name, it, n, j, K=KT):
                act.wait_ge(w_used, n * K // BLK * it + (CHUNK0[name] + (j + 1) * K // BLK))

            def norm_rms(name, width):
                act.wait_ge(sem("norm_sum"), NORM[name])
                A(rr[:, :], pb[5][:, 0, :], ACT.Sqrt, bias=c1("eps"), scale=1.0 / width)\
                    .then_inc(sem("rms_ready"), 1)

            def norm_hi(name, nt=KT, h0=0):
                for k in range(nt):
                    act.wait_ge(sem("tn_ready"), TN0[name] + k + 1)
                    A(h_hi[:, h0 + k], tn[:, k % 4], ACT.Copy).then_inc(sem("h_hi_ready"), 1)

            def split_h(name, src):
                for k in range(KT):
                    A(h_hi[:, k], src[:, k], ACT.Copy).then_inc(sem("h_hi_ready"), 1)

            for c in range(SLOTS):
                split(c)
            act.wait_ge(sem("cst_in"), 16)
            act.wait_ge(sem("cols_in"), 16)
            norm_rms("mem", D)
            norm_hi("mem")
            with act.Fori(0, 4) as it:
                units("xk", it, 2)
            with act.Fori(0, 4) as it:
                units("xv", it, 2)

            norm_rms("mix", D)
            act.wait_ge(w_used, CHUNK0["ba"])
            norm_hi("mix")
            split(CHUNK0["ba"] + SLOTS)
            act.wait_ge(evacuated, UNIT0["ba"] + 1)
            r = rows
            A(r[0:8, 2], r[0:8, 1], ACT.Abs, bias=col("dtb", 0, slice(0, 8))).then_inc(sem("ba_act"), 1)
            A(r[32:40, 0], r[32:40, 1], ACT.Sigmoid).then_inc(sem("ba_act"), 1)
            A(sm[0:8, EA_COL:EA_COL + 1], col("alog", 0, slice(0, 8)), ACT.Exp).then_inc(sem("ba_act"), 1)
            act.wait_ge(sem("ba_act"), 1)
            A(r[0:8, 2], r[0:8, 2], ACT.Exp, scale=-1.0).then_inc(sem("ba_act"), 1)
            split(CHUNK0["ba"] + SLOTS + 1)
            act.wait_ge(sem("ba_dve"), 1)
            A(r[0:8, 2], r[0:8, 2], ACT.Ln).then_inc(sem("ba_act"), 1)

            def qkv_body(it):
                def evac(j):
                    done("qkv", it, 2, j)
                    b = bank[(UNIT0["qkv"] + j) % 2]
                    c = (cy, cz)[j]
                    for t in range(2):
                        A(c[:, t], b[:, t], ACT.Copy, scale=col("gconv", 24 * 3 + (4 * it + (2 * j + t))))\
                            .then_inc(sem("qkv_tap0"), 1)
                    act.wait_ge(evacuated, 2 * it + (UNIT0["qkv"] + j + 1))
                    A(qkv[:, sl(4 * it + 2 * j, 2)], c[:, :], ACT.Silu).then_inc(sem("qkv_ready"), 1)
                units("qkv", it, 2, evac)
            with act.Fori(0, 6) as it:
                qkv_body(it)

            act.wait_ge(sem("ba_dve"), 7)
            A(smc(EG_COL, 8), smc(G_COL + 8, 8), ACT.Exp).then_inc(sem("ba_act"), 1)

            def gdn(g, it):
                if g == 0:
                    A(dec[:, :, :], qkv[:, sl(2 * it, 2)].rearrange("p a (b c) -> p (a b) c", b=2), ACT.Square)\
                        .then_inc(sem("qk_squares"), 1)
                    A(aT[:, :, :], qkv[:, sl(2 * it + 8, 2)].rearrange("p a (b c) -> p (a b) c", b=2), ACT.Square)\
                        .then_inc(sem("qk_squares"), 1)
                    act.wait_ge(sem("qk_sums"), it + 1)
                    A(inv[:, :, :], pb4[0], ACT.Sqrt, bias=c1("eps")).then_inc(sem("qk_rms"), 1)
                    A(invT[:, :, :], pb4[1], ACT.Sqrt, bias=c1("eps")).then_inc(sem("qk_rms"), 1)
                elif g == 2:
                    act.wait_ge(sem("dec_args"), 6 * it + 6)
                    A(dec[:, :, :], dec[:, :, :], ACT.Exp).then_inc(sem("dec_ready"), 1)
                    A(qd[:, :, :], pb4[2].rearrange("p (i n) c -> p n i c", n=2)[:, 1], ACT.Exp)\
                        .then_inc(sem("q_decay"), 1)
                    A(smc(KD_COL, 2), smc(KD_ARG, 2), ACT.Exp).then_inc(sem("k_decay"), 1)
                    act.wait_ge(sem("kv_token_major"), it + 1)
                    for b in range(4):
                        A(vb[:, b], pb4[5][:, b], ACT.Copy, scale=smc(B_COL + (b % 2) * 8 + b // 2 + 2 * it))\
                            .then_inc(sem("kv_scaled"), 1)
                    act.wait_ge(sem("k_decay"), it + 1)
                    for i in range(2):
                        A(kd[:, i], pb4[4][:, i], ACT.Copy, scale=smc(KD_COL + i)).then_inc(sem("kv_scaled"), 1)
                elif g == 3:
                    act.wait_ge(sem("inv0_turned"), it + 1)
                    A(inv[:, :, :], pb4[0], ACT.Copy).then_inc(sem("inv0_copied"), 1)
                elif 4 <= g < 16 and g % 2 == 0:
                    act.wait_ge(sem("level_product"), 6 * it + ((g - 4) // 2 + 1))
                    A(lp[:, :, :], pb4[1], ACT.Copy).then_inc(sem("level_copied"), 1)
                elif g in (16, 19):
                    n = (g - 16) // 3
                    act.wait_ge(sem(f"new{n}"), it + 1)
                    A(vn[:, :, :].rearrange("p (i n) c -> p n i c", n=2)[:, n], pb4[3 * n][:, 0:2], ACT.Copy)\
                        .then_inc(sem("new_copied"), 1)
                elif g == 17:
                    act.wait_ge(sem("state"), it + 1)
                    A(s1[:, :, :], pb4[1][:, 0:2], ACT.Copy).then_inc(sem("state_copied"), 1)
                elif g == 20:
                    act.wait_ge(sem("gdn_out"), it + 1)
                    A(osq[:, :, :], pb[4][:, :, :], ACT.Square).then_inc(sem("out_squares"), 1)
                elif g == 21:
                    act.wait_ge(sem("out_sums"), it + 1)
                    A(osq[:, :, :], pb[5][:, :, :], ACT.Sqrt, bias=c1("eps"), scale=1.0 / P)\
                        .then_inc(sem("out_rms"), 1)

            act.wait_ge(sem("qkv_ready"), 12)
            with act.Fori(0, 4) as it:
                def react(j, i):
                    for g in (8 * j + 2 * i, 8 * j + 2 * i + 1):
                        if g < 22:
                            gdn(g, it)

                def evac(j):
                    if j == 0:
                        act.wait_ge(evacuated, 4 * it + (UNIT0["gdn"] + 1))
                        A(zs[:, :], zs[:, :], ACT.Silu).then_inc(sem("z_ready"), 1)
                    elif j == 3:
                        act.wait_ge(evacuated, 4 * it + (UNIT0["gdn"] + 4))
                        for t in range(2):
                            A(cv[:, t], cw[:, t], ACT.Copy, scale=col("sconv", 8 * 2 + (2 * it + t)))\
                                .then_inc(sem("sc_tap0"), 1)
                units("gdn", it, 4, evac, react)

            act.wait_ge(sem("gdn_y"), 8)
            act.wait_ge(sem("sc_y"), 4)
            act.wait_ge(w_used, CHUNK0["mixo"])
            split_h("y", y)
            with act.Fori(0, 4) as it:
                units("mixo", it, 2)
            norm_rms("xa", D)
            act.wait_ge(w_used, CHUNK0["xq"])
            norm_hi("xa")

            XSC = 512 ** -0.5

            def xa(a, h):
                if a == 0:
                    act.wait_ge(sem("xa_nmax"), 2 * h + 2)
                    for t in range(2):
                        A(pr[:, t], pb[0][:, t], ACT.Exp, bias=smc(NMAX + t), scale=XSC,
                          accum_out=smc(RSUM + t)).then_inc(sem("xa_exp"), 1)
                elif a == 1:
                    act.wait_ge(sem("xa_turned"), h + 1)
                    A(pT[:, 0:2], pb[1][:, :, :], ACT.Copy).then_inc(sem("xa_prob_copied"), 1)

            with act.Fori(0, 1) as it:
                units("xq", 0, 2)
            with act.Fori(1, 4) as it:
                def react(j, i):
                    if (j, i) == (0, 0):
                        xa(0, it - 1)
                    elif (j, i) == (0, 2):
                        xa(1, it - 1)
                units("xq", it, 2, react=react)
            xa(0, XH - 1)
            xa(1, XH - 1)
            act.wait_ge(sem("xa_o"), 2 * XH)
            split_h("o", y)
            with act.Fori(0, 4) as it:
                units("xo", it, 2)
            norm_rms("ffn", D)
            act.wait_ge(w_used, CHUNK0["up0"])
            norm_hi("ffn")
            tile0 = 0
            for s, nt in enumerate(SEGS):
                name = f"up{s}"
                g0 = sum(SEGS[:s]) // 2
                with act.Fori(0, nt // 2) as it:
                    def evac(j):
                        done(name, it, 2, j)
                        b = bank[(UNIT0[name] + j) % 2]
                        c = (cy, cw)[j]
                        for t in range(2):
                            A(c[:, t], b[:, t], ACT.Copy,
                              scale=col("fconv", 88 * 2 + 44 * j + tile0 + t + 2 * it)).then_inc(sem("up_tap0"), 1)
                        act.wait_ge(evacuated, 2 * it + (UNIT0[name] + j + 1))
                        if j == 0:
                            A(cz[:, :], cy[:, :], ACT.Silu).then_inc(sem("gate_ready"), 1)
                        else:
                            act.wait_ge(sem("gated"), it + (g0 + 1))
                            A(g_hi[:, sl(2 * it, 2)], cv[:, :], ACT.Copy).then_inc(sem("g_hi_ready"), 1)
                    units(name, it, 2, evac)
                tile0 += nt
                with act.Fori(0, 2) as it:
                    units(f"down{s}", it, 4, K=nt)
                act.wait_ge(w_used, CHUNK0[f"down{s}"] + 2 * nt)
            norm_rms("fin", D)
            norm_rms("pre", D)
            act.wait_ge(w_used, CHUNK0["lat"])
            norm_hi("pre")
            act.wait_ge(sem("rope_dve"), 8)
            A(qm[:, :], sinr[:, :], ACT.Abs).then_inc(sem("rope_act"), 1)
            A(sinr[:, :], sinr[:, :], ACT.Sin).then_inc(sem("rope_act"), 1)
            act.wait_ge(sem("rope_act"), 1)
            A(cosr[:, :], qm[:, :], ACT.Sin, bias=c1("hpi"), scale=-1.0).then_inc(sem("rope_act"), 1)
            with act.Fori(0, 3) as it:
                units("lat", it, 2)
            act.wait_ge(evacuated, UNIT0["lat"] + 6)
            A(qm[0:64, :], lat[64:128, 10], ACT.Copy).then_inc(sem("kr_swap"), 1)
            A(qm[64:128, :], lat[0:64, 10], ACT.Copy).then_inc(sem("kr_swap"), 1)
            A(r[0:8, 2], lat[0:8, 11], ACT.Abs, bias=col("bfor", 0, slice(0, 8))).then_inc(sem("forget_act"), 1)
            act.wait_ge(sem("forget_act"), 1)
            A(r[0:8, 2], r[0:8, 2], ACT.Exp, scale=-1.0).then_inc(sem("forget_act"), 1)
            act.wait_ge(sem("forget_dve"), 1)
            A(r[0:8, 2], r[0:8, 2], ACT.Ln).then_inc(sem("forget_act"), 1)

            with act.Fori(0, 2) as it:
                def evac(j):
                    act.wait_ge(evacuated, 2 * it + (UNIT0["gm"] + j + 1))
                    g = gmla[:, sl(4 * it + 2 * j, 2)]
                    A(g, g, ACT.Silu).then_inc(sem("gmla_ready"), 1)
                units("gm", it, 2, evac)

            def ca(a, n):
                if a == 0:
                    act.wait_ge(sem("ca_nmax"), n + 1)
                    for q in range(4):
                        A(pr[:, q], db[:, q], ACT.Exp, bias=smc(NMAX + q), accum_out=smc(RSUM + q))\
                            .then_inc(sem("ca_exp"), 1)
                elif a == 1:
                    act.wait_ge(sem("ca_turned"), n + 1)
                    A(pT[:, 0:2], pb[3][:, :, :], ACT.Copy).then_inc(sem("ca_prob_copied"), 1)

            def fox_gate(it):
                act.wait_ge(evacuated, 4 * it + (UNIT0["fox"] + 3))
                A(fg[:, :], fg[:, :], ACT.Silu).then_inc(sem("fg_ready"), 1)
            with act.Fori(0, 1) as it:
                units("fox", 0, 4, lambda j: fox_gate(0) if j == 2 else None)
            with act.Fori(1, 4) as it:
                def react(j, i):
                    if (j, i) == (0, 0):
                        ca(0, it - 1)
                    elif (j, i) == (1, 0):
                        ca(1, it - 1)
                units("fox", it, 4, lambda j: fox_gate(it) if j == 2 else None, react)
            ca(0, 3)
            ca(1, 3)
            norm_rms("gq", 768)
            act.wait_ge(w_used, CHUNK0["uq"])
            norm_hi("gq", 6)
            norm_rms("gkv", 512)
            norm_hi("gkv", 4, 6)
            for c in range(9 + 8):
                split(CHUNK0["uq"] + c + SLOTS)
            for p in range(4):
                if p:
                    act.wait_ge(sem("qrope_ready"), 3 * p)
                else:
                    act.wait_ge(evacuated, UNIT0["uq"] + 6)
                A(qm[0:64, :], lat[64:128, p], ACT.Copy).then_inc(sem("qr_swap"), 1)
                A(qm[64:128, :], lat[0:64, p], ACT.Copy).then_inc(sem("qr_swap"), 1)
            for p in range(4):
                ca(0, 4 + p)
                ca(1, 4 + p)
            act.wait_ge(sem("ca_o"), 8)
            split_h("o2", y)
            with act.Fori(0, 3) as it:
                units("out", it, 2)
            units("out", 3, 2)
            norm_rms("post", D)

        @block.vector
        def _(dve):
            V = nc.vector

            def tt(out, a, b, op):
                return V.tensor_tensor(out, a, b, op)

            def split(c, per=0, it=0):
                if isinstance(it, int):
                    c, it, per = c + per * it, 0, 0
                    if c >= N_CHUNKS:
                        return
                s = c % SLOTS
                dve.wait_ge(hi_ready, per * it + (c + 1))
                tt(w_lo[:, s], raw[:, s], w_hi[:, s].bitcast(F32), ALU.subtract).then_inc(lo_ready, 1)

            def units(name, it, n, evac=None, react=None, K=KT):
                m = n * K // BLK
                for j in range(n):
                    for i in range(K // BLK):
                        if react is not None:
                            react(j, i)
                        if i == K // BLK - 1:
                            evac(j)
                        split(CHUNK0[name] + j * K // BLK + i + SLOTS, m, it)

            def done(name, it, n, j, K=KT):
                dve.wait_ge(w_used, n * K // BLK * it + (CHUNK0[name] + (j + 1) * K // BLK))
                return bank[(UNIT0[name] + j + (n * it if isinstance(it, int) else 0)) % 2]

            def copy_to(name, it, n, j, out, K=KT):
                b = done(name, it, n, j, K)
                V.tensor_copy(out, b[:, :, :]).then_inc(evacuated, 1)

            def add_x(name, it, n, j, K=KT):
                b = done(name, it, n, j, K)
                t = x[:, sl(n * it + j + (n * it + j), 2)] if isinstance(it, int) else x[:, sl(2 * n * it + 2 * j, 2)]
                tt(t, b[:, :, :], t, ALU.add).then_inc(evacuated, 1)

            def rsqrt(name):
                dve.wait_ge(sem("rms_ready"), NORM[name])
                V.reciprocal(rr[:, :], rr[:, :]).then_inc(sem("rsqrt_ready"), 1)
                dve.wait_ge(sem("rsqrt_ready"), NORM[name])

            def norm(name, src, gain, nt=KT, h0=0):
                rsqrt(name)
                if HFILL[name]:
                    dve.wait_ge(h_ready, HFILL[name])
                for k in range(nt + 2):
                    if k < nt:
                        if k >= 4:
                            dve.wait_ge(h_ready, HFILL[name] + k - 3)
                        V.scalar_tensor_tensor(tn[:, k % 4], src[:, k], col(gain, k), rr[:, :],
                                               ALU.mult, ALU.mult).then_inc(sem("tn_ready"), 1)
                    if k >= 2:
                        dve.wait_ge(sem("h_hi_ready"), HFILL[name] + k - 1)
                        tt(h_lo[:, h0 + k - 2], tn[:, (k - 2) % 4], h_hi[:, h0 + k - 2].bitcast(F32),
                           ALU.subtract).then_inc(h_ready, 1)

            def split_h(name, src):
                for k in range(KT):
                    dve.wait_ge(sem("h_hi_ready"), HFILL[name] + k + 1)
                    tt(h_lo[:, k], src[:, k], h_hi[:, k].bitcast(F32), ALU.subtract).then_inc(h_ready, 1)

            def taps(name, b, acc_, wcol, n, base, shifted=None):
                for q in range(2 * n):
                    tap, t = q // 2, q % 2
                    if tap:
                        dve.wait_ge(sem(name), base + (q - 1))
                    V.scalar_tensor_tensor(acc_[:, t, tap + 1:], b[:, t, :S - tap - 1], wcol(tap, t),
                                           acc_[:, t, tap + 1:], ALU.mult, ALU.add)\
                        .then_inc(*((evacuated, 1) if q == 2 * n - 1 and shifted is None else (sem(name), 1)))

            dve.wait_ge(sem("cols_in"), 16)
            for c in range(SLOTS):
                split(c)
            norm("mem", x, "mem")
            with dve.Fori(0, 4) as it:
                units("xk", it, 2, lambda j: copy_to("xk", it, 2, j, kx[:, sl(4 * it + 2 * j, 2)]))
            with dve.Fori(0, 4) as it:
                units("xv", it, 2, lambda j: copy_to("xv", it, 2, j, vx[:, :, sl(512 * it + 256 * j, 256)]))

            norm("mix", x, "mix")
            split(CHUNK0["ba"] + SLOTS)
            r = rows
            dve.wait_ge(w_used, CHUNK0["ba"] + 2)
            V.tensor_copy(r[:, 1], bank[UNIT0["ba"] % 2][:, 0]).then_inc(evacuated, 1)
            split(CHUNK0["ba"] + SLOTS + 1)
            b_dve = sem("ba_dve")
            dve.wait_ge(sem("ba_act"), 4)
            V.tensor_scalar(r[0:8, 2], r[0:8, 2], 1.0, None, ALU.add).then_inc(b_dve, 1)
            V.tensor_scalar(r[0:8, 3], r[0:8, 1], col("dtb", 0, slice(0, 8)), 0.0, ALU.add, ALU.max)\
                .then_inc(b_dve, 1)
            dve.wait_ge(sem("ba_act"), 5)
            dve.wait_ge(b_dve, 2)
            tt(r[0:8, 3], r[0:8, 3], r[0:8, 2], ALU.add).then_inc(b_dve, 1)
            dve.wait_ge(b_dve, 3)
            V.tensor_scalar(r[0:8, 3], r[0:8, 3], sm[0:8, EA_COL:EA_COL + 1], -1.0, ALU.mult, ALU.mult)\
                .then_inc(b_dve, 1)
            dve.wait_ge(b_dve, 4)
            for n in range(2):
                hs = slice(n * P, (n + 1) * P)
                V.tensor_tensor_scan(r[0:8, 0, hs], ones[0:8, :], r[0:8, 3, hs], 0.0, ALU.mult, ALU.add)\
                    .then_inc(b_dve, 1)

            with dve.Fori(0, 6) as it:
                def evac(j):
                    b = done("qkv", it, 2, j)
                    dve.wait_ge(sem("qkv_tap0"), 4 * it + (2 * j + 2))
                    taps("qkv_taps", b, (cy, cz)[j],
                         lambda tap, t: col("gconv", 24 * (2 - tap) + (4 * it + (2 * j + t))), 3, 10 * it + 5 * j)
                units("qkv", it, 2, evac)

            dve.wait_ge(sem("ba_cols"), 2)
            V.tensor_copy(smc(G_COL, 16), pb[5][:, 0, 0:16]).then_inc(b_dve, 1)
            V.tensor_copy(smc(B_COL, 16), pb[4][:, 0, 0:16]).then_inc(b_dve, 1)
            dve.wait_ge(b_dve, 8)
            dve.wait_ge(sem("ba_act"), 6)
            V.scalar_tensor_tensor(smc(NBEG_COL, 8), smc(B_COL + 8, 8), -1.0, smc(EG_COL, 8),
                                   ALU.mult, ALU.mult).then_inc(b_dve, 1)
            dve.wait_ge(b_dve, 9)

            def lev(l):
                return levT[:, l:l + 1, :].to_broadcast([P, 4, P])

            def level_part(l):
                tt(lv[:, :, :], lev(l + 1), aT[:, :, :], ALU.mult).then_inc(sem("level_part"), 1)

            def gdn(g, it):
                if g == 0:
                    for i in range(2):
                        for p0 in (0, 32):
                            ps = slice(p0, p0 + 8)
                            V.tensor_scalar(r[ps, 2 + i], r[ps, 0],
                                            cst[ps, sl(CST["ident"] + p0 + i + 2 * it, 1)], None, ALU.mult)\
                                .then_inc(sem("head_rows"), 1)
                    dve.wait_ge(sem("qk_rms"), 2 * it + 1)
                    V.reciprocal(inv[:, :, :], inv[:, :, :]).then_inc(sem("qk_rsqrt"), 1)
                    dve.wait_ge(sem("qk_rms"), 2 * it + 2)
                    V.reciprocal(invT[:, :, :], invT[:, :, :]).then_inc(sem("qk_rsqrt"), 1)
                    dve.wait_ge(sem("qk_rsqrt"), 2 * it + 1)
                    V.scalar_tensor_tensor(qn[:, :, :], qkv[:, sl(2 * it, 2)], P ** -0.5,
                                           inv[:, :, :].rearrange(pair4, a=2), ALU.mult, ALU.mult)\
                        .then_inc(sem("qk_normed"), 1)
                    dve.wait_ge(sem("qk_rsqrt"), 2 * it + 2)
                    tt(kn[:, :, :], qkv[:, sl(2 * it + 8, 2)], invT[:, :, :].rearrange(pair4, a=2), ALU.mult)\
                        .then_inc(sem("qk_normed"), 1)
                elif g == 2:
                    dve.wait_ge(sem("rows_spread"), it + 1)
                    for b in range(4):
                        V.tensor_scalar(dec[:, b], pb4[2][:, b], smc(G_COL + (b % 2) * 8 + b // 2 + 2 * it), 0.0,
                                        ALU.subtract, ALU.min).then_inc(sem("dec_args"), 1)
                    for i in range(2):
                        tt(smc(KD_ARG + i), pb4[2][:, 2 * i, P - 1:P], smc(G_COL + i + 2 * it), ALU.subtract)\
                            .then_inc(sem("dec_args"), 1)
                    dve.wait_ge(sem("dec_ready"), it + 1)
                    dve.wait_ge(sem("grams"), it + 1)
                    tt(aT[:, :, :], pb4[0], dec[:, :, :], ALU.mult).then_inc(sem("a_steps"), 1)
                    dve.wait_ge(sem("a_steps"), 2 * it + 1)
                    tt(aT[:, :, :], aT[:, :, :], pb4[3], ALU.mult).then_inc(sem("a_steps"), 1)
                    dve.wait_ge(sem("a_steps"), 2 * it + 2)
                    tt(lv[:, :, :], lev(0), aT[:, :, :], ALU.mult).then_inc(sem("inv0_part"), 1)
                    dve.wait_ge(sem("inv0_part"), it + 1)
                    tt(invT[:, :, :], ident.unsqueeze(1).to_broadcast([P, 4, P]), lv[:, :, :], ALU.subtract)\
                        .then_inc(sem("inv0_ready"), 1)
                    dve.wait_ge(sem("inv0_ready"), it + 1)
                    tt(attT[:, :, :], pb4[1], dec[:, :, :], ALU.mult).then_inc(sem("att_ready"), 1)
                    level_part(0)
                    dve.wait_ge(sem("att_ready"), 3 * it + 1)
                    tt(attT[:, :, :], attT[:, :, :], causT.unsqueeze(1).to_broadcast([P, 4, P]), ALU.mult)\
                        .then_inc(sem("att_ready"), 1)
                    dve.wait_ge(sem("q_decay"), it + 1)
                    tt(qd[:, :, :], qn[:, :, P:2 * P], qd[:, :, :], ALU.mult).then_inc(sem("att_ready"), 1)
                elif 4 <= g < 16 and g % 2 == 0:
                    l = (g - 4) // 2
                    if l < 5:
                        dve.wait_ge(sem("level_product"), 6 * it + (l + 1))
                        level_part(l + 1)
                elif 5 <= g < 16:
                    l = (g - 5) // 2
                    dve.wait_ge(sem("level_update"), 6 * it + (l + 1))
                    if l < 5:
                        tt(inv[:, :, :], inv[:, :, :], pb4[2], ALU.subtract).then_inc(sem("inv_updated"), 1)
                    tt(invT[:, :, :], invT[:, :, :], pb4[3], ALU.subtract).then_inc(sem("inv_updated"), 1)
                elif g == 18:
                    dve.wait_ge(sem("k_state"), it + 1)
                    for i in range(2):
                        V.scalar_tensor_tensor(r1[:, i], pb4[2][:, i], smc(NBEG_COL + i + 2 * it),
                                               vb[:, 2 * i + 1], ALU.mult, ALU.add).then_inc(sem("rest_ready"), 1)
                elif g == 21:
                    dve.wait_ge(sem("out_rms"), it + 1)
                    V.reciprocal(osq[:, :, :], osq[:, :, :]).then_inc(sem("out_rsqrt"), 1)
                    dve.wait_ge(sem("out_rsqrt"), it + 1)
                    yy = y[:, sl(2 * it, 2)]
                    V.scalar_tensor_tensor(yy, pb[4][:, :, :], col("ogain"), osq[:, :, :], ALU.mult, ALU.mult)\
                        .then_inc(sem("gdn_y"), 1)
                    dve.wait_ge(sem("gdn_y"), 2 * it + 1)
                    dve.wait_ge(sem("z_ready"), it + 1)
                    tt(yy, yy, zs[:, :], ALU.mult).then_inc(sem("gdn_y"), 1)

            dve.wait_ge(sem("qkv_ready"), 12)
            with dve.Fori(0, 4) as it:
                def react(j, i):
                    for g in (8 * j + 2 * i, 8 * j + 2 * i + 1):
                        if g < 22:
                            gdn(g, it)

                def evac(j):
                    if j < 3:
                        copy_to("gdn", it, 4, j, (zs, cy, cz)[j][:, :])
                        return
                    b = done("gdn", it, 4, j)
                    tt(cw[:, :], b[:, :, :], cz[:, :], ALU.mult).then_inc(evacuated, 1)
                    dve.wait_ge(sem("sc_tap0"), 2 * it + 2)
                    taps("sc_taps", cw, cv, lambda tap, t: col("sconv", 8 * (1 - tap) + (2 * it + t)), 2, 4 * it,
                         shifted=True)
                    dve.wait_ge(sem("sc_taps"), 4 * it + 4)
                    tt(y[:, sl(2 * it + 8, 2)], cv[:, :], cy[:, :], ALU.mult).then_inc(sem("sc_y"), 1)
                units("gdn", it, 4, evac, react)

            split_h("y", y)
            dve.wait_ge(sem("x_again"), 16)
            with dve.Fori(0, 4) as it:
                units("mixo", it, 2, lambda j: add_x("mixo", it, 2, j))
            norm("xa", x, "xa")

            XSC = 512 ** -0.5

            def xa(a, h):
                if a == 0:
                    dve.wait_ge(sem("xa_scores"), h + 1)
                    V.tensor_reduce(smc(NMAX, 2), pb[0][:, :, :], AX.X, ALU.max, negate=True).then_inc(sem("xa_nmax"), 1)
                    dve.wait_ge(sem("xa_nmax"), 2 * h + 1)
                    V.tensor_scalar(smc(NMAX, 2), smc(NMAX, 2), XSC, None, ALU.mult).then_inc(sem("xa_nmax"), 1)
                    dve.wait_ge(sem("xa_exp"), 2 * h + 2)
                    V.reciprocal(smc(RINV, 2), smc(RSUM, 2)).then_inc(sem("xa_rinv"), 1)
                    dve.wait_ge(sem("xa_rinv"), h + 1)
                    for t in range(2):
                        V.tensor_scalar(pr[:, t], pr[:, t], smc(RINV + t), None, ALU.mult).then_inc(sem("xa_prob"), 1)
                elif a == 2:
                    dve.wait_ge(sem("xa_pv"), h + 1)
                    for q in range(2):
                        V.tensor_copy(y[:, sl(4 * h + 2 * q, 2)], pb[2 + q][:, :, :]).then_inc(sem("xa_o"), 1)

            def q_evac(it, j):
                copy_to("xq", it, 2, j, xq[:, 2 * j:2 * j + 2])
            units("xq", 0, 2, lambda j: q_evac(0, j))
            with dve.Fori(1, 4) as it:
                def react(j, i):
                    if (j, i) == (0, 0):
                        xa(0, it - 1)
                    elif (j, i) == (1, 0):
                        xa(2, it - 1)
                units("xq", it, 2, lambda j: q_evac(it, j), react)
            xa(0, XH - 1)
            xa(2, XH - 1)
            split_h("o", y)
            with dve.Fori(0, 4) as it:
                units("xo", it, 2, lambda j: add_x("xo", it, 2, j))
            norm("ffn", x, "ffn")
            tile0 = 0
            for s, nt in enumerate(SEGS):
                name = f"up{s}"
                g0 = sum(SEGS[:s]) // 2
                with dve.Fori(0, nt // 2) as it:
                    def evac(j):
                        b = done(name, it, 2, j)
                        dve.wait_ge(sem("up_tap0"), 4 * it + (4 * g0 + 2 * j + 2))
                        taps("up_taps", b, (cy, cw)[j],
                             lambda tap, t: col("fconv", 88 * (1 - tap) + 44 * j + tile0 + t + 2 * it), 2,
                             6 * it + (6 * g0 + 3 * j))
                        if j == 1:
                            dve.wait_ge(sem("gate_ready"), it + (g0 + 1))
                            dve.wait_ge(evacuated, 2 * it + (UNIT0[name] + 2))
                            tt(cv[:, :], cw[:, :], cz[:, :], ALU.mult).then_inc(sem("gated"), 1)
                            dve.wait_ge(sem("g_hi_ready"), it + (g0 + 1))
                            gt = sl(2 * it, 2)
                            tt(g_lo[:, gt], cv[:, :], g_hi[:, gt].bitcast(F32), ALU.subtract)\
                                .then_inc(sem("g_ready"), 1)
                    units(name, it, 2, evac)
                tile0 += nt
                with dve.Fori(0, 2) as it:
                    units(f"down{s}", it, 4, lambda j: add_x(f"down{s}", it, 4, j, K=nt), K=nt)

            rsqrt("fin")
            for k in range(KT):
                V.scalar_tensor_tensor(x[:, k], x[:, k], col("fin", k), rr[:, :], ALU.mult, ALU.mult)\
                    .then_inc(sem("x_final"), 1)
            rd = sem("rope_dve")
            dve.wait_ge(sem("pos_in"), 16)
            V.tensor_copy(sinr[:, :], pos[:, :]).then_inc(rd, 1)
            dve.wait_ge(rd, 1)
            V.tensor_scalar(sinr[:, :], sinr[:, :], c1("invf"), None, ALU.mult).then_inc(rd, 1)
            dve.wait_ge(rd, 2)
            V.tensor_scalar(cosr[:, :], sinr[:, :], 1.0 / (2 * np.pi), MAGIC, ALU.mult, ALU.add).then_inc(rd, 1)
            dve.wait_ge(rd, 3)
            V.tensor_scalar(cosr[:, :], cosr[:, :], MAGIC, None, ALU.subtract).then_inc(rd, 1)
            for q in range(3):
                dve.wait_ge(rd, 4 + q)
                V.scalar_tensor_tensor(sinr[:, :], cosr[:, :], -TWO_PI[q], sinr[:, :], ALU.mult, ALU.add)\
                    .then_inc(rd, 1)
            dve.wait_ge(rd, 7)
            V.tensor_scalar(sinr[:, :], sinr[:, :], 3.1415925, -3.1415925, ALU.min, ALU.max).then_inc(rd, 1)
            norm("pre", x, "pre")
            dve.wait_ge(sem("rope_act"), 3)
            V.tensor_scalar(sinr[:, :], sinr[:, :], c1("sgn"), None, ALU.mult).then_inc(rd, 1)
            with dve.Fori(0, 3) as it:
                units("lat", it, 2, lambda j: copy_to("lat", it, 2, j, lat[:, sl(4 * it + 2 * j, 2)]))
            dve.wait_ge(rd, 9)
            dve.wait_ge(evacuated, UNIT0["lat"] + 6)
            kd_ = sem("kr_dve")
            tt(kr[:, :], lat[:, 10], cosr[:, :], ALU.mult).then_inc(kd_, 1)
            dve.wait_ge(sem("kr_swap"), 2)
            tt(tn[:, 0], qm[:, :], sinr[:, :], ALU.mult).then_inc(kd_, 1)
            dve.wait_ge(kd_, 2)
            tt(kr[:, :], kr[:, :], tn[:, 0], ALU.add).then_inc(kd_, 1)
            fd = sem("forget_dve")
            dve.wait_ge(sem("forget_act"), 2)
            V.tensor_scalar(r[0:8, 2], r[0:8, 2], 1.0, None, ALU.add).then_inc(fd, 1)
            V.tensor_scalar(r[0:8, 3], lat[0:8, 11], col("bfor", 0, slice(0, 8)), 0.0, ALU.add, ALU.min)\
                .then_inc(fd, 1)
            dve.wait_ge(sem("forget_act"), 3)
            dve.wait_ge(fd, 2)
            tt(r[0:8, 3], r[0:8, 3], r[0:8, 2], ALU.subtract).then_inc(fd, 1)
            dve.wait_ge(fd, 3)
            V.tensor_tensor_scan(r[0:8, 0, 0:P], ones[0:8, :], r[0:8, 3, 0:P], 0.0, ALU.mult, ALU.add).then_inc(fd, 1)
            dve.wait_ge(fd, 4)
            V.tensor_copy(sm[0:8, EA_COL:EA_COL + 1], r[0:8, 0, P - 1:P]).then_inc(fd, 1)
            dve.wait_ge(fd, 5)
            V.tensor_tensor_scan(r[0:8, 0, P:S], ones[0:8, :], r[0:8, 3, P:S], sm[0:8, EA_COL:EA_COL + 1],
                                 ALU.mult, ALU.add).then_inc(fd, 1)
            with dve.Fori(0, 2) as it:
                units("gm", it, 2, lambda j: copy_to("gm", it, 2, j, gmla[:, sl(4 * it + 2 * j, 2)]))
            dve.wait_ge(sem("forget_cols"), 1)
            V.tensor_copy(smc(C_COL, 16), pb[5][:, 0, 0:16]).then_inc(fd, 1)
            dve.wait_ge(fd, 7)

            def ca(a, n, p=None):
                cd = sem("ca_logits")
                if a == 0:
                    if p is None:
                        for i in range(2):
                            V.tensor_scalar(r[0:8, 2 + i], r[0:8, 0], cst[0:8, sl(CST["ident"] + i + 2 * n, 1)],
                                            None, ALU.mult).then_inc(sem("forget_rows"), 1)
                        dve.wait_ge(sem("ca_scores"), n + 1)
                        for i in range(2):
                            for t in range(2):
                                V.tensor_scalar(db[:, 2 * i + t], pb[2][:, i], smc(C_COL + 8 * t + i + 2 * n), -1.0,
                                                ALU.subtract, ALU.mult).then_inc(cd, 1)
                        dve.wait_ge(cd, 8 * n + 4)
                        for i in range(2):
                            tt(db[:, 2 * i:2 * i + 2], db[:, 2 * i:2 * i + 2], cmask, ALU.add).then_inc(cd, 1)
                        for i in range(2):
                            dve.wait_ge(cd, 8 * n + (5 + i))
                            V.scalar_tensor_tensor(db[:, 2 * i:2 * i + 2], pb[i][:, :, :], P ** -0.5,
                                                   db[:, 2 * i:2 * i + 2], ALU.mult, ALU.add).then_inc(cd, 1)
                        dve.wait_ge(cd, 8 * n + 8)
                    else:
                        if p:
                            dve.wait_ge(sem("ca_scores"), n)
                        for i in range(2):
                            V.tensor_scalar(qmask[:, i], qrope[:, p], c1(f"head{i}"), None, ALU.mult)\
                                .then_inc(sem("mla_q_masked"), 1)
                        dve.wait_ge(sem("ca_scores"), n + 1)
                        for i in range(2):
                            V.scalar_tensor_tensor(db[:, 2 * i:2 * i + 2], pb[i][:, :, :], 192 ** -0.5,
                                                   cmask, ALU.mult, ALU.add).then_inc(cd, 1)
                        dve.wait_ge(cd, 32 + 2 * p + 2)
                    V.tensor_reduce(smc(NMAX, 4), db[:, :, :], AX.X, ALU.max, negate=True).then_inc(sem("ca_nmax"), 1)
                    dve.wait_ge(sem("ca_exp"), 4 * n + 4)
                    V.reciprocal(smc(RINV, 4), smc(RSUM, 4)).then_inc(sem("ca_rinv"), 1)
                    dve.wait_ge(sem("ca_rinv"), n + 1)
                    for q in range(4):
                        V.tensor_scalar(pr[:, q], pr[:, q], smc(RINV + q), None, ALU.mult).then_inc(sem("ca_prob"), 1)
                elif a == 1:
                    dve.wait_ge(sem("ca_turned"), n + 1)
                    V.tensor_copy(pT[:, 2:4], pb[4][:, :, :]).then_inc(sem("ca_prob_copied"), 1)
                else:
                    dve.wait_ge(sem("ca_pv"), n + 1)
                    if p is None:
                        dve.wait_ge(sem("fg_ready"), n + 1)
                        tt(y[:, sl(2 * n + 8, 2)], pb[5][:, :, :], fg[:, :], ALU.mult).then_inc(sem("ca_o"), 1)
                    else:
                        tt(y[:, 2 * p:2 * p + 2], pb[5][:, :, :], gmla[:, 2 * p:2 * p + 2], ALU.mult)\
                            .then_inc(sem("ca_o"), 1)

            def fox_evac(it, j):
                if j == 3:
                    b = done("fox", it, 4, j)
                    V.tensor_copy(fv[:, :, :], b[:, :, :]).then_inc(evacuated, 1)
                else:
                    copy_to("fox", it, 4, j, (fq, fk, fg)[j][:, :])
            units("fox", 0, 4, lambda j: fox_evac(0, j))
            with dve.Fori(1, 4) as it:
                def react(j, i):
                    if (j, i) == (0, 0):
                        ca(0, it - 1)
                    elif (j, i) == (1, 0):
                        ca(1, it - 1)
                    elif (j, i) == (1, 3):
                        ca(2, it - 1)
                units("fox", it, 4, lambda j: fox_evac(it, j), react)
            for a in range(3):
                ca(a, 3)
            norm("gq", lat, "gq", 6)
            norm("gkv", lat[:, 6:10], "gkv", 4, 6)

            def uq_evac(u):
                if u % 2:
                    dve.wait_ge(w_used, CHUNK0["uq"] + 6 * (u + 1) // BLK)
                else:
                    dve.wait_ge(sem("mid_chunk"), u // 2 + 1)
                to = qnope[:, 2 * u:2 * u + 2] if u < 4 else lat[:, 2 * u - 8:2 * u - 6]
                V.tensor_copy(to, bank[(UNIT0["uq"] + u) % 2][:, :, :]).then_inc(evacuated, 1)
            u = 0
            for c in range(9):
                while u < 6 and (6 * (u + 1) - 1) // BLK == c:
                    uq_evac(u)
                    u += 1
                split(CHUNK0["uq"] + c + SLOTS)
            for u in range(8):
                dve.wait_ge(w_used, CHUNK0["ukv"] + u + 1)
                to = knope[:, 2 * u:2 * u + 2] if u < 4 else vm[:, :, 256 * (u - 4):256 * (u - 3)]
                V.tensor_copy(to, bank[(UNIT0["ukv"] + u) % 2][:, :, :]).then_inc(evacuated, 1)
                split(CHUNK0["ukv"] + u + SLOTS)
            qd_ = sem("qrope_ready")
            for p in range(4):
                tt(qrope[:, p], lat[:, p], cosr[:, :], ALU.mult).then_inc(qd_, 1)
                dve.wait_ge(sem("qr_swap"), 2 * p + 2)
                tt(tn[:, p], qm[:, :], sinr[:, :], ALU.mult).then_inc(qd_, 1)
                dve.wait_ge(qd_, 3 * p + 2)
                tt(qrope[:, p], qrope[:, p], tn[:, p], ALU.add).then_inc(qd_, 1)
            dve.wait_ge(qd_, 12)
            dve.wait_ge(sem("gmla_ready"), 4)
            for p in range(4):
                for a in range(3):
                    ca(a, 4 + p, p)
            split_h("o2", y)
            with dve.Fori(0, 3) as it:
                units("out", it, 2, lambda j: copy_to("out", it, 2, j, y[:, sl(4 * it + 2 * j, 2)]))
            units("out", 3, 2, lambda j: copy_to("out", 3, 2, j, y[:, 12 + 2 * j:14 + 2 * j]))
            rsqrt("post")
            for k in range(KT + 1):
                if k < KT:
                    V.scalar_tensor_tensor(y[:, k], y[:, k], col("post", k), rr[:, :],
                                           ALU.mult, ALU.mult).then_inc(sem("post_tile"), 1)
                if k:
                    dve.wait_ge(sem("post_tile"), k)
                    tt(x[:, k - 1], x[:, k - 1], y[:, k - 1], ALU.add).then_inc(sem("out_ready"), 1)


def constants():
    c = np.zeros((P, N_CST), np.float32)
    i = np.arange(P)
    c[:, CST["ident"]:CST["ident"] + P] = np.eye(P)
    c[:, CST["ones"]:CST["ones"] + P] = 1
    c[:, CST["causT"]:CST["causT"] + P] = i[:, None] <= i[None, :]
    for l in range(NLEV):
        m = (i[:, None] >> l) + 1 == (i[None, :] >> l)
        m &= (i[None, :] >> l) % 2 == 1
        c[:, CST["levT"] + l * P:CST["levT"] + (l + 1) * P] = m
    for t in range(2):
        q, k = i[:, None] + t * P, np.arange(S)[None, :]
        c[:, CST["cmask"] + t * S:CST["cmask"] + (t + 1) * S] = np.where(k <= q, 0, NEG)
    c[:, CST["eps"]] = EPS
    c[:, CST["invf"]] = 10000.0 ** (-(i % 32) * 2.0 / 64)
    c[:, CST["sgn"]] = np.where(i < 64, -1, 1)
    c[:, CST["hpi"]] = np.pi / 2
    for h in range(2):
        c[:, CST[f"head{h}"]] = (i // 32) % 2 == h
    return c


def tiles(v):
    return np.asarray(v).reshape(-1, P).T


def feature_major(a):
    return np.ascontiguousarray(a.T.reshape(-1, P, a.shape[0]).transpose(1, 0, 2))


def stream_of(w):
    blocks = []

    def units(a, width=BW):
        k, n = a.shape
        blocks.append(a.reshape(k // P, P, n // width, width).transpose(2, 0, 1, 3).reshape(-1, P, width))

    def narrow(a):
        blocks.append(a.reshape(-1, 2, P, P).transpose(0, 2, 1, 3).reshape(-1, P, BW))

    def placed(n, parts):
        out = np.zeros((D, n), np.float32)
        for at_, a in parts:
            out[:, at_:at_ + a.shape[1]] = a
        return out

    mi, wi = w["w_mix_in"][0], w["w_in_2"][0]
    gw = 1024
    units(w["w_xk"][0])
    units(w["w_xv"][0])
    narrow(placed(P, [(0, mi[:, 4 * gw + 8:4 * gw + 16]), (32, mi[:, 4 * gw:4 * gw + 8])]))
    units(mi[:, :3 * gw])
    off = 4 * gw + 16
    for p in range(4):
        for base in (3 * gw, off, off + gw, off + 2 * gw):
            units(mi[:, base + p * BW:base + (p + 1) * BW])
    units(w["w_mix_out"][0])
    units(w["w_xq"][0])
    units(w["w_xo"][0])
    up, down = w["w_ffn_up"][0], w["w_ffn_down"][0]
    t0 = 0
    for nt in SEGS:
        for c in range(t0 * P, (t0 + nt) * P, BW):
            units(up[:, c:c + BW])
            units(up[:, FT * P + c:FT * P + c + BW])
        units(down[t0 * P:(t0 + nt) * P])
        t0 += nt
    units(wi[:, :1280])
    krope = wi[:, 1280:1344]
    f0 = 1344 + 4 * gw
    units(placed(BW, [(0, krope[:, :32]), (32, krope[:, :32]), (64, krope[:, 32:]), (96, krope[:, 32:]),
                      (P, wi[:, f0:f0 + 8])]))
    units(wi[:, 1344:1344 + gw])
    for p in range(4):
        for base in (1344 + gw, 1344 + 2 * gw, f0 + 8, 1344 + 3 * gw):
            units(wi[:, base + p * BW:base + (p + 1) * BW])
    uq = w["w_uq_2"][0].reshape(768, 8, 192)
    units(np.ascontiguousarray(uq[:, :, :P]).reshape(768, -1))
    rope = uq[:, :, P:].reshape(768, 4, 2, 2, 32).transpose(0, 1, 3, 2, 4)
    units(np.ascontiguousarray(rope).reshape(768, -1))
    ukv = w["w_ukv_2"][0].reshape(512, 8, 256)
    units(np.ascontiguousarray(ukv[:, :, :P]).reshape(512, -1))
    units(np.ascontiguousarray(ukv[:, :, P:]).reshape(512, -1))
    units(w["w_out_2"][0])
    b = np.concatenate(blocks)
    assert b.shape[0] == N_CHUNKS * BLK, (b.shape, N_CHUNKS)
    return np.ascontiguousarray(b.reshape(N_CHUNKS, BLK, P, BW).transpose(0, 2, 1, 3)).reshape(N_CHUNKS, P, BLK * BW)


def small_vectors(w):
    c = np.zeros((P, N_COLS), np.float32)

    def put(name, a):
        c[:a.shape[0], COLS[name]:COLS[name] + a.shape[1]] = a
    for name, key in (("mix", "mix_norm"), ("xa", "xattn_norm"), ("mem", "mem_norm"), ("ffn", "ffn_norm"),
                      ("pre", "g_pre_2"), ("post", "g_post_2"), ("gq", "g_q_latent_2"), ("gkv", "g_kv_latent_2"),
                      ("ogain", "gdn_out_norm"), ("gconv", "gdn_conv"), ("sconv", "sc_conv"), ("fconv", "ffn_conv")):
        put(name, tiles(np.asarray(w[key])[0].reshape(-1)))
    put("fin", tiles(w["final_norm"]))
    put("alog", np.asarray(w["gdn_a_log"])[0][:, None])
    put("dtb", np.asarray(w["gdn_dt_bias"])[0][:, None])
    put("bfor", np.asarray(w["b_forget_2"])[0][:, None])
    return c


def kernel(**inputs):
    from concourse import bacc
    from concourse.bass_utils import run_bass_kernel_spmd

    w = {k: np.asarray(v) for k, v in inputs.items()}
    arrays = {
        "weights": stream_of(w), "x_in": feature_major(w["x"][0]), "mem_in": feature_major(w["mem"][0]),
        "small_vectors": small_vectors(w), "constants": constants(),
        "positions": np.ascontiguousarray(w["positions_2"].reshape(1, S)),
    }
    nc = bacc.Bacc("TRN2", target_bir_lowering=False, num_devices=1)
    args = [nc.dram_tensor(n, a.shape, mybir.dt.from_np(a.dtype), kind="ExternalInput").ap()
            for n, a in arrays.items()]
    out = nc.dram_tensor("y_out", (P, KT, S), F32, kind="ExternalOutput").ap()
    build_program(nc, *args, out)
    r = run_bass_kernel_spmd(nc, [arrays], core_ids=[0])
    got = r.results[0]["y_out"]
    return np.ascontiguousarray(got.transpose(2, 1, 0)).reshape(1, S, D)
```

```python
import concourse.bass as bass
from concourse import mybir
from contextlib import ExitStack
import numpy as np

F32 = mybir.dt.float32
F32R = mybir.dt.float32r
I32 = mybir.dt.int32
ALU = mybir.AluOpType
ACT = mybir.ActivationFunctionType
AX = mybir.AxisListType

P = 128
S = 256
D = 2048
KT = D // P
CHUNK = 128
NLEV = 7
GH = 8
XH = 4
FT = 5632 // P
SEGS = [16, 16, 12]
SLOTS = 4
BLK = 4
BW = 256
EPS = 1e-6
NEG = -1e30
MAGIC = 1.5 * 2.0 ** 23
TWO_PI = (6.28125, 0.0019350051879882812, 3.019916050561733e-07)


STREAM = ([("xk", 8, KT), ("xv", 8, KT), ("ba", 1, 8), ("qkv", 12, KT), ("gdn", 16, KT),
           ("mixo", 8, KT), ("xq", 8, KT), ("xo", 8, KT)]
          + [x for i, n in enumerate(SEGS) for x in ((f"up{i}", n, KT), (f"down{i}", 8, n))]
          + [("lat", 6, KT), ("uq", 6, 6), ("ukv", 8, 4), ("fox", 16, KT), ("gm", 4, KT),
             ("out", 8, KT)])
UNIT0, CHUNK0 = {}, {}
_u = _b = 0
for _name, _n, _k in STREAM:
    UNIT0[_name], CHUNK0[_name] = _u, _b // BLK
    _u += _n
    _b += _n * _k
N_CHUNKS = _b // BLK
assert _b % BLK == 0

COLS, _at = {}, 0
for _name, _n in (("mix", KT), ("xa", KT), ("mem", KT), ("ffn", KT), ("fin", KT), ("pre", KT),
                  ("post", KT), ("gq", 6), ("gkv", 4), ("ogain", 1), ("gconv", 24 * 4),
                  ("sconv", 8 * 3), ("fconv", 88 * 3), ("alog", 1), ("dtb", 1), ("bfor", 1)):
    COLS[_name] = _at
    _at += _n
N_COLS = _at
CST, _at = {}, 0
for _name, _n in (("ident", P), ("ones", P), ("causT", P), ("levT", NLEV * P), ("cmask", 2 * S),
                  ("head0", 1), ("head1", 1), ("eps", 1), ("invf", 1), ("sgn", 1), ("hpi", 1)):
    CST[_name] = _at
    _at += _n
N_CST = _at



HFILL, _h = {}, 0
for _name, _n in (("mem", KT), ("mix", KT), ("y", KT), ("xa", KT), ("o", KT), ("ffn", KT),
                  ("pre", KT), ("gq", 6), ("gkv", 4), ("o2", KT)):
    HFILL[_name] = _h
    _h += _n
NORM, SQ0, TN0, _s, _t = {}, {}, {}, 0, 0
for _i, (_name, _n) in enumerate((("mem", 8), ("mix", 8), ("xa", 8), ("ffn", 8), ("pre", 8),
                                  ("gq", 3), ("gkv", 2), ("post", 8))):
    NORM[_name], SQ0[_name], TN0[_name] = _i + 1, _s, _t
    _s += 2 * _n - 1 if _name != "pre" else 0
    _t += 2 * _n
G_COL, B_COL, EG_COL, NBEG_COL, KD_ARG, KD_COL, EA_COL = 0, 16, 32, 40, 48, 50, 52
NMAX, RSUM, RINV, C_COL, R_COL, RF_COL, R2_COL, RKV_COL = 60, 64, 68, 72, 88, 90, 92, 94


def sl(start, n):
    return slice(start, start + n) if isinstance(start, int) else bass.ds(start, n)


def build_program(nc, wst, xT, memT, cols_d, cst_d, pos_d, out_d):
    ctx = ExitStack()
    with ctx:
        def at(name, kb, shape, dt=F32):
            return nc.alloc_sbuf_tensor_at(name, [P] + list(shape), dt, offset=16512 + int(kb * 1024))

        raw = at("raw", 0, [SLOTS, BLK * BW])
        w_hi = at("w_hi", 16, [SLOTS, BLK * BW], F32R)
        w_lo = at("w_lo", 32, [SLOTS, BLK * BW], F32R)
        h_hi = at("h_hi", 48, [KT, S], F32R)
        h_lo = at("h_lo", 64, [KT, S], F32R)
        x = at("x", 80, [KT, S])
        kx = at("kx", 96, [KT, S])
        vx = at("vx", 112, [2, D])
        qkv = at("qkv", 128, [24, S])
        y = at("y", 160, [KT, S])
        cst = at("cst", 176, [N_CST])
        cols = at("cols", 183.5, [N_COLS])
        tn = at("tn", 186, [4, S])
        acc = at("acc", 190, [2, S])
        sq = at("sq", 192, [2, S])
        rr = at("rr", 194, [S])
        cy = at("cy", 195, [2, S])
        cz = at("cz", 197, [2, S])
        cw = at("cw", 199, [2, S])
        cv = at("cv", 201, [2, S])
        rows = at("rows", 203, [4, S])
        sm = at("sm", 207, [160])
        qn, kn = at("qn", 80, [2, S]), at("kn", 82, [2, S])
        dec, aT, attT = at("dec", 84, [4, P]), at("aT", 86, [4, P]), at("attT", 88, [4, P])
        inv, invT, lv = at("inv", 90, [4, P]), at("invT", 92, [4, P]), at("lv", 94, [4, P])
        vs, zs, vb = at("vs", 152, [2, S]), at("zs", 154, [2, S]), at("vb", 156, [4, P])
        kd, qd = at("kd", 158, [2, P]), at("qd", 159, [2, P])
        vn, s1, r1 = at("vn", 186, [4, P]), at("s1", 188, [2, P]), at("r1", 189, [2, P])
        lp, osq = at("lp", 190, [4, P]), at("osq", 192, [2, S])
        xq = at("xq", 128, [4, S])
        vh = at("vh", 132, [2, 512])
        pr = at("pr", 136, [4, S])
        pT = at("pT", 140, [4, S])
        g_hi = at("g_hi", 96, [KT, S], F32R)
        g_lo = at("g_lo", 112, [KT, S], F32R)
        lat = at("lat", 96, [12, S])
        lh_hi = at("lh_hi", 108, [10, S], F32R)
        lh_lo = at("lh_lo", 118, [10, S], F32R)
        qnope, qrope = at("qnope", 128, [8, S]), at("qrope", 136, [4, S])
        knope, vm = at("knope", 140, [8, S]), at("vm", 148, [2, 1024])
        kr = at("kr", 156, [S])
        qpair, vpair = at("qpair", 157, [2, S]), at("vpair", 100, [2, S])
        gg = at("gg", 104, [2, 2, S])
        fq, fk = at("fq", 108, [2, S]), at("fk", 110, [2, S])
        fg, fv = at("fg", 112, [2, S]), at("fv", 114, [2, S])
        pr2, pT2, db = at("pr2", 116, [4, S]), at("pT2", 120, [4, S]), at("db", 124, [4, S])
        acc2 = at("acc2", 195, [2, S])
        qmask = at("qmask", 195, [2, S])
        cosr, sinr = at("cosr", 197, [S]), at("sinr", 198, [S])
        qm = at("qm", 199, [S])
        pos = at("pos", 200, [S], I32)
        rq, rkv, rf = at("rq", 201, [S]), at("rkv", 202, [S]), at("rf", 202, [S])

        ident = cst[:, CST["ident"]:CST["ident"] + P]
        ones = cst[:, CST["ones"]:CST["ones"] + P]
        causT = cst[:, CST["causT"]:CST["causT"] + P]
        levT = cst[:, CST["levT"]:CST["levT"] + NLEV * P].rearrange("p (l m) -> p l m", l=NLEV)
        cmask = cst[:, CST["cmask"]:CST["cmask"] + 2 * S].rearrange("p (t m) -> p t m", t=2)

        def c1(name, parts=slice(0, P)):
            return cst[parts, CST[name]:CST[name] + 1]

        def col(name, i=0, parts=slice(0, P)):
            return cols[parts, sl(COLS[name] + i, 1)]

        bank = [ctx.enter_context(nc.psum_tensor(f"unit{i}", [P, 2, S], F32)) for i in range(2)]
        pb = [ctx.enter_context(nc.psum_tensor(f"pb{i}", [P, 2, S], F32)) for i in range(6)]
        pb4 = [b[:, :, :].rearrange("p a (b c) -> p (a b) c", b=2) for b in pb]

        sems = {}

        def sem(name):
            if name not in sems:
                sems[name] = ctx.enter_context(nc.semaphore(name))
            return sems[name]

        raw_ready = [sem(f"raw_ready{i}") for i in range(SLOTS)]
        hi_ready, lo_ready, w_used = sem("hi_ready"), sem("lo_ready"), sem("w_used")
        evacuated = sem("evacuated")
        h_ready = sem("h_ready")

        def loop(eng, n, body, first=False):
            if first:
                body(0)
            with eng.Fori(1 if first else 0, n) as it:
                body(it)

        block = ctx.enter_context(nc.Block())

        @block.sync
        def _(sp):
            for s in range(SLOTS):
                sp.dma_start(x[:, 4 * s:4 * s + 4, :], memT[:, 4 * s:4 * s + 4, :]).then_inc(sem(f"mem_in{s}"), 16)
                sp.dma_start(raw[:, s], wst[s]).then_inc(raw_ready[s], 16)
            with sp.Fori(1, N_CHUNKS // SLOTS) as it:
                for s in range(SLOTS):
                    sp.wait_ge(lo_ready, SLOTS * it + (s - SLOTS + 1))
                    sp.dma_start(raw[:, s], wst[SLOTS * it + s]).then_inc(raw_ready[s], 16)
            for c in range(N_CHUNKS // SLOTS * SLOTS, N_CHUNKS):
                sp.wait_ge(lo_ready, c - SLOTS + 1)
                sp.dma_start(raw[:, c % SLOTS], wst[c]).then_inc(raw_ready[c % SLOTS], 16)
            for g in range(4):
                if g < 3:
                    sp.wait_ge(sem("out_dve"), 2 * g + 2)
                else:
                    sp.wait_ge(sem("out_pool"), 4)
                t = slice(4 * g, 4 * g + 4)
                sp.dma_start(out_d[:, t, :], x[:, t, :]).then_inc(sem("stored"), 16)
            sp.wait_ge(sem("stored"), 64)

        @block.gpsimd
        def _(pool):
            pool.dma_start(cst[:, :], cst_d).then_inc(sem("cst_in"), 16)
            pool.dma_start(cols[:, :], cols_d).then_inc(sem("cols_in"), 16)

            def sum_squares(name, src, ready, nt=8):
                done, s0 = sem("squares"), SQ0[name]
                ready(0)
                nc.gpsimd.tensor_tensor(acc[:, :, :], src(0), src(0), ALU.mult).then_inc(done, 1)
                with pool.Fori(1, nt) as j:
                    ready(j)
                    nc.gpsimd.tensor_tensor(sq[:, :, :], src(j), src(j), ALU.mult).then_inc(done, 1)
                    pool.wait_ge(done, 2 * j + s0)
                    nc.gpsimd.tensor_tensor(acc[:, :, :], acc[:, :, :], sq[:, :, :], ALU.add)\
                        .then_inc(done, 1)
                    pool.wait_ge(done, 2 * j + (s0 + 1))

            def pair(t, first=0):
                return lambda j: t[:, sl(2 * j + first, 2), :]

            with_mem = sem("squares")
            for j in range(8):
                pool.wait_ge(sem(f"mem_in{j // 2}"), 16)
                to = sq if j else acc
                nc.gpsimd.tensor_tensor(to[:, :, :], pair(x)(j), pair(x)(j), ALU.mult).then_inc(with_mem, 1)
                if j:
                    pool.wait_ge(with_mem, 2 * j)
                    nc.gpsimd.tensor_tensor(acc[:, :, :], acc[:, :, :], sq[:, :, :], ALU.add)\
                        .then_inc(with_mem, 1)
                    pool.wait_ge(with_mem, 2 * j + 1)
            pool.wait_ge(h_ready, HFILL["mem"] + KT)
            pool.dma_start(x[:, :, :], xT).then_inc(sem("x_in"), 16)
            pool.wait_ge(sem("rms_ready"), NORM["mem"])
            sum_squares("mix", pair(x), lambda j: pool.wait_ge(sem("x_in"), 16))

            pool.wait_ge(sem("qkv_ready"), 12)
            def copy_v(it):
                if not isinstance(it, int):
                    pool.wait_ge(sem("kv_token_major"), it)
                nc.gpsimd.tensor_copy(vs[:, :, :], qkv[:, sl(2 * it + 16, 2), :]).then_inc(sem("vs_ready"), 1)
            loop(pool, 4, copy_v, first=True)

            pool.wait_ge(sem("gdn_y"), 8)
            pool.dma_start(x[:, :, :], xT).then_inc(sem("x_again"), 16)
            sum_squares("xa", pair(x), lambda j: pool.wait_ge(evacuated, j + (UNIT0["mixo"] + 1)))

            def copy_vh(h):
                if not isinstance(h, int):
                    pool.wait_ge(sem("xa_pv"), h)
                nc.gpsimd.tensor_copy(vh[:, :, :], vx[:, :, sl(512 * h, 512)]).then_inc(sem("vh_ready"), 1)
            loop(pool, XH, copy_vh, first=True)
            sum_squares("ffn", pair(x), lambda j: pool.wait_ge(evacuated, j + (UNIT0["xo"] + 1)))
            pool.wait_ge(sem("g_ready"), FT // 2)
            pool.dma_start(pos[:, :], pos_d.partition_broadcast(P)).then_inc(sem("pos_in"), 16)

            ps = sem("pre_squares")

            def gains(name, j):
                return cols[:, sl(COLS[name] + 2 * j, 2)].unsqueeze(2).to_broadcast([P, 2, S])

            def pre_squares(j):
                first = isinstance(j, int)
                pool.wait_ge(evacuated, j + (UNIT0["down2"] + 1))
                def step(out, a, b, op):
                    nc.gpsimd.tensor_tensor(out, a, b, op).then_inc(ps, 1)
                xp = pair(x)(j)
                if first:
                    step(acc[:, :, :], xp, xp, ALU.mult)
                else:
                    step(sq[:, :, :], xp, xp, ALU.mult)
                    pool.wait_ge(ps, 5 * j - 1)
                    step(acc[:, :, :], acc[:, :, :], sq[:, :, :], ALU.add)
                    pool.wait_ge(ps, 5 * j)
                k = 1 if first else 5 * j
                to = acc2 if first else sq
                step(to[:, :, :], xp, gains("fin", j), ALU.mult)
                pool.wait_ge(ps, k + 1)
                step(to[:, :, :], to[:, :, :], to[:, :, :], ALU.mult)
                pool.wait_ge(ps, k + 2)
                if not first:
                    step(acc2[:, :, :], acc2[:, :, :], sq[:, :, :], ALU.add)
                    pool.wait_ge(ps, 5 * j + 3)
            pre_squares(0)
            with pool.Fori(1, 8) as j:
                pre_squares(j)
            pool.wait_ge(sem("pre_dve"), 1)
            sum_squares("gq", pair(lat), lambda j: pool.wait_ge(evacuated, j + (UNIT0["lat"] + 1)), nt=3)
            pool.wait_ge(sem("rms_ready"), NORM["gq"])
            sum_squares("gkv", pair(lat, 6), lambda j: pool.wait_ge(evacuated, j + (UNIT0["lat"] + 4)), nt=2)

            def mla_pair(it):
                pool.wait_ge(evacuated, UNIT0["ukv"] + 8)
                if not isinstance(it, int):
                    pool.wait_ge(sem("ca_pv"), 2 * it - 1)
                nc.gpsimd.tensor_copy(qpair[:, :, :], qnope[:, sl(2 * it, 2)]).then_inc(sem("qpair_ready"), 1)
                nc.gpsimd.tensor_copy(vpair[:, :, :], vm[:, :, sl(256 * it, 256)]).then_inc(sem("vpair_ready"), 1)
            loop(pool, 4, mla_pair, first=True)

            ro, done = sem("post_scaled"), sem("squares")

            def post(j):
                first = isinstance(j, int)
                s0 = SQ0["post"]
                pool.wait_ge(evacuated, j + (UNIT0["out"] + 1))
                yp = pair(y)(j)
                nc.gpsimd.tensor_tensor((acc if first else sq)[:, :, :], yp, yp, ALU.mult).then_inc(done, 1)
                if not first:
                    pool.wait_ge(done, 2 * j + s0)
                    nc.gpsimd.tensor_tensor(acc[:, :, :], acc[:, :, :], sq[:, :, :], ALU.add).then_inc(done, 1)
                pool.wait_ge(done, 1 + s0 if first else 2 * j + (s0 + 1))
                nc.gpsimd.tensor_tensor(yp, yp, gains("post", j), ALU.mult).then_inc(ro, 1)
            loop(pool, 8, post, first=True)
            pool.wait_ge(sem("rsqrt_ready"), NORM["post"])
            pool.wait_ge(ro, 8)
            for n, j in enumerate((6, 7)):
                yp, xp = pair(y)(j), pair(x)(j)
                nc.gpsimd.tensor_tensor(yp, yp, rr[:, :].unsqueeze(1).to_broadcast([P, 2, S]), ALU.mult)\
                    .then_inc(sem("out_pool"), 1)
                pool.wait_ge(sem("out_pool"), 2 * n + 1)
                nc.gpsimd.tensor_tensor(xp, xp, yp, ALU.add).then_inc(sem("out_pool"), 1)

        @block.tensor
        def _(pe):
            def mm(out, lhsT, rhs, start=True, stop=True):
                return nc.tensor.matmul(out, lhsT, rhs, start=start, stop=stop, skip_group_check=True)

            def turn(out, in_, idn):
                return nc.tensor.transpose(out, in_, idn)

            def unit(name, it, n, j, K=KT, tokens=False, src=None, hwait=None, step=None,
                     narrow=False, hoff=0, gwait=None):
                hi, lo = src or (h_hi, h_lo)
                u = UNIT0[name] + j
                blk0 = j * K if isinstance(it, int) and it == 0 else j * K
                if isinstance(it, int):
                    blk0 += it * n * K
                    if UNIT0[name] + n * it + j >= 2:
                        pe.wait_ge(evacuated, UNIT0[name] + n * it + j - 1)
                else:
                    pe.wait_ge(evacuated, n * it + (u - 1))
                per = 0 if isinstance(it, int) else n * K // BLK
                for k in range(K):
                    blk = blk0 + (k // 2 if narrow else k)
                    half = (k % 2) * P if narrow else 0
                    c, sub = CHUNK0[name] + blk // BLK, blk % BLK
                    w0 = sub * BW + half
                    slot = c % SLOTS
                    if (sub == 0 or k == 0) and half == 0:
                        pe.wait_ge(lo_ready, per * it + (c + 1))
                    if hwait is not None:
                        pe.wait_ge(h_ready, hwait + k + 1)
                    if gwait is not None and k % 2 == 0:
                        pe.wait_ge(sem("g_ready"), gwait + k // 2 + 1)
                    for t in range(1 if narrow else 2):
                        o = bank[(UNIT0[name] + j + (n * it if isinstance(it, int) else 0)) % 2][:, t, :]
                        if tokens:
                            wh, wl = w_hi[:, slot, w0:w0 + BW], w_lo[:, slot, w0:w0 + BW]
                            ah = hi[:, hoff + k, t * P:(t + 1) * P]
                            al = lo[:, hoff + k, t * P:(t + 1) * P]
                            mm(o, ah, wh, k == 0 and t == 0, False)
                            mm(o, al, wh, False, False)
                            last = mm(o, ah, wl, False, k == K - 1)
                        else:
                            wh = w_hi[:, slot, w0 + t * P:w0 + (t + 1) * P]
                            wl = w_lo[:, slot, w0 + t * P:w0 + (t + 1) * P]
                            mm(o, wh, hi[:, hoff + k, :], k == 0 and t == 0, False)
                            mm(o, wh, lo[:, hoff + k, :], False, False)
                            last = mm(o, wl, hi[:, hoff + k, :], False, k == K - 1)
                    if sub == BLK - 1 and (not narrow or half):
                        last.then_inc(w_used, 1)
                    elif k == K - 1:
                        last.then_inc(sem("mid_chunk"), 1)
                    if step is not None and sub % 2 == 1:
                        step(K // BLK * 2 * j + k // 2)

            def token_sums(a, out):
                for t in range(2):
                    for i in range(2):
                        last = mm(out[:, t:t + 1], a[:, i, t * P:(t + 1) * P], ones[:, 0:1], i == 0, i == 1)
                return last

            def norm_sum(name, nt=8, columns=False):
                pe.wait_ge(sem("squares"), SQ0[name] + 2 * nt - 1)
                if NORM[name] > 1:
                    pe.wait_ge(sem("rms_ready"), NORM[name] - 1)
                mm(pb[5][:, 0, :], ones, acc[:, 0, :], True, False)
                last = mm(pb[5][:, 0, :], ones, acc[:, 1, :], False, True)
                if columns:
                    last = token_sums(acc, pb[5][:, 1, 0:2])
                last.then_inc(sem("norm_sum"), 1)

            def gdn(g, it):
                if g == 0:
                    pe.wait_ge(sem("qk_squares"), 2 * it + 2)
                    mm(pb4[0], ones, dec[:, :, :])
                    mm(pb4[1], ones, aT[:, :, :]).then_inc(sem("qk_sums"), 1)
                elif g == 1:
                    pe.wait_ge(sem("qk_normed"), 2 * it + 2)
                    for b in range(4):
                        kb = kn[:, b // 2, (b % 2) * P:(b % 2 + 1) * P]
                        mm(pb4[0][:, b], kb, kb)
                    for b in range(4):
                        kb, qb = (t[:, b // 2, (b % 2) * P:(b % 2 + 1) * P] for t in (kn, qn))
                        last = mm(pb4[1][:, b], kb, qb)
                    last.then_inc(sem("grams"), 1)
                elif g == 2:
                    pe.wait_ge(sem("head_rows"), 4 * it + 4)
                    mm(pb4[2], ones[0:8, :], rows[0:8, 2:4, :].rearrange("p a b -> p (a b)"))
                    mm(pb4[3], ones[32:40, :], rows[32:40, 2:4, :].rearrange("p a b -> p (a b)"))\
                        .then_inc(sem("rows_spread"), 1)
                    for i in range(2):
                        turn(pb4[4][:, i], kn[:, i, 0:P], ident)
                    pe.wait_ge(sem("vs_ready"), it + 1)
                    for b in range(4):
                        last = turn(pb4[5][:, b], vs[:, b // 2, (b % 2) * P:(b % 2 + 1) * P], ident)
                    last.then_inc(sem("kv_token_major"), 1)
                elif g == 3:
                    pe.wait_ge(sem("inv0_ready"), it + 1)
                    for b in range(4):
                        last = turn(pb4[0][:, b], invT[:, b], ident)
                    last.then_inc(sem("inv0_turned"), 1)
                elif g < 16 and g % 2 == 0:
                    l = (g - 4) // 2
                    pe.wait_ge(sem("level_part"), 6 * it + (l + 1))
                    if l == 0:
                        pe.wait_ge(sem("inv0_copied"), it + 1)
                    else:
                        pe.wait_ge(sem("inv_updated"), 11 * it + 2 * l)
                    for b in range(4):
                        last = mm(pb4[1][:, b], lv[:, b], inv[:, b])
                    last.then_inc(sem("level_product"), 1)
                elif g < 16:
                    l = (g - 5) // 2
                    pe.wait_ge(sem("level_copied"), 6 * it + (l + 1))
                    if l < 5:
                        for b in range(4):
                            mm(pb4[2][:, b], invT[:, b], lp[:, b])
                    for b in range(4):
                        last = mm(pb4[3][:, b], lp[:, b], invT[:, b])
                    last.then_inc(sem("level_update"), 1)
                elif g == 16:
                    pe.wait_ge(sem("inv_updated"), 11 * it + 11)
                    pe.wait_ge(sem("kv_scaled"), 6 * it + 6)
                    for i in range(2):
                        last = mm(pb4[0][:, i], invT[:, 2 * i], vb[:, 2 * i])
                    last.then_inc(sem("new0"), 1)
                elif g == 17:
                    pe.wait_ge(sem("new_copied"), 2 * it + 1)
                    for i in range(2):
                        last = mm(pb4[1][:, i], kd[:, i], vn[:, 2 * i])
                    last.then_inc(sem("state"), 1)
                elif g == 18:
                    pe.wait_ge(sem("state_copied"), it + 1)
                    for i in range(2):
                        last = mm(pb4[2][:, i], kn[:, i, P:2 * P], s1[:, i])
                    last.then_inc(sem("k_state"), 1)
                elif g == 19:
                    pe.wait_ge(sem("rest_ready"), 2 * it + 2)
                    for i in range(2):
                        last = mm(pb4[3][:, i], invT[:, 2 * i + 1], r1[:, i])
                    last.then_inc(sem("new1"), 1)
                elif g == 20:
                    pe.wait_ge(sem("new_copied"), 2 * it + 2)
                    pe.wait_ge(sem("att_ready"), 3 * it + 3)
                    for b in range(4):
                        last = mm(pb4[4][:, b], vn[:, b], attT[:, b], True, b % 2 == 0)
                        if b % 2:
                            last = mm(pb4[4][:, b], s1[:, b // 2], qd[:, b // 2], False, True)
                    last.then_inc(sem("gdn_out"), 1)
                elif g == 21:
                    pe.wait_ge(sem("out_squares"), it + 1)
                    mm(pb[5][:, :, :], ones, osq[:, :, :]).then_inc(sem("out_sums"), 1)

            def xa(a, h):
                if a == 0:
                    pe.wait_ge(evacuated, 2 * h + (UNIT0["xq"] + 2))
                    for t in range(2):
                        for kk in range(4):
                            last = mm(pb[0][:, t, :], xq[:, kk, t * P:(t + 1) * P],
                                      kx[:, sl(4 * h + kk, 1), :], kk == 0, kk == 3)
                    last.then_inc(sem("xa_scores"), 1)
                elif a == 1:
                    pe.wait_ge(sem("xa_prob"), 2 * h + 2)
                    for t in range(2):
                        for m in range(2):
                            last = turn(pb[1][:, m, t * P:(t + 1) * P], pr[:, t, m * P:(m + 1) * P], ident)
                    last.then_inc(sem("xa_turned"), 1)
                else:
                    pe.wait_ge(sem("xa_prob_copied"), h + 1)
                    pe.wait_ge(sem("vh_ready"), h + 1)
                    for jj in range(4):
                        for m in range(2):
                            last = mm(pb[2 + jj // 2][:, jj % 2, :], vh[:, m, jj * P:(jj + 1) * P],
                                      pT[:, m, :], m == 0, m == 1)
                    last.then_inc(sem("xa_pv"), 1)

            def ca(a, kind, it):
                def n(k):
                    return 2 * k * it + (k if kind == "mla" else 0)
                if a == 0:
                    if kind == "fox":
                        pe.wait_ge(sem("forget_rows"), 2 * it)
                        mm(pb4[2], ones[0:8, :], rows[0:8, 2:4, :].rearrange("p a b -> p (a b)"))
                        for i in range(2):
                            for t in range(2):
                                last = mm(pb[i][:, t, :], fq[:, i, t * P:(t + 1) * P], fk[:, i, :])
                    else:
                        pe.wait_ge(sem("mla_q_masked"), 2 * it + 2)
                        pe.wait_ge(sem("qpair_ready"), it + 1)
                        for i in range(2):
                            for t in range(2):
                                q = slice(t * P, (t + 1) * P)
                                mm(pb[i][:, t, :], qpair[:, i, q], knope[:, sl(2 * it + i, 1), :], True, False)
                                last = mm(pb[i][:, t, :], qmask[:, i, q], kr[:, :], False, True)
                    last.then_inc(sem("ca_scores"), 1)
                elif a == 1:
                    pe.wait_ge(sem("ca_prob"), n(4))
                    for i in range(2):
                        for t in range(2):
                            for m in range(2):
                                last = turn(pb[3 + i][:, m, t * P:(t + 1) * P],
                                            pr2[:, 2 * i + t, m * P:(m + 1) * P], ident)
                    last.then_inc(sem("ca_turned"), 1)
                else:
                    pe.wait_ge(sem("ca_prob_copied"), n(2))
                    if kind == "mla":
                        pe.wait_ge(sem("vpair_ready"), it + 1)
                    v = fv if kind == "fox" else vpair
                    for i in range(2):
                        for m in range(2):
                            last = mm(pb[5][:, i, :], v[:, m, i * P:(i + 1) * P], pT2[:, 2 * i + m, :],
                                      m == 0, m == 1)
                    last.then_inc(sem("ca_pv"), 1)

            pe.wait_ge(sem("cst_in"), 16)

            def phase(name, count, norm=None, hwait=None, columns=False, **kw):
                unit(name, 0, 2, 0, hwait=hwait, **kw)
                if norm is not None:
                    norm_sum(norm, columns=columns)
                unit(name, 0, 2, 1, **kw)
                with pe.Fori(1, count // 2) as it:
                    for j in range(2):
                        unit(name, it, 2, j, **kw)

            phase("xk", 8, norm="mem", hwait=HFILL["mem"], columns=True)
            with pe.Fori(0, 4) as it:
                for j in range(2):
                    unit("xv", it, 2, j, tokens=True)

            unit("ba", 0, 1, 0, K=KT, narrow=True, hwait=HFILL["mix"])
            norm_sum("mix")
            with pe.Fori(0, 6) as it:
                for j in range(2):
                    unit("qkv", it, 2, j)
            pe.wait_ge(sem("ba_dve"), 6)
            pe.wait_ge(sem("ba_act"), 4)
            for n in range(2):
                g_last = turn(pb[5][:, 0, 8 * n:8 * n + 8], rows[0:8, 0, n * P:(n + 1) * P], ident[0:8, 0:8])
            g_last.then_inc(sem("ba_cols"), 1)
            for n in range(2):
                last = turn(pb[4][:, 0, 8 * n:8 * n + 8], rows[32:40, 0, n * P:(n + 1) * P],
                            ident[32:40, 32:40])
            last.then_inc(sem("ba_cols"), 1)
            with pe.Fori(0, 4) as it:
                for j in range(4):
                    def step(s):
                        if s < 22:
                            gdn(s, it)
                    unit("gdn", it, 4, j, step=step)

            phase("mixo", 8, hwait=HFILL["y"])

            def xq_units(it):
                def step(s):
                    if isinstance(it, int):
                        return
                    if s == 0:
                        xa(0, it - 1)
                    elif s == 5:
                        xa(1, it - 1)
                    elif s == 9:
                        xa(2, it - 1)
                for j in range(2):
                    unit("xq", it, 2, j, hwait=HFILL["xa"] if isinstance(it, int) and j == 0 else None, step=step)
                    if isinstance(it, int) and j == 0:
                        norm_sum("xa")
            xq_units(0)
            with pe.Fori(1, 4) as it:
                xq_units(it)
            for a in range(3):
                xa(a, XH - 1)

            phase("xo", 8, hwait=HFILL["o"])
            for s, nt in enumerate(SEGS):
                if s == 0:
                    phase("up0", nt, norm="ffn", hwait=HFILL["ffn"])
                else:
                    with pe.Fori(0, nt // 2) as it:
                        for j in range(2):
                            unit(f"up{s}", it, 2, j)
                g0 = sum(SEGS[:s]) // 2
                n = 2 if nt == KT else 4
                for j in range(n):
                    unit(f"down{s}", 0, n, j, K=nt, src=(g_hi, g_lo), gwait=g0 if j == 0 else None)
                with pe.Fori(1, 8 // n) as it:
                    for j in range(n):
                        unit(f"down{s}", it, n, j, K=nt, src=(g_hi, g_lo))
            unit("lat", 0, 2, 0, hwait=HFILL["pre"])
            pe.wait_ge(sem("pre_squares"), 5 * 8 - 2)
            for i, a in enumerate((acc, acc2)):
                mm(pb[5][:, i, :], ones, a[:, 0, :], True, False)
                mm(pb[5][:, i, :], ones, a[:, 1, :], False, True)
                last = token_sums(a, pb[4][:, 0, 2 * i:2 * i + 2])
            last.then_inc(sem("norm_sum"), 1)
            unit("lat", 0, 2, 1)
            with pe.Fori(1, 3) as it:
                for j in range(2):
                    unit("lat", it, 2, j)
            pe.wait_ge(sem("pre_dve"), 1)
            norm_sum("gq", 3)
            latents = (lh_hi, lh_lo)
            for u in range(6):
                unit("uq", 0, 6, u, K=6, src=latents, hwait=HFILL["gq"] if u == 0 else None)
                if u == 2:
                    norm_sum("gkv", 2, columns=True)
            for u in range(8):
                unit("ukv", 0, 8, u, K=4, tokens=u >= 4, src=latents, hoff=6,
                     hwait=HFILL["gkv"] if u == 0 else None)
                if u == 3:
                    pe.wait_ge(sem("forget_dve"), 6)
                    for n in range(2):
                        last = turn(pb[2][:, 0, 8 * n:8 * n + 8], rows[0:8, 0, n * P:(n + 1) * P],
                                    ident[0:8, 0:8])
                    last.then_inc(sem("forget_cols"), 1)

            FOX_AT, MLA_AT = {1: 0, 6: 1, 10: 2}, {15: 0, 20: 1, 24: 2}

            def fox(it):
                def step(s):
                    if s in FOX_AT and not isinstance(it, int):
                        ca(FOX_AT[s], "fox", it)
                    elif s in MLA_AT:
                        ca(MLA_AT[s], "mla", it)
                for j in range(4):
                    unit("fox", it, 4, j, tokens=j == 3, step=step)
            fox(0)
            with pe.Fori(1, 4) as it:
                fox(it)
            for j in range(4):
                unit("gm", 0, 4, j, step=lambda s: ca(FOX_AT[s], "fox", 4) if s in FOX_AT else None)
            phase("out", 8, hwait=HFILL["o2"])
            norm_sum("post")

        pair4 = "p (a b) c -> p a (b c)"
        CA_FOX, CA_MLA = {1: 0, 4: 1, 6: 2}, {8: 0, 11: 1, 13: 2}

        def smc(c, n=1):
            return sm[:, sl(c, n)]

        @block.scalar
        def _(act):
            def A(out, in_, func, bias=0.0, scale=1.0, **kw):
                return nc.scalar.activation(out, in_, func, bias=bias, scale=scale, **kw)

            def split(c, per=0, it=0):
                if isinstance(it, int):
                    c, it, per = c + per * it, 0, 0
                    if c >= N_CHUNKS:
                        return
                s = c % SLOTS
                act.wait_ge(raw_ready[s], 16 * per // SLOTS * it + 16 * (c // SLOTS + 1))
                if c >= SLOTS:
                    act.wait_ge(w_used, per * it + (c - SLOTS + 1))
                A(w_hi[:, s], raw[:, s], ACT.Copy).then_inc(hi_ready, 1)

            def units(name, it, n, evac=None, react=None, K=KT, j0=0):
                m = n * K // BLK
                for j in range(j0, n):
                    for i in range(K // BLK):
                        if react is not None:
                            react(j, i)
                        if i == K // BLK - 1 and evac is not None:
                            evac(j)
                        split(CHUNK0[name] + j * K // BLK + i + SLOTS, m, it)

            def done(name, it, n, j, K=KT):
                act.wait_ge(w_used, n * K // BLK * it + (CHUNK0[name] + (j + 1) * K // BLK))

            def norm_rms(name, width, out=rr, column=None):
                act.wait_ge(sem("norm_sum"), NORM[name])
                a = A(out[:, :], pb[5][:, 0, :], ACT.Sqrt, bias=c1("eps"), scale=1.0 / width)
                if column is not None:
                    a = A(smc(column, 2), pb[5][:, 1, 0:2], ACT.Sqrt, bias=c1("eps"), scale=1.0 / width)
                a.then_inc(sem("rms_ready"), 1)

            def hi(name, k, out, in_):
                if name in TN0:
                    act.wait_ge(sem("tn_ready"), TN0[name] + k + 1)
                    in_ = tn[:, k % 4]
                A(out, in_, ACT.Copy).then_inc(sem("h_hi_ready"), 1)

            def fill(name, after, g, src=None):
                act.wait_ge(w_used, after - 3 + g)
                for k in range(4 * g, 4 * g + 4):
                    hi(name, k, h_hi[:, k], None if src is None else src[:, k])

            def fill_latent(name, k0, k1, at_=0):
                for k in range(k0, k1):
                    hi(name, k, lh_hi[:, at_ + k], None)

            def phase(name, count, n=2, evac=None, first=None, last=None, K=KT):
                def ev(it):
                    def e(j):
                        if first is not None and isinstance(it, int) and it == 0 and j == 0:
                            first()
                        if evac is not None:
                            evac(it, j)
                    return e

                def re(j, i):
                    g = i - 1 + 4 - K // BLK
                    if j == n - 1 and g >= 0:
                        last(g)
                its = count // n
                lo_ = 0 if first is None else 1
                up_ = its if last is None else its - 1
                if lo_:
                    units(name, 0, n, ev(0), K=K)
                if up_ > lo_:
                    with act.Fori(lo_, up_) as it:
                        units(name, it, n, ev(it), K=K)
                if last is not None:
                    units(name, its - 1, n, ev(its - 1), re, K=K)
                    last(3)

            for c in range(SLOTS):
                split(c)
                if c == 0:
                    act.wait_ge(sem("cst_in"), 16)
                    act.wait_ge(sem("cols_in"), 16)
                for k in range(4 * c, 4 * c + 4):
                    hi("mem", k, h_hi[:, k], None)
            phase("xk", 8, first=lambda: norm_rms("mem", D, column=R_COL))
            phase("xv", 8, last=lambda g: fill("mix", CHUNK0["ba"], g))
            split(CHUNK0["ba"] + SLOTS)
            norm_rms("mix", D)
            act.wait_ge(evacuated, UNIT0["ba"] + 1)
            r = rows
            A(r[0:8, 2], r[0:8, 1], ACT.Abs, bias=col("dtb", 0, slice(0, 8))).then_inc(sem("ba_act"), 1)
            A(r[32:40, 0], r[32:40, 1], ACT.Sigmoid).then_inc(sem("ba_act"), 1)
            A(sm[0:8, EA_COL:EA_COL + 1], col("alog", 0, slice(0, 8)), ACT.Exp).then_inc(sem("ba_act"), 1)
            act.wait_ge(sem("ba_act"), 1)
            A(r[0:8, 2], r[0:8, 2], ACT.Exp, scale=-1.0).then_inc(sem("ba_act"), 1)
            split(CHUNK0["ba"] + SLOTS + 1)
            act.wait_ge(sem("ba_dve"), 1)
            A(r[0:8, 2], r[0:8, 2], ACT.Ln).then_inc(sem("ba_act"), 1)

            def qkv_body(it):
                def evac(j):
                    act.wait_ge(sem("bank_scaled"), 2 * it + (j + 1))
                    b = bank[(UNIT0["qkv"] + j) % 2]
                    c = (cy, cz)[j]
                    for t in range(2):
                        A(c[:, t], b[:, t], ACT.Copy, scale=col("gconv", 24 * 3 + (4 * it + (2 * j + t))))\
                            .then_inc(sem("qkv_tap0"), 1)
                    act.wait_ge(evacuated, 2 * it + (UNIT0["qkv"] + j + 1))
                    A(qkv[:, sl(4 * it + 2 * j, 2)], c[:, :], ACT.Silu).then_inc(sem("qkv_ready"), 1)
                units("qkv", it, 2, evac)
            with act.Fori(0, 6) as it:
                qkv_body(it)

            act.wait_ge(sem("ba_dve"), 7)
            A(smc(EG_COL, 8), smc(G_COL + 8, 8), ACT.Exp).then_inc(sem("ba_act"), 1)

            def gdn(g, it):
                if g == 0:
                    A(dec[:, :, :], qkv[:, sl(2 * it, 2)].rearrange("p a (b c) -> p (a b) c", b=2), ACT.Square)\
                        .then_inc(sem("qk_squares"), 1)
                    A(aT[:, :, :], qkv[:, sl(2 * it + 8, 2)].rearrange("p a (b c) -> p (a b) c", b=2), ACT.Square)\
                        .then_inc(sem("qk_squares"), 1)
                    act.wait_ge(sem("qk_sums"), it + 1)
                    A(inv[:, :, :], pb4[0], ACT.Sqrt, bias=c1("eps")).then_inc(sem("qk_rms"), 1)
                    A(invT[:, :, :], pb4[1], ACT.Sqrt, bias=c1("eps")).then_inc(sem("qk_rms"), 1)
                elif g == 2:
                    act.wait_ge(sem("dec_args"), 6 * it + 6)
                    A(dec[:, :, :], dec[:, :, :], ACT.Exp).then_inc(sem("dec_ready"), 1)
                    A(qd[:, :, :], pb4[2].rearrange("p (i n) c -> p n i c", n=2)[:, 1], ACT.Exp)\
                        .then_inc(sem("q_decay"), 1)
                    A(smc(KD_COL, 2), smc(KD_ARG, 2), ACT.Exp).then_inc(sem("k_decay"), 1)
                    act.wait_ge(sem("kv_token_major"), it + 1)
                    for b in range(4):
                        A(vb[:, b], pb4[5][:, b], ACT.Copy, scale=smc(B_COL + (b % 2) * 8 + b // 2 + 2 * it))\
                            .then_inc(sem("kv_scaled"), 1)
                    act.wait_ge(sem("k_decay"), it + 1)
                    for i in range(2):
                        A(kd[:, i], pb4[4][:, i], ACT.Copy, scale=smc(KD_COL + i)).then_inc(sem("kv_scaled"), 1)
                elif g == 3:
                    act.wait_ge(sem("inv0_turned"), it + 1)
                    A(inv[:, :, :], pb4[0], ACT.Copy).then_inc(sem("inv0_copied"), 1)
                elif 4 <= g < 16 and g % 2 == 0:
                    act.wait_ge(sem("level_product"), 6 * it + ((g - 4) // 2 + 1))
                    A(lp[:, :, :], pb4[1], ACT.Copy).then_inc(sem("level_copied"), 1)
                elif g in (16, 19):
                    n = (g - 16) // 3
                    act.wait_ge(sem(f"new{n}"), it + 1)
                    A(vn[:, :, :].rearrange("p (i n) c -> p n i c", n=2)[:, n], pb4[3 * n][:, 0:2], ACT.Copy)\
                        .then_inc(sem("new_copied"), 1)
                elif g == 17:
                    act.wait_ge(sem("state"), it + 1)
                    A(s1[:, :, :], pb4[1][:, 0:2], ACT.Copy).then_inc(sem("state_copied"), 1)
                elif g == 20:
                    act.wait_ge(sem("gdn_out"), it + 1)
                    A(osq[:, :, :], pb[4][:, :, :], ACT.Square).then_inc(sem("out_squares"), 1)
                elif g == 21:
                    act.wait_ge(sem("out_sums"), it + 1)
                    A(osq[:, :, :], pb[5][:, :, :], ACT.Sqrt, bias=c1("eps"), scale=1.0 / P)\
                        .then_inc(sem("out_rms"), 1)

            def gdn_unit(it, fills=False):
                def react(j, i):
                    for g in (8 * j + 2 * i, 8 * j + 2 * i + 1):
                        if g < 22:
                            gdn(g, it)
                    if fills and j == 3 and i > 0:
                        fill_y(i - 1)

                def evac(j):
                    if j == 0:
                        act.wait_ge(evacuated, 4 * it + (UNIT0["gdn"] + 1))
                        A(zs[:, :], zs[:, :], ACT.Silu).then_inc(sem("z_ready"), 1)
                    elif j == 3:
                        act.wait_ge(evacuated, 4 * it + (UNIT0["gdn"] + 4))
                        for t in range(2):
                            A(cv[:, t], cw[:, t], ACT.Copy, scale=col("sconv", 8 * 2 + (2 * it + t)))\
                                .then_inc(sem("sc_tap0"), 1)
                return react, evac

            def fill_y(g):
                if g < 2:
                    act.wait_ge(sem("gdn_y"), 4 * g + 4)
                else:
                    act.wait_ge(sem("sc_y"), 2 * g - 2)
                fill("y", CHUNK0["mixo"], g, y)

            act.wait_ge(sem("qkv_ready"), 12)
            with act.Fori(0, 3) as it:
                react, evac = gdn_unit(it)
                units("gdn", it, 4, evac, react)
            react, evac = gdn_unit(3, fills=True)
            units("gdn", 3, 4, evac, react)
            fill_y(3)
            phase("mixo", 8, last=lambda g: fill("xa", CHUNK0["xq"], g))

            XSC = 512 ** -0.5

            def xa(a, h):
                if a == 0:
                    act.wait_ge(sem("xa_nmax"), 2 * h + 2)
                    for t in range(2):
                        A(pr[:, t], pb[0][:, t], ACT.Exp, bias=smc(NMAX + t), scale=XSC,
                          accum_out=smc(RSUM + t)).then_inc(sem("xa_exp"), 1)
                elif a == 1:
                    act.wait_ge(sem("xa_turned"), h + 1)
                    A(pT[:, 0:2], pb[1][:, :, :], ACT.Copy).then_inc(sem("xa_prob_copied"), 1)

            units("xq", 0, 2, lambda j: norm_rms("xa", D) if j == 0 else None)

            def xq_react(it):
                def react(j, i):
                    if (j, i) == (0, 0):
                        xa(0, it - 1)
                    elif (j, i) == (0, 2):
                        xa(1, it - 1)
                    elif isinstance(it, int) and j == 1 and i > 0:
                        fill_o(i - 1)
                return react

            def fill_o(g):
                act.wait_ge(sem("xa_o"), 2 * g + 2)
                fill("o", CHUNK0["xo"], g, y)
            with act.Fori(1, 3) as it:
                units("xq", it, 2, react=xq_react(it))
            units("xq", 3, 2, react=xq_react(3))
            xa(0, XH - 1)
            xa(1, XH - 1)
            fill_o(3)
            phase("xo", 8, last=lambda g: fill("ffn", CHUNK0["up0"], g))
            tile0 = 0
            for s, nt in enumerate(SEGS):
                name = f"up{s}"
                g0 = sum(SEGS[:s]) // 2

                def evac(it, j):
                    act.wait_ge(sem("bank_scaled"), 2 * it + (12 + 2 * g0 + j + 1))
                    b = bank[(UNIT0[name] + j) % 2]
                    c = (cy, cw)[j]
                    for t in range(2):
                        A(c[:, t], b[:, t], ACT.Copy,
                          scale=col("fconv", 88 * 2 + 44 * j + tile0 + t + 2 * it)).then_inc(sem("up_tap0"), 1)
                    act.wait_ge(evacuated, 2 * it + (UNIT0[name] + j + 1))
                    if j == 0:
                        A(cz[:, :], cy[:, :], ACT.Silu).then_inc(sem("gate_ready"), 1)
                    else:
                        act.wait_ge(sem("gated"), it + (g0 + 1))
                        A(g_hi[:, sl(2 * it, 2)], cv[:, :], ACT.Copy).then_inc(sem("g_hi_ready"), 1)
                phase(name, nt, evac=evac, first=(lambda: norm_rms("ffn", D)) if s == 0 else None)
                tile0 += nt
                if nt == KT:
                    phase(f"down{s}", 8)
                    act.wait_ge(w_used, CHUNK0[f"down{s}"] + 2 * nt)
                else:
                    phase(f"down{s}", 8, n=4, K=nt, last=lambda g: fill("pre", CHUNK0[f"down{s}"] + 3, g))

            def pre_rms():
                act.wait_ge(sem("norm_sum"), NORM["pre"])
                A(rf[:, :], pb[5][:, 0, :], ACT.Sqrt, bias=c1("eps"), scale=1.0 / D)
                A(smc(RF_COL, 2), pb[4][:, 0, 0:2], ACT.Sqrt, bias=c1("eps"), scale=1.0 / D)\
                    .then_inc(sem("pre_rms"), 1)
                act.wait_ge(sem("pre_dve"), 1)
                A(rr[:, :], rr[:, :], ACT.Sqrt, bias=c1("eps"), scale=1.0 / D)
                A(smc(R_COL, 2), smc(R2_COL, 2), ACT.Sqrt, bias=c1("eps"), scale=1.0 / D)\
                    .then_inc(sem("rms_ready"), 1)
            units("lat", 0, 2, lambda j: pre_rms() if j == 0 else None)

            def lat_react(it):
                def react(j, i):
                    if (it, j, i) == (1, 0, 2):
                        act.wait_ge(sem("rope_dve"), 8)
                        A(qm[:, :], sinr[:, :], ACT.Abs).then_inc(sem("rope_act"), 1)
                        A(sinr[:, :], sinr[:, :], ACT.Sin).then_inc(sem("rope_act"), 1)
                        act.wait_ge(sem("rope_act"), 1)
                        A(cosr[:, :], qm[:, :], ACT.Sin, bias=c1("hpi"), scale=-1.0).then_inc(sem("rope_act"), 1)
                    elif (it, j, i) == (2, 0, 1):
                        fill_latent("gq", 0, 4)
                    elif (it, j, i) == (2, 0, 2):
                        fill_latent("gq", 4, 6)
                    elif (it, j, i) == (2, 1, 1):
                        fill_latent("gkv", 0, 4, 6)
                return react
            for it in (1, 2):
                units("lat", it, 2, react=lat_react(it))
            norm_rms("gq", 768, out=rq)
            for c in range(9 + 8):
                split(CHUNK0["uq"] + c + SLOTS)
                if c == 0:
                    act.wait_ge(evacuated, UNIT0["lat"] + 6)
                    A(qm[0:64, :], lat[64:128, 10], ACT.Copy).then_inc(sem("kr_swap"), 1)
                    A(qm[64:128, :], lat[0:64, 10], ACT.Copy).then_inc(sem("kr_swap"), 1)
                    A(r[0:8, 2], lat[0:8, 11], ACT.Abs, bias=col("bfor", 0, slice(0, 8))).then_inc(sem("forget_act"), 1)
                    act.wait_ge(sem("forget_act"), 1)
                    A(r[0:8, 2], r[0:8, 2], ACT.Exp, scale=-1.0).then_inc(sem("forget_act"), 1)
                elif c == 1:
                    act.wait_ge(sem("forget_dve"), 1)
                    A(r[0:8, 2], r[0:8, 2], ACT.Ln).then_inc(sem("forget_act"), 1)
                elif c == 6:
                    norm_rms("gkv", 512, out=rkv, column=RKV_COL)
                elif c in (10, 12):
                    for p in range((c - 10), (c - 10) + 2):
                        act.wait_ge(evacuated, UNIT0["uq"] + (5 if p < 2 else 6))
                        A(tn[0:64, p], lat[64:128, p], ACT.Copy).then_inc(sem("qr_swap"), 1)
                        A(tn[64:128, p], lat[0:64, p], ACT.Copy).then_inc(sem("qr_swap"), 1)

            def ca(a, kind, it):
                def n(k):
                    return 2 * k * it + (k if kind == "mla" else 0)
                if a == 0:
                    act.wait_ge(sem("ca_nmax"), n(1))
                    for q in range(4):
                        A(pr2[:, q], db[:, q], ACT.Exp, bias=smc(NMAX + q), accum_out=smc(RSUM + q))\
                            .then_inc(sem("ca_exp"), 1)
                elif a == 1:
                    act.wait_ge(sem("ca_turned"), n(1))
                    A(pT2[:, 0:2], pb[3][:, :, :], ACT.Copy).then_inc(sem("ca_prob_copied"), 1)

            def fox_react(it, fox=True, mla=True):
                def react(j, i):
                    q = 4 * j + i
                    if q in CA_FOX and fox:
                        ca(CA_FOX[q], "fox", it)
                    elif q in CA_MLA and mla:
                        ca(CA_MLA[q], "mla", it)
                    elif not mla and j == 3 and i > 0:
                        fill_o2(i - 1)
                return react

            def fox_evac(it):
                def evac(j):
                    if j == 2:
                        act.wait_ge(evacuated, 4 * it + (UNIT0["fox"] + 3))
                        A(fg[:, :], fg[:, :], ACT.Silu).then_inc(sem("fg_ready"), 1)
                return evac
            units("fox", 0, 4, fox_evac(0), fox_react(0, fox=False))
            with act.Fori(1, 4) as it:
                units("fox", it, 4, fox_evac(it), fox_react(it))

            def gm_evac(j):
                act.wait_ge(evacuated, UNIT0["gm"] + j + 1)
                A(gg[:, j % 2], gg[:, j % 2], ACT.Silu).then_inc(sem("gate2_ready"), 1)

            def fill_o2(g):
                if g < 2:
                    act.wait_ge(sem("ca_o"), 8)
                else:
                    act.wait_ge(sem("o_gated"), 2 * g - 2)
                fill("o2", CHUNK0["out"], g, y)
            units("gm", 0, 4, gm_evac, fox_react(4, mla=False))
            fill_o2(3)
            phase("out", 8, last=lambda g: None)
            norm_rms("post", D)

        @block.vector
        def _(dve):
            V = nc.vector

            def tt(out, a, b, op):
                return V.tensor_tensor(out, a, b, op)

            def split(c, per=0, it=0):
                if isinstance(it, int):
                    c, it, per = c + per * it, 0, 0
                    if c >= N_CHUNKS:
                        return
                s = c % SLOTS
                dve.wait_ge(hi_ready, per * it + (c + 1))
                tt(w_lo[:, s], raw[:, s], w_hi[:, s].bitcast(F32), ALU.subtract).then_inc(lo_ready, 1)

            def units(name, it, n, evac=None, react=None, K=KT):
                m = n * K // BLK
                for j in range(n):
                    for i in range(K // BLK):
                        if react is not None:
                            react(j, i)
                        if i == K // BLK - 1:
                            evac(j)
                        split(CHUNK0[name] + j * K // BLK + i + SLOTS, m, it)

            def done(name, it, n, j, K=KT):
                dve.wait_ge(w_used, n * K // BLK * it + (CHUNK0[name] + (j + 1) * K // BLK))
                return bank[(UNIT0[name] + j + (n * it if isinstance(it, int) else 0)) % 2]

            def copy_to(name, it, n, j, out, K=KT):
                b = done(name, it, n, j, K)
                V.tensor_copy(out, b[:, :, :]).then_inc(evacuated, 1)

            def both(a):
                return a[:, :].unsqueeze(1).to_broadcast([P, 2, S])

            def scale_to(name, it, n, j, out, by=rr):
                b = done(name, it, n, j)
                tt(out, b[:, :, :], both(by), ALU.mult).then_inc(evacuated, 1)

            def scale_tokens(b, out, column=R_COL):
                tt(out, b[:, :, :], smc(column, 2).unsqueeze(2).to_broadcast([P, 2, S]), ALU.mult)\
                    .then_inc(evacuated, 1)

            def scale_bank(name, it, n, j):
                b = done(name, it, n, j)
                tt(b[:, :, :], b[:, :, :], both(rr), ALU.mult).then_inc(sem("bank_scaled"), 1)
                return b

            def add_x(name, it, n, j, K=KT):
                b = done(name, it, n, j, K)
                t = x[:, sl(n * it + j + (n * it + j), 2)] if isinstance(it, int) else x[:, sl(2 * n * it + 2 * j, 2)]
                tt(t, b[:, :, :], t, ALU.add).then_inc(evacuated, 1)

            def rsqrt(name, out=rr, column=None):
                dve.wait_ge(sem("rms_ready"), NORM[name])
                if column is not None:
                    V.reciprocal(smc(column, 2), smc(column, 2))
                V.reciprocal(out[:, :], out[:, :]).then_inc(sem("rsqrt_ready"), 1)
                dve.wait_ge(sem("rsqrt_ready"), NORM[name])

            def fill_scaled(name, k0, k1, src, gain, hi_, lo_, at_=0, gain2=None):
                if HFILL[name] + k0:
                    dve.wait_ge(h_ready, HFILL[name] + k0)
                for k in range(k0, k1):
                    V.tensor_scalar(tn[:, k % 4], src[:, k], col(gain, k), col(gain2, k) if gain2 else None,
                                    ALU.mult, *([ALU.mult] if gain2 else [])).then_inc(sem("tn_ready"), 1)
                for k in range(k0, k1):
                    dve.wait_ge(sem("h_hi_ready"), HFILL[name] + k + 1)
                    tt(lo_[:, at_ + k], tn[:, k % 4], hi_[:, at_ + k].bitcast(F32), ALU.subtract)\
                        .then_inc(h_ready, 1)

            def fill_x(name, prev, g, gain2=None):
                if prev:
                    dve.wait_ge(evacuated, UNIT0[prev] + 2 * g + 2)
                fill_scaled(name, 4 * g, 4 * g + 4, x, "fin" if gain2 else name, h_hi, h_lo, gain2=gain2)

            def fill_y(name, g):
                for k in range(4 * g, 4 * g + 4):
                    dve.wait_ge(sem("h_hi_ready"), HFILL[name] + k + 1)
                    tt(h_lo[:, k], y[:, k], h_hi[:, k].bitcast(F32), ALU.subtract).then_inc(h_ready, 1)

            def phase(name, count, evac, n=2, first=None, last=None, K=KT):
                def ev(it):
                    def e(j):
                        if first is not None and isinstance(it, int) and it == 0 and j == 0:
                            first()
                        evac(it, j)
                    return e

                def re(j, i):
                    g = i - 1 + 4 - K // BLK
                    if j == n - 1 and g >= 0:
                        last(g)
                its = count // n
                lo_ = 0 if first is None else 1
                up_ = its if last is None else its - 1
                if lo_:
                    units(name, 0, n, ev(0), K=K)
                if up_ > lo_:
                    with dve.Fori(lo_, up_) as it:
                        units(name, it, n, ev(it), K=K)
                if last is not None:
                    units(name, its - 1, n, ev(its - 1), re, K=K)
                    last(3)

            def taps(name, b, acc_, wcol, n, base, shifted=None):
                for q in range(2 * n):
                    tap, t = q // 2, q % 2
                    if tap:
                        dve.wait_ge(sem(name), base + (q - 1))
                    V.scalar_tensor_tensor(acc_[:, t, tap + 1:], b[:, t, :S - tap - 1], wcol(tap, t),
                                           acc_[:, t, tap + 1:], ALU.mult, ALU.add)\
                        .then_inc(*((evacuated, 1) if q == 2 * n - 1 and shifted is None else (sem(name), 1)))

            dve.wait_ge(sem("cols_in"), 16)
            for c in range(SLOTS):
                split(c)
                dve.wait_ge(sem(f"mem_in{c}"), 16)
                fill_scaled("mem", 4 * c, 4 * c + 4, x, "mem", h_hi, h_lo)
            phase("xk", 8, lambda it, j: scale_to("xk", it, 2, j, kx[:, sl(4 * it + 2 * j, 2)]),
                  first=lambda: rsqrt("mem", column=R_COL))

            def mix_fill(g):
                if g == 0:
                    dve.wait_ge(sem("x_in"), 16)
                fill_x("mix", None, g)
            phase("xv", 8, lambda it, j: scale_tokens(done("xv", it, 2, j), vx[:, :, sl(512 * it + 256 * j, 256)]),
                  last=mix_fill)
            split(CHUNK0["ba"] + SLOTS)
            r = rows
            dve.wait_ge(w_used, CHUNK0["ba"] + 2)
            rsqrt("mix")
            tt(r[:, 1], bank[UNIT0["ba"] % 2][:, 0], rr[:, :], ALU.mult).then_inc(evacuated, 1)
            split(CHUNK0["ba"] + SLOTS + 1)
            b_dve = sem("ba_dve")
            dve.wait_ge(sem("ba_act"), 4)
            V.tensor_scalar(r[0:8, 2], r[0:8, 2], 1.0, None, ALU.add).then_inc(b_dve, 1)
            V.tensor_scalar(r[0:8, 3], r[0:8, 1], col("dtb", 0, slice(0, 8)), 0.0, ALU.add, ALU.max)\
                .then_inc(b_dve, 1)
            dve.wait_ge(sem("ba_act"), 5)
            dve.wait_ge(b_dve, 2)
            tt(r[0:8, 3], r[0:8, 3], r[0:8, 2], ALU.add).then_inc(b_dve, 1)
            dve.wait_ge(b_dve, 3)
            V.tensor_scalar(r[0:8, 3], r[0:8, 3], sm[0:8, EA_COL:EA_COL + 1], -1.0, ALU.mult, ALU.mult)\
                .then_inc(b_dve, 1)
            dve.wait_ge(b_dve, 4)
            for n in range(2):
                hs = slice(n * P, (n + 1) * P)
                V.tensor_tensor_scan(r[0:8, 0, hs], ones[0:8, :], r[0:8, 3, hs], 0.0, ALU.mult, ALU.add)\
                    .then_inc(b_dve, 1)

            with dve.Fori(0, 6) as it:
                def evac(j):
                    b = scale_bank("qkv", it, 2, j)
                    dve.wait_ge(sem("qkv_tap0"), 4 * it + (2 * j + 2))
                    taps("qkv_taps", b, (cy, cz)[j],
                         lambda tap, t: col("gconv", 24 * (2 - tap) + (4 * it + (2 * j + t))), 3, 10 * it + 5 * j)
                units("qkv", it, 2, evac)

            dve.wait_ge(sem("ba_cols"), 2)
            V.tensor_copy(smc(G_COL, 16), pb[5][:, 0, 0:16]).then_inc(b_dve, 1)
            V.tensor_copy(smc(B_COL, 16), pb[4][:, 0, 0:16]).then_inc(b_dve, 1)
            dve.wait_ge(b_dve, 8)
            dve.wait_ge(sem("ba_act"), 6)
            V.scalar_tensor_tensor(smc(NBEG_COL, 8), smc(B_COL + 8, 8), -1.0, smc(EG_COL, 8),
                                   ALU.mult, ALU.mult).then_inc(b_dve, 1)
            dve.wait_ge(b_dve, 9)

            def lev(l):
                return levT[:, l:l + 1, :].to_broadcast([P, 4, P])

            def level_part(l):
                tt(lv[:, :, :], lev(l + 1), aT[:, :, :], ALU.mult).then_inc(sem("level_part"), 1)

            def gdn(g, it):
                if g == 0:
                    for i in range(2):
                        for p0 in (0, 32):
                            ps = slice(p0, p0 + 8)
                            V.tensor_scalar(r[ps, 2 + i], r[ps, 0],
                                            cst[ps, sl(CST["ident"] + p0 + i + 2 * it, 1)], None, ALU.mult)\
                                .then_inc(sem("head_rows"), 1)
                    dve.wait_ge(sem("qk_rms"), 2 * it + 1)
                    V.reciprocal(inv[:, :, :], inv[:, :, :]).then_inc(sem("qk_rsqrt"), 1)
                    dve.wait_ge(sem("qk_rms"), 2 * it + 2)
                    V.reciprocal(invT[:, :, :], invT[:, :, :]).then_inc(sem("qk_rsqrt"), 1)
                    dve.wait_ge(sem("qk_rsqrt"), 2 * it + 1)
                    V.scalar_tensor_tensor(qn[:, :, :], qkv[:, sl(2 * it, 2)], P ** -0.5,
                                           inv[:, :, :].rearrange(pair4, a=2), ALU.mult, ALU.mult)\
                        .then_inc(sem("qk_normed"), 1)
                    dve.wait_ge(sem("qk_rsqrt"), 2 * it + 2)
                    tt(kn[:, :, :], qkv[:, sl(2 * it + 8, 2)], invT[:, :, :].rearrange(pair4, a=2), ALU.mult)\
                        .then_inc(sem("qk_normed"), 1)
                elif g == 2:
                    dve.wait_ge(sem("rows_spread"), it + 1)
                    for b in range(4):
                        V.tensor_scalar(dec[:, b], pb4[2][:, b], smc(G_COL + (b % 2) * 8 + b // 2 + 2 * it), 0.0,
                                        ALU.subtract, ALU.min).then_inc(sem("dec_args"), 1)
                    for i in range(2):
                        tt(smc(KD_ARG + i), pb4[2][:, 2 * i, P - 1:P], smc(G_COL + i + 2 * it), ALU.subtract)\
                            .then_inc(sem("dec_args"), 1)
                    dve.wait_ge(sem("dec_ready"), it + 1)
                    dve.wait_ge(sem("grams"), it + 1)
                    tt(aT[:, :, :], pb4[0], dec[:, :, :], ALU.mult).then_inc(sem("a_steps"), 1)
                    dve.wait_ge(sem("a_steps"), 2 * it + 1)
                    tt(aT[:, :, :], aT[:, :, :], pb4[3], ALU.mult).then_inc(sem("a_steps"), 1)
                    dve.wait_ge(sem("a_steps"), 2 * it + 2)
                    tt(lv[:, :, :], lev(0), aT[:, :, :], ALU.mult).then_inc(sem("inv0_part"), 1)
                    dve.wait_ge(sem("inv0_part"), it + 1)
                    tt(invT[:, :, :], ident.unsqueeze(1).to_broadcast([P, 4, P]), lv[:, :, :], ALU.subtract)\
                        .then_inc(sem("inv0_ready"), 1)
                    dve.wait_ge(sem("inv0_ready"), it + 1)
                    tt(attT[:, :, :], pb4[1], dec[:, :, :], ALU.mult).then_inc(sem("att_ready"), 1)
                    level_part(0)
                    dve.wait_ge(sem("att_ready"), 3 * it + 1)
                    tt(attT[:, :, :], attT[:, :, :], causT.unsqueeze(1).to_broadcast([P, 4, P]), ALU.mult)\
                        .then_inc(sem("att_ready"), 1)
                    dve.wait_ge(sem("q_decay"), it + 1)
                    tt(qd[:, :, :], qn[:, :, P:2 * P], qd[:, :, :], ALU.mult).then_inc(sem("att_ready"), 1)
                elif 4 <= g < 16 and g % 2 == 0:
                    l = (g - 4) // 2
                    if l < 5:
                        dve.wait_ge(sem("level_product"), 6 * it + (l + 1))
                        level_part(l + 1)
                elif 5 <= g < 16:
                    l = (g - 5) // 2
                    dve.wait_ge(sem("level_update"), 6 * it + (l + 1))
                    if l < 5:
                        tt(inv[:, :, :], inv[:, :, :], pb4[2], ALU.subtract).then_inc(sem("inv_updated"), 1)
                    tt(invT[:, :, :], invT[:, :, :], pb4[3], ALU.subtract).then_inc(sem("inv_updated"), 1)
                elif g == 18:
                    dve.wait_ge(sem("k_state"), it + 1)
                    for i in range(2):
                        V.scalar_tensor_tensor(r1[:, i], pb4[2][:, i], smc(NBEG_COL + i + 2 * it),
                                               vb[:, 2 * i + 1], ALU.mult, ALU.add).then_inc(sem("rest_ready"), 1)
                elif g == 21:
                    dve.wait_ge(sem("out_rms"), it + 1)
                    V.reciprocal(osq[:, :, :], osq[:, :, :]).then_inc(sem("out_rsqrt"), 1)
                    dve.wait_ge(sem("out_rsqrt"), it + 1)
                    yy = y[:, sl(2 * it, 2)]
                    V.scalar_tensor_tensor(yy, pb[4][:, :, :], col("ogain"), osq[:, :, :], ALU.mult, ALU.mult)\
                        .then_inc(sem("gdn_y"), 1)
                    dve.wait_ge(sem("gdn_y"), 2 * it + 1)
                    dve.wait_ge(sem("z_ready"), it + 1)
                    tt(yy, yy, zs[:, :], ALU.mult).then_inc(sem("gdn_y"), 1)

            def gdn_unit(it, fills=False):
                def react(j, i):
                    for g in (8 * j + 2 * i, 8 * j + 2 * i + 1):
                        if g < 22:
                            gdn(g, it)
                    if fills and j == 3 and i > 0:
                        fill_y("y", i - 1)

                def evac(j):
                    if j < 3:
                        scale_to("gdn", it, 4, j, (zs, cy, cz)[j][:, :])
                        return
                    cs = sem("sc_scaled")
                    dve.wait_ge(evacuated, 4 * it + (UNIT0["gdn"] + 3))
                    tt(cz[:, :], cz[:, :], both(rr), ALU.mult).then_inc(cs, 1)
                    dve.wait_ge(cs, it + 1)
                    b = done("gdn", it, 4, j)
                    tt(cw[:, :], b[:, :, :], cz[:, :], ALU.mult).then_inc(evacuated, 1)
                    dve.wait_ge(sem("sc_tap0"), 2 * it + 2)
                    taps("sc_taps", cw, cv, lambda tap, t: col("sconv", 8 * (1 - tap) + (2 * it + t)), 2, 4 * it,
                         shifted=True)
                    dve.wait_ge(sem("sc_taps"), 4 * it + 4)
                    tt(y[:, sl(2 * it + 8, 2)], cv[:, :], cy[:, :], ALU.mult).then_inc(sem("sc_y"), 1)
                return react, evac

            dve.wait_ge(sem("qkv_ready"), 12)
            with dve.Fori(0, 3) as it:
                react, evac = gdn_unit(it)
                units("gdn", it, 4, evac, react)
            react, evac = gdn_unit(3, fills=True)
            units("gdn", 3, 4, evac, react)
            fill_y("y", 3)
            dve.wait_ge(sem("x_again"), 16)
            phase("mixo", 8, lambda it, j: add_x("mixo", it, 2, j), last=lambda g: fill_x("xa", "mixo", g))

            XSC = 512 ** -0.5

            def xa(a, h):
                if a == 0:
                    dve.wait_ge(sem("xa_scores"), h + 1)
                    V.tensor_reduce(smc(NMAX, 2), pb[0][:, :, :], AX.X, ALU.max, negate=True).then_inc(sem("xa_nmax"), 1)
                    dve.wait_ge(sem("xa_nmax"), 2 * h + 1)
                    V.tensor_scalar(smc(NMAX, 2), smc(NMAX, 2), XSC, None, ALU.mult).then_inc(sem("xa_nmax"), 1)
                    dve.wait_ge(sem("xa_exp"), 2 * h + 2)
                    V.reciprocal(smc(RINV, 2), smc(RSUM, 2)).then_inc(sem("xa_rinv"), 1)
                    dve.wait_ge(sem("xa_rinv"), h + 1)
                    for t in range(2):
                        V.tensor_scalar(pr[:, t], pr[:, t], smc(RINV + t), None, ALU.mult).then_inc(sem("xa_prob"), 1)
                elif a == 2:
                    dve.wait_ge(sem("xa_pv"), h + 1)
                    for q in range(2):
                        V.tensor_copy(y[:, sl(4 * h + 2 * q, 2)], pb[2 + q][:, :, :]).then_inc(sem("xa_o"), 1)

            def q_evac(it, j):
                if isinstance(it, int) and it == 0 and j == 0:
                    rsqrt("xa")
                scale_to("xq", it, 2, j, xq[:, 2 * j:2 * j + 2])
            units("xq", 0, 2, lambda j: q_evac(0, j))

            def xq_react(it):
                def react(j, i):
                    if (j, i) == (0, 0):
                        xa(0, it - 1)
                    elif (j, i) == (1, 0):
                        xa(2, it - 1)
                    elif isinstance(it, int) and j == 1:
                        fill_y("o", i - 1)
                return react
            with dve.Fori(1, 3) as it:
                units("xq", it, 2, lambda j: q_evac(it, j), xq_react(it))
            units("xq", 3, 2, lambda j: q_evac(3, j), xq_react(3))
            xa(0, XH - 1)
            xa(2, XH - 1)
            fill_y("o", 3)
            phase("xo", 8, lambda it, j: add_x("xo", it, 2, j), last=lambda g: fill_x("ffn", "xo", g))
            tile0 = 0
            for s, nt in enumerate(SEGS):
                name = f"up{s}"
                g0 = sum(SEGS[:s]) // 2

                def evac(it, j):
                    b = scale_bank(name, it, 2, j)
                    dve.wait_ge(sem("up_tap0"), 4 * it + (4 * g0 + 2 * j + 2))
                    taps("up_taps", b, (cy, cw)[j],
                         lambda tap, t: col("fconv", 88 * (1 - tap) + 44 * j + tile0 + t + 2 * it), 2,
                         6 * it + (6 * g0 + 3 * j))
                    if j == 1:
                        dve.wait_ge(sem("gate_ready"), it + (g0 + 1))
                        dve.wait_ge(evacuated, 2 * it + (UNIT0[name] + 2))
                        tt(cv[:, :], cw[:, :], cz[:, :], ALU.mult).then_inc(sem("gated"), 1)
                        dve.wait_ge(sem("g_hi_ready"), it + (g0 + 1))
                        gt = sl(2 * it, 2)
                        tt(g_lo[:, gt], cv[:, :], g_hi[:, gt].bitcast(F32), ALU.subtract)\
                            .then_inc(sem("g_ready"), 1)
                phase(name, nt, evac, first=(lambda: rsqrt("ffn")) if s == 0 else None)
                tile0 += nt
                if nt == KT:
                    phase(f"down{s}", 8, lambda it, j: add_x(f"down{s}", it, 2, j))
                else:
                    phase(f"down{s}", 8, lambda it, j: add_x(f"down{s}", it, 4, j, K=nt), n=4, K=nt,
                          last=lambda g: fill_x("pre", f"down{s}", g, gain2="pre"))

            pd = sem("pre_dve")
            m2 = smc(R2_COL, 2)

            def pre_norm():
                dve.wait_ge(sem("pre_rms"), 1)
                V.reciprocal(smc(RF_COL, 2), smc(RF_COL, 2))
                V.reciprocal(rf[:, :], rf[:, :]).then_inc(sem("pre_steps"), 1)
                dve.wait_ge(sem("pre_steps"), 1)
                tt(rr[:, :], pb[5][:, 1, :], rf[:, :], ALU.mult)
                tt(m2, pb[4][:, 0, 2:4], smc(RF_COL, 2), ALU.mult).then_inc(sem("pre_steps"), 1)
                dve.wait_ge(sem("pre_steps"), 2)
                tt(m2, m2, smc(RF_COL, 2), ALU.mult)
                tt(rr[:, :], rr[:, :], rf[:, :], ALU.mult).then_inc(pd, 1)
                dve.wait_ge(sem("rms_ready"), NORM["pre"])
                V.reciprocal(smc(R_COL, 2), smc(R_COL, 2))
                V.reciprocal(rr[:, :], rr[:, :]).then_inc(sem("rsqrt_ready"), 1)
                dve.wait_ge(sem("rsqrt_ready"), NORM["pre"])
                tt(smc(R_COL, 2), smc(R_COL, 2), smc(RF_COL, 2), ALU.mult)
                tt(rr[:, :], rr[:, :], rf[:, :], ALU.mult).then_inc(sem("pre_steps"), 1)
                dve.wait_ge(sem("pre_steps"), 3)

            rd = sem("rope_dve")

            def rope_angles():
                dve.wait_ge(sem("pos_in"), 16)
                V.tensor_copy(sinr[:, :], pos[:, :]).then_inc(rd, 1)
                dve.wait_ge(rd, 1)
                V.tensor_scalar(sinr[:, :], sinr[:, :], c1("invf"), None, ALU.mult).then_inc(rd, 1)
                dve.wait_ge(rd, 2)
                V.tensor_scalar(cosr[:, :], sinr[:, :], 1.0 / (2 * np.pi), MAGIC, ALU.mult, ALU.add).then_inc(rd, 1)
                dve.wait_ge(rd, 3)
                V.tensor_scalar(cosr[:, :], cosr[:, :], MAGIC, None, ALU.subtract).then_inc(rd, 1)
                for q in range(3):
                    dve.wait_ge(rd, 4 + q)
                    V.scalar_tensor_tensor(sinr[:, :], cosr[:, :], -TWO_PI[q], sinr[:, :], ALU.mult, ALU.add)\
                        .then_inc(rd, 1)
                dve.wait_ge(rd, 7)
                V.tensor_scalar(sinr[:, :], sinr[:, :], 3.1415925, -3.1415925, ALU.min, ALU.max).then_inc(rd, 1)

            def lat_react(it):
                def react(j, i):
                    if (it, j, i) == (0, 1, 2):
                        rope_angles()
                    elif it == 1:
                        if j == 0:
                            for k in range(4 * i, 4 * i + 4):
                                V.scalar_tensor_tensor(x[:, k], x[:, k], col("fin", k), rf[:, :], ALU.mult,
                                                       ALU.mult).then_inc(sem("x_final"), 1)
                        elif i == 0:
                            dve.wait_ge(sem("rope_act"), 3)
                            V.tensor_scalar(sinr[:, :], sinr[:, :], c1("sgn"), None, ALU.mult).then_inc(rd, 1)
                    elif (it, j) == (2, 0) and i in (1, 2):
                        dve.wait_ge(evacuated, UNIT0["lat"] + 3)
                        fill_scaled("gq", 4 * i - 4, min(4 * i, 6), lat, "gq", lh_hi, lh_lo)
                    elif (it, j, i) == (2, 1, 1):
                        dve.wait_ge(evacuated, UNIT0["lat"] + 5)
                        fill_scaled("gkv", 0, 4, lat[:, 6:10], "gkv", lh_hi, lh_lo, 6)
                return react

            def lat_evac(it, j):
                if (it, j) == (0, 0):
                    pre_norm()
                scale_to("lat", it, 2, j, lat[:, 4 * it + 2 * j:4 * it + 2 * j + 2])
            for it in range(3):
                units("lat", it, 2, lambda j: lat_evac(it, j), lat_react(it))
            def rope_key():
                dve.wait_ge(rd, 9)
                dve.wait_ge(evacuated, UNIT0["lat"] + 6)
                kd_ = sem("kr_dve")
                tt(kr[:, :], lat[:, 10], cosr[:, :], ALU.mult).then_inc(kd_, 1)
                dve.wait_ge(sem("kr_swap"), 2)
                tt(tn[:, 0], qm[:, :], sinr[:, :], ALU.mult).then_inc(kd_, 1)
                dve.wait_ge(kd_, 2)
                tt(kr[:, :], kr[:, :], tn[:, 0], ALU.add).then_inc(kd_, 1)

            fd = sem("forget_dve")

            def forget_first():
                dve.wait_ge(sem("forget_act"), 2)
                V.tensor_scalar(r[0:8, 2], r[0:8, 2], 1.0, None, ALU.add).then_inc(fd, 1)
                V.tensor_scalar(r[0:8, 3], lat[0:8, 11], col("bfor", 0, slice(0, 8)), 0.0, ALU.add, ALU.min)\
                    .then_inc(fd, 1)

            def forget_rest():
                dve.wait_ge(sem("forget_act"), 3)
                dve.wait_ge(fd, 2)
                tt(r[0:8, 3], r[0:8, 3], r[0:8, 2], ALU.subtract).then_inc(fd, 1)
                dve.wait_ge(fd, 3)
                V.tensor_tensor_scan(r[0:8, 0, 0:P], ones[0:8, :], r[0:8, 3, 0:P], 0.0, ALU.mult, ALU.add).then_inc(fd, 1)
                dve.wait_ge(fd, 4)
                V.tensor_copy(sm[0:8, EA_COL:EA_COL + 1], r[0:8, 0, P - 1:P]).then_inc(fd, 1)
                dve.wait_ge(fd, 5)
                V.tensor_tensor_scan(r[0:8, 0, P:S], ones[0:8, :], r[0:8, 3, P:S], sm[0:8, EA_COL:EA_COL + 1],
                                     ALU.mult, ALU.add).then_inc(fd, 1)

            def ca(a, kind, it):
                cd = sem("ca_logits")
                fox = kind == "fox"

                def n(k):
                    return 2 * k * it + (0 if fox else k)
                if a == 0:
                    if fox:
                        d0 = 10 * it - 8
                        for i in range(2):
                            V.tensor_scalar(r[0:8, 2 + i], r[0:8, 0],
                                            cst[0:8, sl(CST["ident"] + i - 2 + 2 * it, 1)],
                                            None, ALU.mult).then_inc(sem("forget_rows"), 1)
                        dve.wait_ge(sem("ca_scores"), n(1))
                        for i in range(2):
                            for t in range(2):
                                V.tensor_scalar(db[:, 2 * i + t], pb[2][:, i],
                                                smc(C_COL + 8 * t + i - 2 + 2 * it), -1.0,
                                                ALU.subtract, ALU.mult).then_inc(cd, 1)
                        dve.wait_ge(cd, 10 * it - 4)
                        for i in range(2):
                            tt(db[:, 2 * i:2 * i + 2], db[:, 2 * i:2 * i + 2], cmask, ALU.add).then_inc(cd, 1)
                        for i in range(2):
                            dve.wait_ge(cd, 10 * it + (i - 3))
                            V.scalar_tensor_tensor(db[:, 2 * i:2 * i + 2], pb[i][:, :, :], P ** -0.5,
                                                   db[:, 2 * i:2 * i + 2], ALU.mult, ALU.add).then_inc(cd, 1)
                        dve.wait_ge(cd, 10 * it)
                    else:
                        for i in range(2):
                            V.tensor_scalar(qmask[:, i], qrope[:, sl(it, 1)].rearrange("p a b -> p (a b)"),
                                            c1(f"head{i}"), None, ALU.mult).then_inc(sem("mla_q_masked"), 1)
                        dve.wait_ge(sem("ca_scores"), n(1))
                        for i in range(2):
                            V.scalar_tensor_tensor(db[:, 2 * i:2 * i + 2], pb[i][:, :, :], 192 ** -0.5,
                                                   cmask, ALU.mult, ALU.add).then_inc(cd, 1)
                        dve.wait_ge(cd, 10 * it + 2)
                    V.tensor_reduce(smc(NMAX, 4), db[:, :, :], AX.X, ALU.max, negate=True).then_inc(sem("ca_nmax"), 1)
                    dve.wait_ge(sem("ca_exp"), n(4))
                    V.reciprocal(smc(RINV, 4), smc(RSUM, 4)).then_inc(sem("ca_rinv"), 1)
                    dve.wait_ge(sem("ca_rinv"), n(1))
                    for q in range(4):
                        V.tensor_scalar(pr2[:, q], pr2[:, q], smc(RINV + q), None, ALU.mult)\
                            .then_inc(sem("ca_prob"), 1)
                elif a == 1:
                    dve.wait_ge(sem("ca_turned"), n(1))
                    V.tensor_copy(pT2[:, 2:4], pb[4][:, :, :]).then_inc(sem("ca_prob_copied"), 1)
                else:
                    dve.wait_ge(sem("ca_pv"), n(1))
                    if fox:
                        dve.wait_ge(sem("fg_ready"), it)
                        tt(y[:, sl(2 * it - 2, 2)], pb[5][:, :, :], fg[:, :], ALU.mult).then_inc(sem("ca_o"), 1)
                    else:
                        V.tensor_copy(y[:, sl(2 * it + 8, 2)], pb[5][:, :, :]).then_inc(sem("ca_o"), 1)

            rsqrt("gq", out=rq)

            def uq_evac(u):
                if u % 2:
                    dve.wait_ge(w_used, CHUNK0["uq"] + 6 * (u + 1) // BLK)
                else:
                    dve.wait_ge(sem("mid_chunk"), u // 2 + 1)
                to = qnope[:, 2 * u:2 * u + 2] if u < 4 else lat[:, 2 * u - 8:2 * u - 6]
                tt(to, bank[(UNIT0["uq"] + u) % 2][:, :, :], both(rq), ALU.mult).then_inc(evacuated, 1)
            u = 0
            for c in range(9):
                if c == 1:
                    rope_key()
                    forget_first()
                elif c == 2:
                    forget_rest()
                while u < 6 and (6 * (u + 1) - 1) // BLK == c:
                    uq_evac(u)
                    u += 1
                split(CHUNK0["uq"] + c + SLOTS)
            rsqrt("gkv", out=rkv, column=RKV_COL)
            qd_ = sem("qrope_ready")
            for u in range(8):
                if u in (2, 4):
                    for p in range(u - 2, u):
                        tt(qrope[:, p], lat[:, p], cosr[:, :], ALU.mult).then_inc(qd_, 1)
                        dve.wait_ge(sem("qr_swap"), 2 * p + 2)
                        tt(tn[:, p], tn[:, p], sinr[:, :], ALU.mult).then_inc(qd_, 1)
                        dve.wait_ge(qd_, 3 * p + 2)
                        tt(qrope[:, p], qrope[:, p], tn[:, p], ALU.add).then_inc(qd_, 1)
                dve.wait_ge(w_used, CHUNK0["ukv"] + u + 1)
                b = bank[(UNIT0["ukv"] + u) % 2]
                if u < 4:
                    tt(knope[:, 2 * u:2 * u + 2], b[:, :, :], both(rkv), ALU.mult).then_inc(evacuated, 1)
                else:
                    scale_tokens(b, vm[:, :, 256 * (u - 4):256 * (u - 3)], RKV_COL)
                split(CHUNK0["ukv"] + u + SLOTS)
            dve.wait_ge(sem("forget_cols"), 1)
            V.tensor_copy(smc(C_COL, 16), pb[2][:, 0, 0:16]).then_inc(fd, 1)
            dve.wait_ge(fd, 7)
            dve.wait_ge(qd_, 12)

            def fox_react(it, fox=True, mla=True):
                def react(j, i):
                    q = 4 * j + i
                    if q in CA_FOX and fox:
                        ca(CA_FOX[q], "fox", it)
                    elif q in CA_MLA and mla:
                        ca(CA_MLA[q], "mla", it)
                    elif not mla and j == 3 and i > 0:
                        fill_y("o2", i - 1)
                return react

            def fox_evac(it):
                def evac(j):
                    if j == 3:
                        scale_tokens(done("fox", it, 4, j), fv[:, :, :])
                    else:
                        scale_to("fox", it, 4, j, (fq, fk, fg)[j][:, :])
                return evac
            units("fox", 0, 4, fox_evac(0), fox_react(0, fox=False))
            with dve.Fori(1, 4) as it:
                units("fox", it, 4, fox_evac(it), fox_react(it))

            def gm_evac(j):
                if j >= 2:
                    dve.wait_ge(sem("o_gated"), j - 1)
                scale_to("gm", 0, 4, j, gg[:, j % 2])
                dve.wait_ge(sem("gate2_ready"), j + 1)
                yy = y[:, 8 + 2 * j:10 + 2 * j]
                tt(yy, yy, gg[:, j % 2], ALU.mult).then_inc(sem("o_gated"), 1)
            units("gm", 0, 4, gm_evac, fox_react(4, mla=False))
            fill_y("o2", 3)
            phase("out", 8, lambda it, j: copy_to("out", it, 2, j, y[:, sl(4 * it + 2 * j, 2)]), last=lambda g: None)
            rsqrt("post")
            od = sem("out_dve_steps")
            for j in range(7):
                if j < 6:
                    dve.wait_ge(sem("post_scaled"), j + 1)
                    yp = y[:, 2 * j:2 * j + 2]
                    tt(yp, yp, both(rr), ALU.mult).then_inc(od, 1)
                if j:
                    dve.wait_ge(od, j)
                    xp = x[:, 2 * j - 2:2 * j]
                    tt(xp, xp, y[:, 2 * j - 2:2 * j], ALU.add).then_inc(sem("out_dve"), 1)


def constants():
    c = np.zeros((P, N_CST), np.float32)
    i = np.arange(P)
    c[:, CST["ident"]:CST["ident"] + P] = np.eye(P)
    c[:, CST["ones"]:CST["ones"] + P] = 1
    c[:, CST["causT"]:CST["causT"] + P] = i[:, None] <= i[None, :]
    for l in range(NLEV):
        m = (i[:, None] >> l) + 1 == (i[None, :] >> l)
        m &= (i[None, :] >> l) % 2 == 1
        c[:, CST["levT"] + l * P:CST["levT"] + (l + 1) * P] = m
    for t in range(2):
        q, k = i[:, None] + t * P, np.arange(S)[None, :]
        c[:, CST["cmask"] + t * S:CST["cmask"] + (t + 1) * S] = np.where(k <= q, 0, NEG)
    c[:, CST["eps"]] = EPS
    c[:, CST["invf"]] = 10000.0 ** (-(i % 32) * 2.0 / 64)
    c[:, CST["sgn"]] = np.where(i < 64, -1, 1)
    c[:, CST["hpi"]] = np.pi / 2
    for h in range(2):
        c[:, CST[f"head{h}"]] = (i // 32) % 2 == h
    return c


def tiles(v):
    return np.asarray(v).reshape(-1, P).T


def feature_major(a):
    return np.ascontiguousarray(a.T.reshape(-1, P, a.shape[0]).transpose(1, 0, 2))


def stream_of(w):
    blocks = []

    def units(a, width=BW):
        k, n = a.shape
        blocks.append(a.reshape(k // P, P, n // width, width).transpose(2, 0, 1, 3).reshape(-1, P, width))

    def narrow(a):
        blocks.append(a.reshape(-1, 2, P, P).transpose(0, 2, 1, 3).reshape(-1, P, BW))

    def placed(n, parts):
        out = np.zeros((D, n), np.float32)
        for at_, a in parts:
            out[:, at_:at_ + a.shape[1]] = a
        return out

    mi, wi = w["w_mix_in"][0], w["w_in_2"][0]
    gw = 1024
    units(w["w_xk"][0])
    units(w["w_xv"][0])
    narrow(placed(P, [(0, mi[:, 4 * gw + 8:4 * gw + 16]), (32, mi[:, 4 * gw:4 * gw + 8])]))
    units(mi[:, :3 * gw])
    off = 4 * gw + 16
    for p in range(4):
        for base in (3 * gw, off, off + gw, off + 2 * gw):
            units(mi[:, base + p * BW:base + (p + 1) * BW])
    units(w["w_mix_out"][0])
    units(w["w_xq"][0])
    units(w["w_xo"][0])
    up, down = w["w_ffn_up"][0], w["w_ffn_down"][0]
    t0 = 0
    for nt in SEGS:
        for c in range(t0 * P, (t0 + nt) * P, BW):
            units(up[:, c:c + BW])
            units(up[:, FT * P + c:FT * P + c + BW])
        units(down[t0 * P:(t0 + nt) * P])
        t0 += nt
    units(wi[:, :1280])
    krope = wi[:, 1280:1344]
    f0 = 1344 + 4 * gw
    units(placed(BW, [(0, krope[:, :32]), (32, krope[:, :32]), (64, krope[:, 32:]), (96, krope[:, 32:]),
                      (P, wi[:, f0:f0 + 8])]))
    uq = w["w_uq_2"][0].reshape(768, 8, 192)
    units(np.ascontiguousarray(uq[:, :, :P]).reshape(768, -1))
    rope = uq[:, :, P:].reshape(768, 4, 2, 2, 32).transpose(0, 1, 3, 2, 4)
    units(np.ascontiguousarray(rope).reshape(768, -1))
    ukv = w["w_ukv_2"][0].reshape(512, 8, 256)
    units(np.ascontiguousarray(ukv[:, :, :P]).reshape(512, -1))
    units(np.ascontiguousarray(ukv[:, :, P:]).reshape(512, -1))
    for p in range(4):
        for base in (1344 + gw, 1344 + 2 * gw, f0 + 8, 1344 + 3 * gw):
            units(wi[:, base + p * BW:base + (p + 1) * BW])
    units(wi[:, 1344:1344 + gw])
    wo = w["w_out_2"][0]
    units(np.concatenate([wo[gw:], wo[:gw]]))
    b = np.concatenate(blocks)
    assert b.shape[0] == N_CHUNKS * BLK, (b.shape, N_CHUNKS)
    return np.ascontiguousarray(b.reshape(N_CHUNKS, BLK, P, BW).transpose(0, 2, 1, 3)).reshape(N_CHUNKS, P, BLK * BW)


def small_vectors(w):
    c = np.zeros((P, N_COLS), np.float32)

    def put(name, a):
        c[:a.shape[0], COLS[name]:COLS[name] + a.shape[1]] = a
    for name, key in (("mix", "mix_norm"), ("xa", "xattn_norm"), ("mem", "mem_norm"), ("ffn", "ffn_norm"),
                      ("pre", "g_pre_2"), ("post", "g_post_2"), ("gq", "g_q_latent_2"), ("gkv", "g_kv_latent_2"),
                      ("ogain", "gdn_out_norm"), ("gconv", "gdn_conv"), ("sconv", "sc_conv"), ("fconv", "ffn_conv")):
        put(name, tiles(np.asarray(w[key])[0].reshape(-1)))
    put("fin", tiles(w["final_norm"]))
    put("alog", np.asarray(w["gdn_a_log"])[0][:, None])
    put("dtb", np.asarray(w["gdn_dt_bias"])[0][:, None])
    put("bfor", np.asarray(w["b_forget_2"])[0][:, None])
    return c


def kernel(**inputs):
    from concourse import bacc
    from concourse.bass_utils import run_bass_kernel_spmd

    w = {k: np.asarray(v) for k, v in inputs.items()}
    arrays = {
        "weights": stream_of(w), "x_in": feature_major(w["x"][0]), "mem_in": feature_major(w["mem"][0]),
        "small_vectors": small_vectors(w), "constants": constants(),
        "positions": np.ascontiguousarray(w["positions_2"].reshape(1, S)),
    }
    nc = bacc.Bacc("TRN2", target_bir_lowering=False, num_devices=1)
    args = [nc.dram_tensor(n, a.shape, mybir.dt.from_np(a.dtype), kind="ExternalInput").ap()
            for n, a in arrays.items()]
    out = nc.dram_tensor("y_out", (P, KT, S), F32, kind="ExternalOutput").ap()
    build_program(nc, *args, out)
    r = run_bass_kernel_spmd(nc, [arrays], core_ids=[0])
    got = r.results[0]["y_out"]
    return np.ascontiguousarray(got.transpose(2, 1, 0)).reshape(1, S, D)
```

```python
import concourse.bass as bass
from concourse import mybir
from contextlib import ExitStack
import numpy as np

F32 = mybir.dt.float32
F32R = mybir.dt.float32r
I32 = mybir.dt.int32
ALU = mybir.AluOpType
ACT = mybir.ActivationFunctionType
AX = mybir.AxisListType

P = 128
S = 256
D = 2048
KT = D // P
CHUNK = 128
NLEV = 7
GH = 8
XH = 4
FT = 5632 // P
SEGS = [16, 16, 12]
SLOTS = 4
BLK = 4
BW = 256
EPS = 1e-6
NEG = -1e30
MAGIC = 1.5 * 2.0 ** 23
TWO_PI = (6.28125, 0.0019350051879882812, 3.019916050561733e-07)


STREAM = ([("xk", 8, KT), ("xv", 8, KT), ("ba", 1, 8), ("qkv", 12, KT), ("gdn", 16, KT),
           ("mixo", 8, KT), ("xq", 8, KT), ("xo", 8, KT)]
          + [x for i, n in enumerate(SEGS) for x in ((f"up{i}", n, KT), (f"down{i}", 8, n))]
          + [("lat", 6, KT), ("uq", 6, 6), ("ukv", 8, 4), ("fox", 16, KT), ("gm", 4, KT),
             ("out", 8, KT)])
UNIT0, CHUNK0 = {}, {}
_u = _b = 0
for _name, _n, _k in STREAM:
    UNIT0[_name], CHUNK0[_name] = _u, _b // BLK
    _u += _n
    _b += _n * _k
N_CHUNKS = _b // BLK
assert _b % BLK == 0

COLS, _at = {}, 0
for _name, _n in (("mix", KT), ("xa", KT), ("mem", KT), ("ffn", KT), ("fin", KT), ("pre", KT),
                  ("post", KT), ("gq", 6), ("gkv", 4), ("ogain", 1), ("gconv", 24 * 4),
                  ("sconv", 8 * 3), ("fconv", 88 * 3), ("alog", 1), ("dtb", 1), ("bfor", 1)):
    COLS[_name] = _at
    _at += _n
N_COLS = _at
CST, _at = {}, 0
for _name, _n in (("ident", P), ("ones", P), ("causT", P), ("levT", NLEV * P), ("cmask", 2 * S),
                  ("head0", 1), ("head1", 1), ("eps", 1), ("invf", 1), ("sgn", 1), ("hpi", 1),
                  ("epsq0", 1)):
    CST[_name] = _at
    _at += _n
N_CST = _at

HFILL, _h = {}, 0
for _name, _n in (("mem", KT), ("mix", KT), ("y", KT), ("xa", KT), ("o", KT), ("ffn", KT),
                  ("pre", KT), ("gq", 6), ("gkv", 4), ("o2", KT)):
    HFILL[_name] = _h
    _h += _n
NORM, SQ0, _s = {}, {}, 0
for _i, (_name, _n) in enumerate((("mem", 8), ("mix", 8), ("xa", 8), ("ffn", 8), ("pre", 8),
                                  ("gq", 3), ("gkv", 2), ("post", 8))):
    NORM[_name], SQ0[_name] = _i + 1, _s
    _s += 2 * _n - 1 if _name != "pre" else 0
GDN_SLOT = {0: 1, 1: 2, 7: 3, 9: 4, 11: 5, 12: 6, 13: 7, 14: 8, 15: 9, 16: 10, 17: 11, 18: 12, 19: 13,
            20: 14, 21: 15, 22: 16, 23: 17, 25: 18, 26: 19, 28: 20, 31: 21}
GDN_REACT = {**{s: g for s, g in GDN_SLOT.items() if g not in (2, 21)}, 2: 2}
G_COL, B_COL, EG_COL, NBEG_COL, KD_ARG, KD_COL, EA_COL = 0, 16, 32, 40, 48, 50, 52
NMAX, RSUM, RINV, C_COL, R_COL, RF_COL, R2_COL, RKV_COL = 60, 64, 68, 72, 88, 90, 92, 94
GG_COL = 112
RK_COL = 96


def sl(start, n):
    return slice(start, start + n) if isinstance(start, int) else bass.ds(start, n)


def build_program(nc, wst, xT, memT, cols_d, cst_d, pos_d, out_d):
    ctx = ExitStack()
    with ctx:
        def at(name, kb, shape, dt=F32):
            return nc.alloc_sbuf_tensor_at(name, [P] + list(shape), dt, offset=16512 + int(kb * 1024))

        raw = at("raw", 0, [SLOTS, BLK * BW])
        w_hi = at("w_hi", 16, [SLOTS, BLK * BW], F32R)
        w_lo = at("w_lo", 32, [SLOTS, BLK * BW], F32R)
        h_hi = at("h_hi", 48, [KT, S], F32R)
        h_lo = at("h_lo", 64, [KT, S], F32R)
        x = at("x", 80, [KT, S])
        kx = at("kx", 96, [KT, S])
        vx = at("vx", 112, [2, D])
        qkv = at("qkv", 128, [24, S])
        y = at("y", 160, [KT, S])
        cst = at("cst", 176, [N_CST])
        cols = at("cols", 183.75, [N_COLS])
        tn = at("tn", 186, [4, S])
        acc = at("acc", 190, [2, S])
        sq = at("sq", 192, [2, S])
        rr = at("rr", 194, [S])
        cy = at("cy", 195, [2, S])
        cz = at("cz", 197, [2, S])
        cw = at("cw", 199, [2, S])
        cv = at("cv", 201, [2, S])
        rows = at("rows", 203, [4, S])
        sm = at("sm", 207, [160])
        qn, kn = at("qn", 80, [2, S]), at("kn", 82, [2, S])
        dec, aT, attT = at("dec", 84, [4, P]), at("aT", 86, [4, P]), at("attT", 88, [4, P])
        q2 = at("q2", 84, [2, S])
        inv, invT, lv = at("inv", 90, [4, P]), at("invT", 92, [4, P]), at("lv", 94, [4, P])
        vs, zs, vb = at("vs", 152, [2, S]), at("zs", 154, [2, S]), at("vb", 156, [4, P])
        kd, qd = at("kd", 158, [2, P]), at("qd", 159, [2, P])
        vn, s1, r1 = at("vn", 186, [4, P]), at("s1", 188, [2, P]), at("r1", 189, [2, P])
        lp, osq = at("lp", 190, [4, P]), at("osq", 192, [2, S])
        xq = at("xq", 128, [4, S])
        vh = at("vh", 132, [2, 512])
        pr = at("pr", 136, [4, S])
        pT = at("pT", 140, [4, S])
        g_hi = at("g_hi", 96, [KT, S], F32R)
        g_lo = at("g_lo", 112, [KT, S], F32R)
        lat = at("lat", 96, [12, S])
        lh_hi = at("lh_hi", 108, [10, S], F32R)
        lh_lo = at("lh_lo", 118, [10, S], F32R)
        qnope, qrope = at("qnope", 128, [8, S]), at("qrope", 136, [4, S])
        knope, vm = at("knope", 140, [8, S]), at("vm", 148, [2, 1024])
        kr = at("kr", 156, [S])
        qpair, vpair = at("qpair", 157, [2, S]), at("vpair", 100, [2, S])
        gg = at("gg", 104, [2, 2, S])
        fq, fk = at("fq", 108, [2, S]), at("fk", 110, [2, S])
        fg, fv = at("fg", 112, [2, S]), at("fv", 114, [2, S])
        pr2, pT2, db = at("pr2", 116, [4, S]), at("pT2", 120, [4, S]), at("db", 124, [4, S])
        acc2 = at("acc2", 195, [2, S])
        qmask = at("qmask", 195, [2, S])
        cosr, sinr = at("cosr", 197, [S]), at("sinr", 198, [S])
        qm = at("qm", 199, [S])
        pos = at("pos", 200, [S], I32)
        rq, rkv, rf = at("rq", 201, [S]), at("rkv", 202, [S]), at("rf", 202, [S])

        ident = cst[:, CST["ident"]:CST["ident"] + P]
        ones = cst[:, CST["ones"]:CST["ones"] + P]
        causT = cst[:, CST["causT"]:CST["causT"] + P]
        levT = cst[:, CST["levT"]:CST["levT"] + NLEV * P].rearrange("p (l m) -> p l m", l=NLEV)
        cmask = cst[:, CST["cmask"]:CST["cmask"] + 2 * S].rearrange("p (t m) -> p t m", t=2)

        def c1(name, parts=slice(0, P)):
            return cst[parts, CST[name]:CST[name] + 1]

        def col(name, i=0, parts=slice(0, P)):
            return cols[parts, sl(COLS[name] + i, 1)]

        bank = [ctx.enter_context(nc.psum_tensor(f"unit{i}", [P, 2, S], F32)) for i in range(2)]
        pb = [ctx.enter_context(nc.psum_tensor(f"pb{i}", [P, 2, S], F32)) for i in range(6)]
        pb4 = [b[:, :, :].rearrange("p a (b c) -> p (a b) c", b=2) for b in pb]

        sems = {}

        def sem(name):
            if name not in sems:
                sems[name] = ctx.enter_context(nc.semaphore(name))
            return sems[name]

        raw_ready = [sem(f"raw_ready{i}") for i in range(SLOTS)]
        hi_ready, lo_ready, w_used = sem("hi_ready"), sem("lo_ready"), sem("w_used")
        evacuated = sem("evacuated")
        h_ready = sem("h_ready")

        def smc(c, n=1):
            return sm[:, sl(c, n)]

        def loop(eng, n, body, first=False):
            if first:
                body(0)
            with eng.Fori(1 if first else 0, n) as it:
                body(it)

        block = ctx.enter_context(nc.Block())

        @block.sync
        def _(sp):
            sp.dma_start(cols[:, :], cols_d).then_inc(sem("cols_in"), 16)
            for s in range(SLOTS):
                sp.dma_start(x[:, 4 * s:4 * s + 4, :], memT[:, 4 * s:4 * s + 4, :]).then_inc(sem(f"mem_in{s}"), 16)
                sp.dma_start(raw[:, s], wst[s]).then_inc(raw_ready[s], 16)
            sp.dma_start(cst[:, :], cst_d).then_inc(sem("cst_in"), 16)
            with sp.Fori(1, N_CHUNKS // SLOTS) as it:
                for s in range(SLOTS):
                    sp.wait_ge(lo_ready, SLOTS * it + (s - SLOTS + 1))
                    sp.dma_start(raw[:, s], wst[SLOTS * it + s]).then_inc(raw_ready[s], 16)
            for c in range(N_CHUNKS // SLOTS * SLOTS, N_CHUNKS):
                sp.wait_ge(lo_ready, c - SLOTS + 1)
                sp.dma_start(raw[:, c % SLOTS], wst[c]).then_inc(raw_ready[c % SLOTS], 16)
            for g in range(4):
                if g < 2:
                    sp.wait_ge(sem("out_dve"), 2 * g + 2)
                elif g == 2:
                    sp.wait_ge(sem("out_dve"), 5)
                    sp.wait_ge(sem("out_pool"), 2)
                else:
                    sp.wait_ge(sem("out_pool"), 6)
                t = slice(4 * g, 4 * g + 4)
                sp.dma_start(out_d[:, t, :], x[:, t, :]).then_inc(sem("stored"), 16)
            sp.wait_ge(sem("stored"), 64)

        @block.gpsimd
        def _(pool):

            def sum_squares(name, src, ready, nt=8):
                done, s0 = sem("squares"), SQ0[name]
                ready(0)
                nc.gpsimd.tensor_tensor(acc[:, :, :], src(0), src(0), ALU.mult).then_inc(done, 1)
                with pool.Fori(1, nt) as j:
                    ready(j)
                    nc.gpsimd.tensor_tensor(sq[:, :, :], src(j), src(j), ALU.mult).then_inc(done, 1)
                    pool.wait_ge(done, 2 * j + s0)
                    nc.gpsimd.tensor_tensor(acc[:, :, :], acc[:, :, :], sq[:, :, :], ALU.add)\
                        .then_inc(done, 1)
                    pool.wait_ge(done, 2 * j + (s0 + 1))

            def pair(t, first=0):
                return lambda j: t[:, sl(2 * j + first, 2), :]

            done = sem("squares")
            for j in range(8):
                pool.wait_ge(sem(f"mem_in{j // 2}"), 16)
                to = sq if j else acc
                nc.gpsimd.tensor_tensor(to[:, :, :], pair(x)(j), pair(x)(j), ALU.mult).then_inc(done, 1)
                if j:
                    pool.wait_ge(done, 2 * j)
                    nc.gpsimd.tensor_tensor(acc[:, :, :], acc[:, :, :], sq[:, :, :], ALU.add)\
                        .then_inc(done, 1)
                    pool.wait_ge(done, 2 * j + 1)
            pool.wait_ge(h_ready, HFILL["mem"] + KT)
            pool.dma_start(x[:, :, :], xT).then_inc(sem("x_in"), 16)
            pool.wait_ge(sem("rms_ready"), NORM["mem"])
            sum_squares("mix", pair(x), lambda j: pool.wait_ge(sem("x_in"), 16))

            def k_squares(u):
                pool.wait_ge(sem("qkv_ready"), u + 5)
                if not isinstance(u, int):
                    pool.wait_ge(sem("k_summed"), u)
                ks = sem("k_squares")
                nc.gpsimd.tensor_copy(sq[:, :, :], qkv[:, sl(2 * u + 8, 2), :]).then_inc(ks, 1)
                pool.wait_ge(ks, 2 * u + 1)
                nc.gpsimd.tensor_tensor(sq[:, :, :], sq[:, :, :], sq[:, :, :], ALU.mult).then_inc(ks, 1)
            loop(pool, 4, k_squares, first=True)

            def copy_pair(it):
                cp = sem("pair_ready")
                if not isinstance(it, int):
                    pool.wait_ge(cp, 4 * it)
                    pool.wait_ge(sem("k_state"), it)
                for out, head in ((kn, 8), (qn, 0), (vs, 16)):
                    if isinstance(it, int) and head == 16:
                        pool.wait_ge(sem("qkv_ready"), 12)
                    nc.gpsimd.tensor_copy(out[:, :, :], qkv[:, sl(2 * it + head, 2), :]).then_inc(cp, 1)
                pool.wait_ge(sem("att_ready"), 3 * it + 3)
                nc.gpsimd.tensor_tensor(q2[:, :, :], qn[:, :, :], qn[:, :, :], ALU.mult).then_inc(cp, 1)
            loop(pool, 4, copy_pair, first=True)

            pool.wait_ge(sem("gdn_y"), 8)
            pool.dma_start(x[:, :, :], xT).then_inc(sem("x_again"), 16)
            sum_squares("xa", pair(x), lambda j: pool.wait_ge(evacuated, j + (UNIT0["mixo"] + 1)))

            def copy_vh(h):
                if not isinstance(h, int):
                    pool.wait_ge(sem("xa_pv"), h)
                nc.gpsimd.tensor_copy(vh[:, :, :], vx[:, :, sl(512 * h, 512)]).then_inc(sem("vh_ready"), 1)
            loop(pool, XH, copy_vh, first=True)
            sum_squares("ffn", pair(x), lambda j: pool.wait_ge(evacuated, j + (UNIT0["xo"] + 1)))
            pool.wait_ge(sem("g_ready"), FT // 2)
            pool.dma_start(pos[:, :], pos_d.partition_broadcast(P)).then_inc(sem("pos_in"), 16)

            ps = sem("pre_squares")

            def gains(name, j):
                return cols[:, sl(COLS[name] + 2 * j, 2)].unsqueeze(2).to_broadcast([P, 2, S])

            def pre_squares(j):
                first = isinstance(j, int)
                pool.wait_ge(evacuated, j + (UNIT0["down2"] + 1))
                def step(out, a, b, op):
                    nc.gpsimd.tensor_tensor(out, a, b, op).then_inc(ps, 1)
                xp = pair(x)(j)
                if first:
                    step(acc[:, :, :], xp, xp, ALU.mult)
                else:
                    step(sq[:, :, :], xp, xp, ALU.mult)
                    pool.wait_ge(ps, 5 * j - 1)
                    step(acc[:, :, :], acc[:, :, :], sq[:, :, :], ALU.add)
                    pool.wait_ge(ps, 5 * j)
                k = 1 if first else 5 * j
                to = acc2 if first else sq
                step(to[:, :, :], xp, gains("fin", j), ALU.mult)
                pool.wait_ge(ps, k + 1)
                step(to[:, :, :], to[:, :, :], to[:, :, :], ALU.mult)
                pool.wait_ge(ps, k + 2)
                if not first:
                    step(acc2[:, :, :], acc2[:, :, :], sq[:, :, :], ALU.add)
                    pool.wait_ge(ps, 5 * j + 3)
            pre_squares(0)
            with pool.Fori(1, 8) as j:
                pre_squares(j)
            pool.wait_ge(sem("pre_dve"), 1)
            sum_squares("gq", pair(lat), lambda j: pool.wait_ge(evacuated, j + (UNIT0["lat"] + 1)), nt=3)
            pool.wait_ge(sem("rms_ready"), NORM["gq"])
            sum_squares("gkv", pair(lat, 6), lambda j: pool.wait_ge(evacuated, j + (UNIT0["lat"] + 4)), nt=2)

            def mla_pair(it):
                pool.wait_ge(evacuated, UNIT0["ukv"] + 8)
                if not isinstance(it, int):
                    pool.wait_ge(sem("ca_pv"), 2 * it - 1)
                nc.gpsimd.tensor_copy(qpair[:, :, :], qnope[:, sl(2 * it, 2)]).then_inc(sem("qpair_ready"), 1)
                nc.gpsimd.tensor_copy(vpair[:, :, :], vm[:, :, sl(256 * it, 256)]).then_inc(sem("vpair_ready"), 1)
            loop(pool, 4, mla_pair, first=True)

            ro, done = sem("post_scaled"), sem("squares")

            def post(j):
                first = isinstance(j, int)
                s0 = SQ0["post"]
                pool.wait_ge(evacuated, j + (UNIT0["out"] + 1))
                yp = pair(y)(j)
                nc.gpsimd.tensor_tensor((acc if first else sq)[:, :, :], yp, yp, ALU.mult).then_inc(done, 1)
                if not first:
                    pool.wait_ge(done, 2 * j + s0)
                    nc.gpsimd.tensor_tensor(acc[:, :, :], acc[:, :, :], sq[:, :, :], ALU.add).then_inc(done, 1)
                pool.wait_ge(done, 1 + s0 if first else 2 * j + (s0 + 1))
                nc.gpsimd.tensor_tensor(yp, yp, gains("post", j), ALU.mult).then_inc(ro, 1)
            loop(pool, 7, post, first=True)
            pool.wait_ge(sem("last_squares"), 1)
            nc.gpsimd.tensor_tensor(y[:, 14:16], y[:, 14:16], gains("post", 7), ALU.mult).then_inc(ro, 1)
            pool.wait_ge(sem("rsqrt_ready"), NORM["post"])
            pool.wait_ge(ro, 8)
            for n, j in enumerate((5, 6, 7)):
                yp, xp = pair(y)(j), pair(x)(j)
                nc.gpsimd.tensor_tensor(yp, yp, rr[:, :].unsqueeze(1).to_broadcast([P, 2, S]), ALU.mult)\
                    .then_inc(sem("out_pool"), 1)
                pool.wait_ge(sem("out_pool"), 2 * n + 1)
                nc.gpsimd.tensor_tensor(xp, xp, yp, ALU.add).then_inc(sem("out_pool"), 1)

        @block.tensor
        def _(pe):
            def mm(out, lhsT, rhs, start=True, stop=True):
                return nc.tensor.matmul(out, lhsT, rhs, start=start, stop=stop, skip_group_check=True)

            def turn(out, in_, idn):
                return nc.tensor.transpose(out, in_, idn)

            def unit(name, it, n, j, K=KT, tokens=False, src=None, hwait=None, step=None,
                     narrow=False, hoff=0, gwait=None):
                hi, lo = src or (h_hi, h_lo)
                u = UNIT0[name] + j
                blk0 = j * K
                if isinstance(it, int):
                    blk0 += it * n * K
                    if UNIT0[name] + n * it + j >= 2:
                        pe.wait_ge(evacuated, UNIT0[name] + n * it + j - 1)
                else:
                    pe.wait_ge(evacuated, n * it + (u - 1))
                per = 0 if isinstance(it, int) else n * K // BLK
                for k in range(K):
                    blk = blk0 + (k // 2 if narrow else k)
                    half = (k % 2) * P if narrow else 0
                    c, sub = CHUNK0[name] + blk // BLK, blk % BLK
                    w0 = sub * BW + half
                    slot = c % SLOTS
                    if (sub == 0 or k == 0) and half == 0:
                        pe.wait_ge(lo_ready, per * it + (c + 1))
                    if hwait is not None:
                        pe.wait_ge(h_ready, hwait + k + 1)
                    if gwait is not None and k % 2 == 0:
                        pe.wait_ge(sem("g_ready"), gwait + k // 2 + 1)
                    for t in range(1 if narrow else 2):
                        o = bank[(UNIT0[name] + j + (n * it if isinstance(it, int) else 0)) % 2][:, t, :]
                        if tokens:
                            wh, wl = w_hi[:, slot, w0:w0 + BW], w_lo[:, slot, w0:w0 + BW]
                            ah = hi[:, hoff + k, t * P:(t + 1) * P]
                            al = lo[:, hoff + k, t * P:(t + 1) * P]
                            mm(o, ah, wh, k == 0 and t == 0, False)
                            mm(o, al, wh, False, False)
                            last = mm(o, ah, wl, False, k == K - 1)
                        else:
                            wh = w_hi[:, slot, w0 + t * P:w0 + (t + 1) * P]
                            wl = w_lo[:, slot, w0 + t * P:w0 + (t + 1) * P]
                            mm(o, wh, hi[:, hoff + k, :], k == 0 and t == 0, False)
                            mm(o, wh, lo[:, hoff + k, :], False, False)
                            last = mm(o, wl, hi[:, hoff + k, :], False, k == K - 1)
                    if sub == BLK - 1 and (not narrow or half):
                        last.then_inc(w_used, 1)
                    elif k == K - 1:
                        last.then_inc(sem("mid_chunk"), 1)
                    if step is not None and sub % 2 == 1:
                        step(K // BLK * 2 * j + k // 2)

            def token_sums(a, out):
                for t in range(2):
                    for i in range(2):
                        last = mm(out[:, t:t + 1], a[:, i, t * P:(t + 1) * P], ones[:, 0:1], i == 0, i == 1)
                return last

            def norm_sum(name, nt=8, columns=False):
                pe.wait_ge(sem("cst_in"), 16)
                pe.wait_ge(sem("squares"), SQ0[name] + 2 * nt - 1)
                if NORM[name] > 1:
                    pe.wait_ge(sem("rms_ready"), NORM[name] - 1)
                mm(pb[5][:, 0, :], ones, acc[:, 0, :], True, False)
                last = mm(pb[5][:, 0, :], ones, acc[:, 1, :], False, True)
                if columns:
                    last = token_sums(acc, pb[5][:, 1, 0:2])
                last.then_inc(sem("norm_sum"), 1)

            def gdn(g, it):
                if g == 1:
                    pe.wait_ge(sem("pair_ready"), 4 * it + 2)
                    for b in range(4):
                        kb = kn[:, b // 2, (b % 2) * P:(b % 2 + 1) * P]
                        mm(pb4[0][:, b], kb, kb)
                    for b in range(4):
                        kb, qb = (t[:, b // 2, (b % 2) * P:(b % 2 + 1) * P] for t in (kn, qn))
                        last = mm(pb4[1][:, b], kb, qb)
                    last.then_inc(sem("grams"), 1)
                elif g == 2:
                    pe.wait_ge(sem("head_rows"), 4 * it + 4)
                    mm(pb4[2], ones[0:8, :], rows[0:8, 2:4, :].rearrange("p a b -> p (a b)"))
                    mm(pb4[3], ones[32:40, :], rows[32:40, 2:4, :].rearrange("p a b -> p (a b)"))\
                        .then_inc(sem("rows_spread"), 1)
                elif g == 3:
                    pe.wait_ge(sem("inv0_ready"), it + 1)
                    for b in range(4):
                        last = turn(pb4[0][:, b], invT[:, b], ident)
                    last.then_inc(sem("inv0_turned"), 1)
                    for i in range(2):
                        turn(pb4[4][:, i], kn[:, i, 0:P], ident)
                    pe.wait_ge(sem("pair_ready"), 4 * it + 3)
                    for b in range(4):
                        last = turn(pb4[5][:, b], vs[:, b // 2, (b % 2) * P:(b % 2 + 1) * P], ident)
                    last.then_inc(sem("kv_token_major"), 1)
                elif g < 16 and g % 2 == 0:
                    l = (g - 4) // 2
                    pe.wait_ge(sem("level_part"), 6 * it + (l + 1))
                    if l == 0:
                        pe.wait_ge(sem("inv0_copied"), it + 1)
                    else:
                        pe.wait_ge(sem("inv_updated"), 11 * it + (2 * l - 1))
                    for b in range(4):
                        last = mm(pb4[1][:, b], lv[:, b], inv[:, b])
                    last.then_inc(sem("level_product"), 1)
                elif g < 16:
                    l = (g - 5) // 2
                    pe.wait_ge(sem("level_copied"), 6 * it + (l + 1))
                    if l:
                        pe.wait_ge(sem("inv_updated"), 11 * it + 2 * l)
                    if l < 5:
                        for b in range(4):
                            mm(pb4[2][:, b], invT[:, b], lp[:, b])
                    for b in range(4):
                        last = mm(pb4[3][:, b], lp[:, b], invT[:, b])
                    last.then_inc(sem("level_update"), 1)
                elif g == 16:
                    pe.wait_ge(sem("inv_updated"), 11 * it + 11)
                    pe.wait_ge(sem("kv_scaled"), 4 * it + 4)
                    for i in range(2):
                        last = mm(pb4[0][:, i], invT[:, 2 * i], vb[:, 2 * i])
                    last.then_inc(sem("new0"), 1)
                elif g == 17:
                    pe.wait_ge(sem("new_copied"), 2 * it + 1)
                    pe.wait_ge(sem("kd_ready"), it + 1)
                    for i in range(2):
                        last = mm(pb4[1][:, i], kd[:, i], vn[:, 2 * i])
                    last.then_inc(sem("state"), 1)
                elif g == 18:
                    pe.wait_ge(sem("state_copied"), it + 1)
                    for i in range(2):
                        last = mm(pb4[2][:, i], kn[:, i, P:2 * P], s1[:, i])
                    last.then_inc(sem("k_state"), 1)
                elif g == 19:
                    pe.wait_ge(sem("rest_ready"), 2 * it + 2)
                    for i in range(2):
                        last = mm(pb4[3][:, i], invT[:, 2 * i + 1], r1[:, i])
                    last.then_inc(sem("new1"), 1)
                elif g == 20:
                    pe.wait_ge(sem("new_copied"), 2 * it + 2)
                    pe.wait_ge(sem("att_ready"), 3 * it + 3)
                    for b in range(4):
                        last = mm(pb4[4][:, b], vn[:, b], attT[:, b], True, b % 2 == 0)
                        if b % 2:
                            last = mm(pb4[4][:, b], s1[:, b // 2], qd[:, b // 2], False, True)
                    last.then_inc(sem("gdn_out"), 1)
                elif g == 21:
                    pe.wait_ge(sem("out_mixed"), it + 1)
                    mm(pb[5][:, :, :], ones, osq[:, :, :]).then_inc(sem("out_sums"), 1)

            def xa(a, h):
                if a == 0:
                    pe.wait_ge(evacuated, 2 * h + (UNIT0["xq"] + 2))
                    for t in range(2):
                        for kk in range(4):
                            last = mm(pb[0][:, t, :], xq[:, kk, t * P:(t + 1) * P],
                                      kx[:, sl(4 * h + kk, 1), :], kk == 0, kk == 3)
                    last.then_inc(sem("xa_scores"), 1)
                elif a == 1:
                    pe.wait_ge(sem("xa_prob"), 2 * h + 2)
                    for t in range(2):
                        for m in range(2):
                            last = turn(pb[1][:, m, t * P:(t + 1) * P], pr[:, t, m * P:(m + 1) * P], ident)
                    last.then_inc(sem("xa_turned"), 1)
                else:
                    pe.wait_ge(sem("xa_prob_copied"), h + 1)
                    pe.wait_ge(sem("vh_ready"), h + 1)
                    for jj in range(4):
                        for m in range(2):
                            last = mm(pb[2 + jj // 2][:, jj % 2, :], vh[:, m, jj * P:(jj + 1) * P],
                                      pT[:, m, :], m == 0, m == 1)
                    last.then_inc(sem("xa_pv"), 1)

            def ca(a, kind, it):
                def n(k):
                    return 2 * k * it + (k if kind == "mla" else 0)
                if a == 0:
                    if kind == "fox":
                        pe.wait_ge(sem("forget_rows"), 2 * it)
                        mm(pb4[2], ones[0:8, :], rows[0:8, 2:4, :].rearrange("p a b -> p (a b)"))
                        for i in range(2):
                            for t in range(2):
                                last = mm(pb[i][:, t, :], fq[:, i, t * P:(t + 1) * P], fk[:, i, :])
                    else:
                        pe.wait_ge(sem("mla_q_masked"), 2 * it + 2)
                        pe.wait_ge(sem("qpair_ready"), it + 1)
                        for i in range(2):
                            for t in range(2):
                                q = slice(t * P, (t + 1) * P)
                                mm(pb[i][:, t, :], qpair[:, i, q], knope[:, sl(2 * it + i, 1), :], True, False)
                                last = mm(pb[i][:, t, :], qmask[:, i, q], kr[:, :], False, True)
                    last.then_inc(sem("ca_scores"), 1)
                elif a == 1:
                    pe.wait_ge(sem("ca_prob"), n(4))
                    for i in range(2):
                        for t in range(2):
                            for m in range(2):
                                last = turn(pb[3 + i][:, m, t * P:(t + 1) * P],
                                            pr2[:, 2 * i + t, m * P:(m + 1) * P], ident)
                    last.then_inc(sem("ca_turned"), 1)
                else:
                    pe.wait_ge(sem("ca_prob_copied"), n(2))
                    if kind == "mla":
                        pe.wait_ge(sem("vpair_ready"), it + 1)
                    v = fv if kind == "fox" else vpair
                    for i in range(2):
                        for m in range(2):
                            last = mm(pb[5][:, i, m * P:], v[:, m, i * P:(i + 1) * P],
                                      pT2[:, 2 * i + m, m * P:], m == 0, m == 1)
                    last.then_inc(sem("ca_pv"), 1)


            def phase(name, count, norm=None, hwait=None, columns=False, step0=None, late=False, **kw):
                unit(name, 0, 2, 0, hwait=hwait, step=step0, **kw)
                if norm is not None and not late:
                    norm_sum(norm, columns=columns)
                unit(name, 0, 2, 1, step=lambda s: norm_sum(norm, columns=columns) if late and s == 10 else None,
                     **kw)
                with pe.Fori(1, count // 2) as it:
                    for j in range(2):
                        unit(name, it, 2, j, **kw)

            phase("xk", 8, norm="mem", hwait=HFILL["mem"], columns=True, late=True)
            with pe.Fori(0, 4) as it:
                for j in range(2):
                    unit("xv", it, 2, j, tokens=True)

            unit("ba", 0, 1, 0, K=KT, narrow=True, hwait=HFILL["mix"])
            norm_sum("mix")
            with pe.Fori(0, 4) as it:
                for j in range(2):
                    unit("qkv", it, 2, j)
            pe.wait_ge(sem("ba_dve"), 6)
            pe.wait_ge(sem("ba_act"), 4)
            for n in range(2):
                g_last = turn(pb[5][:, 0, 8 * n:8 * n + 8], rows[0:8, 0, n * P:(n + 1) * P], ident[0:8, 0:8])
            g_last.then_inc(sem("ba_cols"), 1)
            for n in range(2):
                last = turn(pb[4][:, 0, 8 * n:8 * n + 8], rows[32:40, 0, n * P:(n + 1) * P],
                            ident[32:40, 32:40])
            last.then_inc(sem("ba_cols"), 1)

            def k_sums(u):
                pe.wait_ge(sem("k_squares"), 2 * u + 2)
                for i in range(2):
                    for t in range(2):
                        last = mm(pb[3][:, 0, 8 * t + 2 * u + i:8 * t + 2 * u + i + 1],
                                  sq[:, i, t * P:(t + 1) * P], ones[:, 0:1])
                last.then_inc(sem("k_summed"), 1)
            for u in range(4):
                unit("qkv", 4 + u // 2, 2, u % 2,
                     step=lambda s: k_sums(2 * u + s % 8 // 4) if u < 2 and s % 4 == 0 else None)
                if u == 2:
                    pe.wait_ge(sem("k_norm"), 1)
                    for t in range(2):
                        last = turn(pb[2][0:8, 0, t * P:(t + 1) * P], smc(RK_COL + 8 * t, 8), ident)
                    last.then_inc(sem("k_rows"), 1)
            with pe.Fori(0, 4) as it:
                for j in range(4):
                    unit("gdn", it, 4, j, step=lambda s: gdn(GDN_SLOT[s], it) if s in GDN_SLOT else None)

            phase("mixo", 8, hwait=HFILL["y"])

            def xq_units(it):
                def step(s):
                    if isinstance(it, int):
                        return
                    if s == 0:
                        xa(0, it - 1)
                    elif s == 5:
                        xa(1, it - 1)
                    elif s == 9:
                        xa(2, it - 1)
                for j in range(2):
                    unit("xq", it, 2, j, hwait=HFILL["xa"] if isinstance(it, int) and j == 0 else None, step=step)
                    if isinstance(it, int) and j == 0:
                        norm_sum("xa")
            xq_units(0)
            with pe.Fori(1, 4) as it:
                xq_units(it)
            LAST_XA = {1: 0, 4: 1, 5: 2}
            phase("xo", 8, hwait=HFILL["o"],
                  step0=lambda s: xa(LAST_XA[s], XH - 1) if s in LAST_XA else None)
            for s, nt in enumerate(SEGS):
                if s == 0:
                    phase("up0", nt, norm="ffn", hwait=HFILL["ffn"])
                else:
                    with pe.Fori(0, nt // 2) as it:
                        for j in range(2):
                            unit(f"up{s}", it, 2, j)
                g0 = sum(SEGS[:s]) // 2
                n = 2 if nt == KT else 4
                for j in range(n):
                    unit(f"down{s}", 0, n, j, K=nt, src=(g_hi, g_lo), gwait=g0 if j == 0 else None)
                with pe.Fori(1, 8 // n) as it:
                    for j in range(n):
                        unit(f"down{s}", it, n, j, K=nt, src=(g_hi, g_lo))
            unit("lat", 0, 2, 0, hwait=HFILL["pre"])
            pe.wait_ge(sem("pre_squares"), 5 * 8 - 2)
            for i, a in enumerate((acc, acc2)):
                mm(pb[5][:, i, :], ones, a[:, 0, :], True, False)
                mm(pb[5][:, i, :], ones, a[:, 1, :], False, True)
                last = token_sums(a, pb[4][:, 0, 2 * i:2 * i + 2])
            last.then_inc(sem("norm_sum"), 1)
            unit("lat", 0, 2, 1)
            with pe.Fori(1, 3) as it:
                for j in range(2):
                    unit("lat", it, 2, j)
            pe.wait_ge(sem("pre_dve"), 1)
            norm_sum("gq", 3)
            latents = (lh_hi, lh_lo)
            for u in range(6):
                unit("uq", 0, 6, u, K=6, src=latents, hwait=HFILL["gq"] if u == 0 else None)
                if u == 2:
                    norm_sum("gkv", 2, columns=True)
            for u in range(8):
                unit("ukv", 0, 8, u, K=4, tokens=u >= 4, src=latents, hoff=6,
                     hwait=HFILL["gkv"] if u == 0 else None)
                if u == 3:
                    pe.wait_ge(sem("forget_dve"), 6)
                    for n in range(2):
                        last = turn(pb[2][:, 0, 8 * n:8 * n + 8], rows[0:8, 0, n * P:(n + 1) * P],
                                    ident[0:8, 0:8])
                    last.then_inc(sem("forget_cols"), 1)

            FOX_AT, MLA_AT = {1: 0, 8: 1, 12: 2}, {15: 0, 21: 1, 25: 2}

            def fox(it):
                def step(s):
                    if s in FOX_AT and not isinstance(it, int):
                        ca(FOX_AT[s], "fox", it)
                    elif s in MLA_AT:
                        ca(MLA_AT[s], "mla", it)
                for j in range(4):
                    unit("fox", it, 4, j, tokens=j == 3, step=step)
            fox(0)
            with pe.Fori(1, 4) as it:
                fox(it)
            for j in range(4):
                unit("gm", 0, 4, j, step=lambda s: ca(FOX_AT[s], "fox", 4) if s in FOX_AT else None)
            phase("out", 8, hwait=HFILL["o2"])
            pe.wait_ge(sem("squares"), SQ0["post"] + 13)
            mm(pb[5][:, 0, :], ones, acc[:, 0, :], True, False)
            mm(pb[5][:, 0, :], ones, acc[:, 1, :], False, False)
            pe.wait_ge(sem("last_squares"), 1)
            mm(pb[5][:, 0, :], ones, acc2[:, 0, :], False, False)
            mm(pb[5][:, 0, :], ones, acc2[:, 1, :], False, True).then_inc(sem("norm_sum"), 1)

        CA_FOX, CA_MLA = {0: -1, 1: 0, 5: 1, 7: 2}, {6: -1, 8: 0, 11: 1, 13: 2}

        @block.scalar
        def _(act):
            def A(out, in_, func, bias=0.0, scale=1.0, **kw):
                return nc.scalar.activation(out, in_, func, bias=bias, scale=scale, **kw)

            def split(c, per=0, it=0):
                if isinstance(it, int):
                    c, it, per = c + per * it, 0, 0
                    if c >= N_CHUNKS:
                        return
                s = c % SLOTS
                act.wait_ge(raw_ready[s], 16 * per // SLOTS * it + 16 * (c // SLOTS + 1))
                if c >= SLOTS:
                    act.wait_ge(w_used, per * it + (c - SLOTS + 1))
                A(w_hi[:, s], raw[:, s], ACT.Copy).then_inc(hi_ready, 1)

            def units(name, it, n, evac=None, react=None, K=KT, after=None):
                m = n * K // BLK
                for j in range(n):
                    for i in range(K // BLK):
                        if react is not None:
                            react(j, i)
                        if i == K // BLK - 1 and evac is not None:
                            evac(j)
                        split(CHUNK0[name] + j * K // BLK + i + SLOTS, m, it)
                    if after is not None:
                        after(j)

            def norm_rms(name, width, out=rr, column=None):
                act.wait_ge(sem("norm_sum"), NORM[name])
                a = A(out[:, :], pb[5][:, 0, :], ACT.Sqrt, bias=c1("eps"), scale=1.0 / width)
                if column is not None:
                    a = A(smc(column, 2), pb[5][:, 1, 0:2], ACT.Sqrt, bias=c1("eps"), scale=1.0 / width)
                a.then_inc(sem("rms_ready"), 1)

            def hi(out, in_, gain=None):
                A(out, in_, ACT.Copy, **({} if gain is None else {"scale": gain})).then_inc(sem("h_hi_ready"), 1)

            def fill(after, g, src, gain=None):
                act.wait_ge(w_used, after - 3 + g)
                for k in range(4 * g, 4 * g + 4):
                    hi(h_hi[:, k], src[:, k], None if gain is None else col(gain, k))

            def fill_x(name, prev, after, g):
                act.wait_ge(evacuated, UNIT0[prev] + 2 * g + 2)
                fill(after, g, x, name)

            def phase(name, count, n=2, evac=None, first=None, last=None, K=KT, after=None, free=False, react0=None):
                def ev(it):
                    def e(j):
                        if first is not None and isinstance(it, int) and it == 0 and j == 0:
                            first()
                        if evac is not None:
                            evac(it, j)
                    return e

                def re(j, i):
                    g = i - 1 + 4 - K // BLK
                    if j == n - 1 and g >= 0:
                        last(g)
                def af(it):
                    return None if after is None else lambda j: after(it, j)
                its = count // n
                lo_ = 0 if first is None and react0 is None else 1
                up_ = its if last is None else its - 1
                if lo_:
                    units(name, 0, n, ev(0), react0, K=K, after=af(0))
                if up_ > lo_:
                    with act.Fori(lo_, up_) as it:
                        units(name, it, n, ev(it), K=K, after=af(it))
                if last is not None and free:
                    def ev_last(j):
                        if j == n - 1:
                            last(3)
                        elif evac is not None:
                            evac(its - 1, j)
                    units(name, its - 1, n, ev_last, re, K=K)
                    if evac is not None:
                        evac(its - 1, n - 1)
                elif last is not None:
                    units(name, its - 1, n, ev(its - 1), re, K=K)
                    last(3)

            for c in range(SLOTS):
                split(c)
                act.wait_ge(sem("cols_in"), 16)
                act.wait_ge(sem(f"mem_in{c}"), 16)
                for k in range(4 * c, 4 * c + 4):
                    hi(h_hi[:, k], x[:, k], col("mem", k))
            act.wait_ge(sem("cst_in"), 16)
            phase("xk", 8, first=lambda: norm_rms("mem", D, column=R_COL))

            def mix_fill(g):
                if g == 0:
                    act.wait_ge(sem("x_in"), 16)
                fill(CHUNK0["ba"], g, x, "mix")
            phase("xv", 8, last=mix_fill, free=True)
            split(CHUNK0["ba"] + SLOTS)
            norm_rms("mix", D)
            split(CHUNK0["ba"] + SLOTS + 1)
            r = rows

            def ba_steps(j, i):
                if (j, i) == (0, 0):
                    act.wait_ge(evacuated, UNIT0["ba"] + 1)
                    A(r[0:8, 2], r[0:8, 1], ACT.Abs, bias=col("dtb", 0, slice(0, 8))).then_inc(sem("ba_act"), 1)
                    A(r[32:40, 0], r[32:40, 1], ACT.Sigmoid).then_inc(sem("ba_act"), 1)
                elif (j, i) == (0, 1):
                    A(sm[0:8, EA_COL:EA_COL + 1], col("alog", 0, slice(0, 8)), ACT.Exp).then_inc(sem("ba_act"), 1)
                    act.wait_ge(sem("ba_act"), 1)
                    A(r[0:8, 2], r[0:8, 2], ACT.Exp, scale=-1.0).then_inc(sem("ba_act"), 1)
                elif (j, i) == (0, 2):
                    act.wait_ge(sem("ba_dve"), 1)
                    A(r[0:8, 2], r[0:8, 2], ACT.Ln).then_inc(sem("ba_act"), 1)

            def qkv_body(it, extra=None):
                def react(j, i):
                    if extra is not None:
                        extra(j, i)

                def evac(j):
                    act.wait_ge(sem("bank_scaled"), 2 * it + (j + 1))
                    b = bank[(UNIT0["qkv"] + j) % 2]
                    c = (cy, cz)[j]
                    for t in range(2):
                        A(c[:, t], b[:, t], ACT.Copy, scale=col("gconv", 24 * 3 + (4 * it + (2 * j + t))))\
                            .then_inc(sem("qkv_tap0"), 1)

                def after(j):
                    act.wait_ge(evacuated, 2 * it + (UNIT0["qkv"] + j + 1))
                    A(qkv[:, sl(4 * it + 2 * j, 2)], (cy, cz)[j][:, :], ACT.Silu).then_inc(sem("qkv_ready"), 1)
                units("qkv", it, 2, evac, react, after=after)
            qkv_body(0, ba_steps)
            with act.Fori(1, 5) as it:
                qkv_body(it)

            def k_norm(j, i):
                if (j, i) == (0, 1):
                    act.wait_ge(sem("k_summed"), 4)
                    A(smc(RK_COL, 16), pb[3][:, 0, 0:16], ACT.Sqrt, bias=c1("eps")).then_inc(sem("k_rms"), 1)
                elif (j, i) == (1, 0):
                    act.wait_ge(sem("k_rows"), 1)
                    A(rows[32:40, 1], pb[2][0:8, 0, :], ACT.Copy).then_inc(sem("k_rows_copied"), 1)
                    act.wait_ge(sem("ba_dve"), 7)
                    A(smc(EG_COL, 8), smc(G_COL + 8, 8), ACT.Exp).then_inc(sem("ba_act"), 1)
            qkv_body(5, k_norm)

            def gdn(g, it):
                if g == 2:
                    act.wait_ge(sem("dec_args"), 6 * it + 6)
                    A(dec[:, :, :], dec[:, :, :], ACT.Exp).then_inc(sem("dec_ready"), 1)
                    A(qd[:, :, :], pb4[2].rearrange("p (i n) c -> p n i c", n=2)[:, 1], ACT.Exp)\
                        .then_inc(sem("q_decay"), 1)
                    A(smc(KD_COL, 2), smc(KD_ARG, 2), ACT.Exp).then_inc(sem("k_decay"), 1)
                elif g == 3:
                    act.wait_ge(sem("inv0_turned"), it + 1)
                    A(inv[:, :, :], pb4[0], ACT.Copy).then_inc(sem("inv0_copied"), 1)
                elif 4 <= g < 16 and g % 2 == 0:
                    act.wait_ge(sem("level_product"), 6 * it + ((g - 4) // 2 + 1))
                    A(lp[:, :, :], pb4[1], ACT.Copy).then_inc(sem("level_copied"), 1)
                    if g == 14:
                        act.wait_ge(sem("kv_token_major"), it + 1)
                        for b in range(4):
                            A(vb[:, b], pb4[5][:, b], ACT.Copy, scale=smc(B_COL + (b % 2) * 8 + b // 2 + 2 * it))\
                                .then_inc(sem("kv_scaled"), 1)
                elif g in (16, 19):
                    n = (g - 16) // 3
                    act.wait_ge(sem(f"new{n}"), it + 1)
                    A(vn[:, :, :].rearrange("p (i n) c -> p n i c", n=2)[:, n], pb4[3 * n][:, 0:2], ACT.Copy)\
                        .then_inc(sem("new_copied"), 1)
                elif g == 17:
                    act.wait_ge(sem("state"), it + 1)
                    A(s1[:, :, :], pb4[1][:, 0:2], ACT.Copy).then_inc(sem("state_copied"), 1)
                elif g == 20:
                    act.wait_ge(sem("gdn_out"), it + 1)
                    A(osq[:, :, :], pb[4][:, :, :], ACT.Square).then_inc(sem("out_squares"), 1)
                elif g == 21:
                    act.wait_ge(sem("out_sums"), it + 1)
                    A(osq[:, :, :], pb[5][:, :, :], ACT.Sqrt, bias=c1("epsq0"), scale=1.0 / P)\
                        .then_inc(sem("out_rms"), 1)

            def gdn_unit(it, fills=False):
                def react(j, i):
                    if (j, i) == (0, 0) and not (isinstance(it, int) and it == 0):
                        gdn(21, it - 1)
                    for s in (8 * j + 2 * i, 8 * j + 2 * i + 1):
                        if s in GDN_REACT:
                            gdn(GDN_REACT[s], it)
                    if fills and j == 3 and i > 0:
                        fill_y(i - 1)

                def evac(j):
                    if j == 0:
                        act.wait_ge(evacuated, 4 * it + (UNIT0["gdn"] + 1))
                        A(zs[:, :], zs[:, :], ACT.Silu).then_inc(sem("z_ready"), 1)
                    elif j == 3 and fills:
                        gdn(21, it)

                def after(j):
                    if j == 3:
                        act.wait_ge(evacuated, 4 * it + (UNIT0["gdn"] + 4))
                        for t in range(2):
                            A(cv[:, t], cw[:, t], ACT.Copy, scale=col("sconv", 8 * 2 + (2 * it + t)))\
                                .then_inc(sem("sc_tap0"), 1)
                return react, evac, after

            def fill_y(g):
                act.wait_ge(sem("sc_y"), g + 1)
                act.wait_ge(w_used, CHUNK0["mixo"] - 3 + g)
                for k in range(4 * g, 4 * g + 4):
                    if k % 4 == 2:
                        act.wait_ge(sem("gdn_y"), 2 * g + 2)
                    hi(h_hi[:, k], y[:, k])

            act.wait_ge(sem("qkv_ready"), 12)
            react, evac, after = gdn_unit(0)
            units("gdn", 0, 4, evac, react, after=after)
            with act.Fori(1, 3) as it:
                react, evac, after = gdn_unit(it)
                units("gdn", it, 4, evac, react, after=after)
            react, evac, after = gdn_unit(3, fills=True)
            units("gdn", 3, 4, evac, react, after=after)

            def last_y(j, i):
                if (j, i) == (0, 1):
                    fill_y(3)
            phase("mixo", 8, react0=last_y, last=lambda g: fill_x("xa", "mixo", CHUNK0["xq"], g))

            XSC = 512 ** -0.5

            def xa(a, h):
                if a == 0:
                    act.wait_ge(sem("xa_nmax"), 2 * h + 2)
                    for t in range(2):
                        A(pr[:, t], pb[0][:, t], ACT.Exp, bias=smc(NMAX + t), scale=XSC,
                          accum_out=smc(RSUM + t)).then_inc(sem("xa_exp"), 1)
                elif a == 1:
                    act.wait_ge(sem("xa_turned"), h + 1)
                    A(pT[:, 0:2], pb[1][:, :, :], ACT.Copy).then_inc(sem("xa_prob_copied"), 1)

            units("xq", 0, 2, lambda j: norm_rms("xa", D) if j == 0 else None)

            def xq_react(it):
                def react(j, i):
                    if (j, i) == (0, 0):
                        xa(0, it - 1)
                    elif (j, i) == (0, 2):
                        xa(1, it - 1)
                    elif isinstance(it, int) and j == 1 and i > 0:
                        fill_o(i - 1)
                return react

            def fill_o(g):
                act.wait_ge(sem("xa_o"), 2 * g + 1)
                act.wait_ge(w_used, CHUNK0["xo"] - 3 + g)
                for k in range(4 * g, 4 * g + 4):
                    if k % 4 == 2:
                        act.wait_ge(sem("xa_o"), 2 * g + 2)
                    hi(h_hi[:, k], y[:, k])
            with act.Fori(1, 3) as it:
                units("xq", it, 2, react=xq_react(it))
            units("xq", 3, 2, react=xq_react(3))

            def last_head(j, i):
                if (j, i) == (0, 1):
                    xa(0, XH - 1)
                elif (j, i) == (0, 2):
                    xa(1, XH - 1)
                elif (j, i) == (0, 3):
                    fill_o(3)
            phase("xo", 8, react0=last_head, last=lambda g: fill_x("ffn", "xo", CHUNK0["up0"], g))

            def fill_pre(g):
                act.wait_ge(sem("gains_ready"), 1)
                act.wait_ge(evacuated, UNIT0["down2"] + 2 * g + 2)
                for k in range(4 * g, 4 * g + 4):
                    hi(h_hi[:, k], x[:, k], smc(GG_COL + k))
            tile0 = 0
            for s, nt in enumerate(SEGS):
                name = f"up{s}"
                g0 = sum(SEGS[:s]) // 2

                def evac(it, j):
                    act.wait_ge(sem("bank_scaled"), 2 * it + (12 + 2 * g0 + j + 1))
                    b = bank[(UNIT0[name] + j) % 2]
                    c = (cy, cw)[j]
                    for t in range(2):
                        A(c[:, t], b[:, t], ACT.Copy,
                          scale=col("fconv", 88 * 2 + 44 * j + tile0 + t + 2 * it)).then_inc(sem("up_tap0"), 1)

                def after(it, j):
                    act.wait_ge(evacuated, 2 * it + (UNIT0[name] + j + 1))
                    if j == 0:
                        A(cz[:, :], cy[:, :], ACT.Silu).then_inc(sem("gate_ready"), 1)
                    else:
                        act.wait_ge(sem("gated"), it + (g0 + 1))
                        A(g_hi[:, sl(2 * it, 2)], cv[:, :], ACT.Copy).then_inc(sem("g_hi_ready"), 1)
                phase(name, nt, evac=evac, after=after, first=(lambda: norm_rms("ffn", D)) if s == 0 else None)
                tile0 += nt
                if nt == KT:
                    phase(f"down{s}", 8)
                    act.wait_ge(w_used, CHUNK0[f"down{s}"] + 2 * nt)
                else:
                    phase(f"down{s}", 8, n=4, K=nt, last=lambda g: fill_pre(g))

            def pre_rms():
                act.wait_ge(sem("norm_sum"), NORM["pre"])
                A(rf[:, :], pb[5][:, 0, :], ACT.Sqrt, bias=c1("eps"), scale=1.0 / D)
                A(smc(RF_COL, 2), pb[4][:, 0, 0:2], ACT.Sqrt, bias=c1("eps"), scale=1.0 / D)\
                    .then_inc(sem("pre_rms"), 1)
                act.wait_ge(sem("pre_dve"), 1)
                A(rr[:, :], rr[:, :], ACT.Sqrt, bias=c1("eps"), scale=1.0 / D)
                A(smc(R_COL, 2), smc(R2_COL, 2), ACT.Sqrt, bias=c1("eps"), scale=1.0 / D)\
                    .then_inc(sem("rms_ready"), 1)
            units("lat", 0, 2, lambda j: pre_rms() if j == 0 else None)

            def lat_react(it):
                def react(j, i):
                    if (it, j, i) == (1, 0, 2):
                        act.wait_ge(sem("rope_dve"), 8)
                        A(qm[:, :], sinr[:, :], ACT.Abs).then_inc(sem("rope_act"), 1)
                        A(sinr[:, :], sinr[:, :], ACT.Sin).then_inc(sem("rope_act"), 1)
                        act.wait_ge(sem("rope_act"), 1)
                        A(cosr[:, :], qm[:, :], ACT.Sin, bias=c1("hpi"), scale=-1.0).then_inc(sem("rope_act"), 1)
                    elif (it, j, i) == (2, 0, 1):
                        act.wait_ge(evacuated, UNIT0["lat"] + 3)
                        for k in range(4):
                            hi(lh_hi[:, k], lat[:, k], col("gq", k))
                    elif (it, j, i) == (2, 0, 2):
                        for k in range(4, 6):
                            hi(lh_hi[:, k], lat[:, k], col("gq", k))
                    elif (it, j, i) == (2, 1, 1):
                        act.wait_ge(evacuated, UNIT0["lat"] + 5)
                        for k in range(4):
                            hi(lh_hi[:, 6 + k], lat[:, 6 + k], col("gkv", k))
                return react
            for it in (1, 2):
                units("lat", it, 2, react=lat_react(it))
            norm_rms("gq", 768, out=rq)
            for c in range(9 + 8):
                split(CHUNK0["uq"] + c + SLOTS)
                if c == 0:
                    act.wait_ge(evacuated, UNIT0["lat"] + 6)
                    A(qm[0:64, :], lat[64:128, 10], ACT.Copy).then_inc(sem("kr_swap"), 1)
                    A(qm[64:128, :], lat[0:64, 10], ACT.Copy).then_inc(sem("kr_swap"), 1)
                    A(r[0:8, 2], lat[0:8, 11], ACT.Abs, bias=col("bfor", 0, slice(0, 8))).then_inc(sem("forget_act"), 1)
                    act.wait_ge(sem("forget_act"), 1)
                    A(r[0:8, 2], r[0:8, 2], ACT.Exp, scale=-1.0).then_inc(sem("forget_act"), 1)
                elif c == 1:
                    act.wait_ge(sem("forget_dve"), 1)
                    A(r[0:8, 2], r[0:8, 2], ACT.Ln).then_inc(sem("forget_act"), 1)
                elif c == 6:
                    norm_rms("gkv", 512, out=rkv, column=RKV_COL)
                elif c in (10, 12):
                    for p in range((c - 10), (c - 10) + 2):
                        act.wait_ge(evacuated, UNIT0["uq"] + (5 if p < 2 else 6))
                        A(tn[0:64, p], lat[64:128, p], ACT.Copy).then_inc(sem("qr_swap"), 1)
                        A(tn[64:128, p], lat[0:64, p], ACT.Copy).then_inc(sem("qr_swap"), 1)

            def ca(a, kind, it):
                def n(k):
                    return 2 * k * it + (k if kind == "mla" else 0)
                if a == 0:
                    act.wait_ge(sem("ca_nmax"), n(1))
                    for q in range(4):
                        A(pr2[:, q], db[:, q], ACT.Exp, bias=smc(NMAX + q), accum_out=smc(RSUM + q))\
                            .then_inc(sem("ca_exp"), 1)
                elif a == 1:
                    act.wait_ge(sem("ca_turned"), n(1))
                    A(pT2[:, 0:2], pb[3][:, :, :], ACT.Copy).then_inc(sem("ca_prob_copied"), 1)

            def fox_react(it, fox=True, mla=True):
                def react(j, i):
                    q = 4 * j + i
                    if q in CA_FOX and fox:
                        ca(CA_FOX[q], "fox", it)
                    elif q in CA_MLA and mla:
                        ca(CA_MLA[q], "mla", it)
                    elif not mla and j == 3 and i > 0:
                        fill_o2(i - 1)
                return react

            def fox_evac(it):
                def evac(j):
                    if j == 2:
                        act.wait_ge(evacuated, 4 * it + (UNIT0["fox"] + 3))
                        A(fg[:, :], fg[:, :], ACT.Silu).then_inc(sem("fg_ready"), 1)
                return evac
            units("fox", 0, 4, fox_evac(0), fox_react(0, fox=False))
            with act.Fori(1, 4) as it:
                units("fox", it, 4, fox_evac(it), fox_react(it))

            def gm_evac(j):
                act.wait_ge(evacuated, UNIT0["gm"] + j + 1)
                A(gg[:, j % 2], gg[:, j % 2], ACT.Silu).then_inc(sem("gate2_ready"), 1)

            def fill_o2(g):
                if g < 2:
                    act.wait_ge(sem("ca_o"), 8)
                else:
                    act.wait_ge(sem("o_gated"), 2 * g - 2)
                fill(CHUNK0["out"], g, y)
            units("gm", 0, 4, gm_evac, fox_react(4, mla=False))
            fill_o2(3)
            phase("out", 8, last=lambda g: None)
            A(smc(R2_COL), c1("eps"), ACT.Sqrt)
            norm_rms("post", D)

        @block.vector
        def _(dve):
            V = nc.vector

            def tt(out, a, b, op):
                return V.tensor_tensor(out, a, b, op)

            def split(c, per=0, it=0):
                if isinstance(it, int):
                    c, it, per = c + per * it, 0, 0
                    if c >= N_CHUNKS:
                        return
                s = c % SLOTS
                dve.wait_ge(hi_ready, per * it + (c + 1))
                tt(w_lo[:, s], raw[:, s], w_hi[:, s].bitcast(F32), ALU.subtract).then_inc(lo_ready, 1)

            def units(name, it, n, evac=None, react=None, K=KT, after=None):
                m = n * K // BLK
                for j in range(n):
                    for i in range(K // BLK):
                        if react is not None:
                            react(j, i)
                        if i == K // BLK - 1:
                            evac(j)
                        split(CHUNK0[name] + j * K // BLK + i + SLOTS, m, it)
                    if after is not None:
                        after(j)

            def done(name, it, n, j, K=KT):
                dve.wait_ge(w_used, n * K // BLK * it + (CHUNK0[name] + (j + 1) * K // BLK))
                return bank[(UNIT0[name] + j + (n * it if isinstance(it, int) else 0)) % 2]

            def copy_to(name, it, n, j, out, K=KT):
                b = done(name, it, n, j, K)
                V.tensor_copy(out, b[:, :, :]).then_inc(evacuated, 1)

            def both(a):
                return a[:, :].unsqueeze(1).to_broadcast([P, 2, S])

            def scale_to(name, it, n, j, out, by=rr):
                b = done(name, it, n, j)
                tt(out, b[:, :, :], both(by), ALU.mult).then_inc(evacuated, 1)

            def scale_tokens(b, out, column=R_COL):
                tt(out, b[:, :, :], smc(column, 2).unsqueeze(2).to_broadcast([P, 2, S]), ALU.mult)\
                    .then_inc(evacuated, 1)

            def scale_bank(name, it, n, j):
                b = done(name, it, n, j)
                tt(b[:, :, :], b[:, :, :], both(rr), ALU.mult).then_inc(sem("bank_scaled"), 1)
                return b

            def add_x(name, it, n, j, K=KT):
                b = done(name, it, n, j, K)
                t = x[:, sl(n * it + j + (n * it + j), 2)] if isinstance(it, int) else x[:, sl(2 * n * it + 2 * j, 2)]
                tt(t, b[:, :, :], t, ALU.add).then_inc(evacuated, 1)

            def rsqrt(name, out=rr, column=None):
                dve.wait_ge(sem("rms_ready"), NORM[name])
                if column is not None:
                    V.reciprocal(smc(column, 2), smc(column, 2))
                V.reciprocal(out[:, :], out[:, :]).then_inc(sem("rsqrt_ready"), 1)
                dve.wait_ge(sem("rsqrt_ready"), NORM[name])

            def fill_scaled(name, k0, k1, src, gain, hi_=h_hi, lo_=h_lo, at_=0):
                for k in range(k0, k1):
                    dve.wait_ge(sem("h_hi_ready"), HFILL[name] + k + 1)
                    V.scalar_tensor_tensor(lo_[:, at_ + k], src[:, k], gain(k), hi_[:, at_ + k].bitcast(F32),
                                           ALU.mult, ALU.subtract).then_inc(h_ready, 1)

            def fill_x(name, g):
                fill_scaled(name, 4 * g, 4 * g + 4, x, lambda k: col(name, k))

            def fill_y(name, g):
                for k in range(4 * g, 4 * g + 4):
                    dve.wait_ge(sem("h_hi_ready"), HFILL[name] + k + 1)
                    tt(h_lo[:, k], y[:, k], h_hi[:, k].bitcast(F32), ALU.subtract).then_inc(h_ready, 1)

            def phase(name, count, evac, n=2, first=None, last=None, K=KT, after=None, free=False, react0=None):
                def ev(it):
                    def e(j):
                        if first is not None and isinstance(it, int) and it == 0 and j == 0:
                            first()
                        evac(it, j)
                    return e

                def re(j, i):
                    g = i - 1 + 4 - K // BLK
                    if j == n - 1 and g >= 0:
                        last(g)
                def af(it):
                    return None if after is None else lambda j: after(it, j)
                its = count // n
                lo_ = 0 if first is None and react0 is None else 1
                up_ = its if last is None else its - 1
                if lo_:
                    units(name, 0, n, ev(0), react0, K=K, after=af(0))
                if up_ > lo_:
                    with dve.Fori(lo_, up_) as it:
                        units(name, it, n, ev(it), K=K, after=af(it))
                if last is not None and free:
                    def ev_last(j):
                        if j == n - 1:
                            last(3)
                        elif evac is not None:
                            evac(its - 1, j)
                    units(name, its - 1, n, ev_last, re, K=K)
                    if evac is not None:
                        evac(its - 1, n - 1)
                elif last is not None:
                    units(name, its - 1, n, ev(its - 1), re, K=K)
                    last(3)

            def taps(name, b, acc_, wcol, n, base, shifted=None):
                for q in range(2 * n):
                    tap, t = q // 2, q % 2
                    if tap:
                        dve.wait_ge(sem(name), base + (q - 1))
                    V.scalar_tensor_tensor(acc_[:, t, tap + 1:], b[:, t, :S - tap - 1], wcol(tap, t),
                                           acc_[:, t, tap + 1:], ALU.mult, ALU.add)\
                        .then_inc(*((evacuated, 1) if q == 2 * n - 1 and shifted is None else (sem(name), 1)))

            dve.wait_ge(sem("cols_in"), 16)
            for c in range(SLOTS):
                split(c)
                fill_x("mem", c)
            phase("xk", 8, lambda it, j: scale_to("xk", it, 2, j, kx[:, sl(4 * it + 2 * j, 2)]),
                  first=lambda: rsqrt("mem", column=R_COL))

            phase("xv", 8, lambda it, j: scale_tokens(done("xv", it, 2, j), vx[:, :, sl(512 * it + 256 * j, 256)]),
                  last=lambda g: fill_x("mix", g), free=True)
            split(CHUNK0["ba"] + SLOTS)
            r = rows
            dve.wait_ge(w_used, CHUNK0["ba"] + 2)
            rsqrt("mix")
            tt(r[:, 1], bank[UNIT0["ba"] % 2][:, 0], rr[:, :], ALU.mult).then_inc(evacuated, 1)
            split(CHUNK0["ba"] + SLOTS + 1)
            b_dve = sem("ba_dve")

            def ba_steps(j, i):
                if (j, i) == (0, 2):
                    dve.wait_ge(sem("ba_act"), 4)
                    V.tensor_scalar(r[0:8, 2], r[0:8, 2], 1.0, None, ALU.add).then_inc(b_dve, 1)
                    V.tensor_scalar(r[0:8, 3], r[0:8, 1], col("dtb", 0, slice(0, 8)), 0.0, ALU.add, ALU.max)\
                        .then_inc(b_dve, 1)
                elif (j, i) == (1, 0):
                    dve.wait_ge(sem("ba_act"), 5)
                    dve.wait_ge(b_dve, 2)
                    tt(r[0:8, 3], r[0:8, 3], r[0:8, 2], ALU.add).then_inc(b_dve, 1)
                    dve.wait_ge(b_dve, 3)
                    V.tensor_scalar(r[0:8, 3], r[0:8, 3], sm[0:8, EA_COL:EA_COL + 1], -1.0, ALU.mult, ALU.mult)\
                        .then_inc(b_dve, 1)
                    dve.wait_ge(b_dve, 4)
                    for n in range(2):
                        hs = slice(n * P, (n + 1) * P)
                        V.tensor_tensor_scan(r[0:8, 0, hs], ones[0:8, :], r[0:8, 3, hs], 0.0, ALU.mult, ALU.add)\
                            .then_inc(b_dve, 1)

            def qkv_evac(it):
                def evac(j):
                    b = scale_bank("qkv", it, 2, j)
                    dve.wait_ge(sem("qkv_tap0"), 4 * it + (2 * j + 2))
                    taps("qkv_taps", b, (cy, cz)[j],
                         lambda tap, t: col("gconv", 24 * (2 - tap) + (4 * it + (2 * j + t))), 3, 10 * it + 5 * j)
                return evac
            units("qkv", 0, 2, qkv_evac(0), ba_steps)
            with dve.Fori(1, 4) as it:
                units("qkv", it, 2, qkv_evac(it))
            dve.wait_ge(sem("ba_cols"), 2)
            V.tensor_copy(smc(G_COL, 16), pb[5][:, 0, 0:16]).then_inc(b_dve, 1)
            V.tensor_copy(smc(B_COL, 16), pb[4][:, 0, 0:16]).then_inc(b_dve, 1)
            units("qkv", 4, 2, qkv_evac(4))

            def head_rows(it, ahead=0):
                for i in range(2):
                    for p0 in (0, 32):
                        ps = slice(p0, p0 + 8)
                        V.tensor_scalar(r[ps, 2 + i], r[ps, 0],
                                        cst[ps, sl(CST["ident"] + p0 + i + 2 * ahead + 2 * it, 1)], None,
                                        ALU.mult).then_inc(sem("head_rows"), 1)

            def k_norm(j, i):
                if (j, i) == (0, 2):
                    dve.wait_ge(sem("k_rms"), 1)
                    V.reciprocal(smc(RK_COL, 16), smc(RK_COL, 16)).then_inc(sem("k_norm"), 1)
                elif (j, i) == (1, 1):
                    dve.wait_ge(sem("k_rows_copied"), 1)
                    tt(r[32:40, 0], r[32:40, 0], r[32:40, 1], ALU.mult).then_inc(sem("k_norm"), 1)
                    dve.wait_ge(sem("ba_act"), 6)
                    dve.wait_ge(b_dve, 8)
                    V.scalar_tensor_tensor(smc(NBEG_COL, 8), smc(B_COL + 8, 8), -1.0, smc(EG_COL, 8),
                                           ALU.mult, ALU.mult).then_inc(b_dve, 1)
                    dve.wait_ge(b_dve, 9)
                    dve.wait_ge(sem("k_norm"), 2)
                    tt(smc(NBEG_COL, 8), smc(NBEG_COL, 8), smc(RK_COL + 8, 8), ALU.mult).then_inc(b_dve, 1)
                    dve.wait_ge(b_dve, 10)
                    head_rows(0)
            units("qkv", 5, 2, qkv_evac(5), k_norm)

            def lev(l):
                return levT[:, l:l + 1, :].to_broadcast([P, 4, P])

            def level_part(l):
                tt(lv[:, :, :], lev(l + 1), aT[:, :, :], ALU.mult).then_inc(sem("level_part"), 1)

            def gdn(g, it):
                if g == 16 and not (isinstance(it, int) and it == 3):
                    head_rows(it, 1)
                elif g == 2:
                    dve.wait_ge(sem("rows_spread"), it + 1)
                    for b in range(4):
                        V.tensor_scalar(dec[:, b], pb4[2][:, b], smc(G_COL + (b % 2) * 8 + b // 2 + 2 * it), 0.0,
                                        ALU.subtract, ALU.min).then_inc(sem("dec_args"), 1)
                    for i in range(2):
                        tt(smc(KD_ARG + i), pb4[2][:, 2 * i, P - 1:P], smc(G_COL + i + 2 * it), ALU.subtract)\
                            .then_inc(sem("dec_args"), 1)
                    dve.wait_ge(sem("dec_ready"), it + 1)
                    dve.wait_ge(sem("grams"), it + 1)
                    for b in range(4):
                        a = V.scalar_tensor_tensor(aT[:, b], pb4[0][:, b],
                                                   smc(RK_COL + (b % 2) * 8 + b // 2 + 2 * it), dec[:, b],
                                                   ALU.mult, ALU.mult)
                    a.then_inc(sem("a_steps"), 1)
                    dve.wait_ge(sem("a_steps"), 2 * it + 1)
                    tt(aT[:, :, :], aT[:, :, :], pb4[3], ALU.mult).then_inc(sem("a_steps"), 1)
                    dve.wait_ge(sem("a_steps"), 2 * it + 2)
                    tt(lv[:, :, :], lev(0), aT[:, :, :], ALU.mult).then_inc(sem("inv0_part"), 1)
                    dve.wait_ge(sem("inv0_part"), it + 1)
                    tt(invT[:, :, :], ident.unsqueeze(1).to_broadcast([P, 4, P]), lv[:, :, :], ALU.subtract)\
                        .then_inc(sem("inv0_ready"), 1)
                    dve.wait_ge(sem("inv0_ready"), it + 1)
                    for b in range(4):
                        a = V.scalar_tensor_tensor(attT[:, b], pb4[1][:, b],
                                                   smc(RK_COL + (b % 2) * 8 + b // 2 + 2 * it), dec[:, b],
                                                   ALU.mult, ALU.mult)
                    a.then_inc(sem("att_ready"), 1)
                    level_part(0)
                    dve.wait_ge(sem("att_ready"), 3 * it + 1)
                    tt(attT[:, :, :], attT[:, :, :], causT.unsqueeze(1).to_broadcast([P, 4, P]), ALU.mult)\
                        .then_inc(sem("att_ready"), 1)
                    dve.wait_ge(sem("q_decay"), it + 1)
                    tt(qd[:, :, :], qn[:, :, P:2 * P], qd[:, :, :], ALU.mult).then_inc(sem("att_ready"), 1)
                elif 4 <= g < 16 and g % 2 == 0:
                    l = (g - 4) // 2
                    if l == 0:
                        dve.wait_ge(sem("k_decay"), it + 1)
                        dve.wait_ge(sem("kv_token_major"), it + 1)
                        for i in range(2):
                            a = V.tensor_scalar(kd[:, i], pb4[4][:, i], smc(KD_COL + i), smc(RK_COL + i + 2 * it),
                                                        ALU.mult, ALU.mult)
                        a.then_inc(sem("kd_ready"), 1)
                    if l < 5:
                        dve.wait_ge(sem("level_product"), 6 * it + (l + 1))
                        level_part(l + 1)
                elif 5 <= g < 16:
                    l = (g - 5) // 2
                    dve.wait_ge(sem("level_update"), 6 * it + (l + 1))
                    if l < 5:
                        tt(inv[:, :, :], inv[:, :, :], pb4[2], ALU.subtract).then_inc(sem("inv_updated"), 1)
                    tt(invT[:, :, :], invT[:, :, :], pb4[3], ALU.subtract).then_inc(sem("inv_updated"), 1)
                elif g == 18:
                    dve.wait_ge(sem("k_state"), it + 1)
                    for i in range(2):
                        V.scalar_tensor_tensor(r1[:, i], pb4[2][:, i], smc(NBEG_COL + i + 2 * it),
                                               vb[:, 2 * i + 1], ALU.mult, ALU.add).then_inc(sem("rest_ready"), 1)
                elif g == 20:
                    dve.wait_ge(sem("out_squares"), it + 1)
                    dve.wait_ge(sem("pair_ready"), 4 * it + 4)
                    V.scalar_tensor_tensor(osq[:, :, :], q2[:, :, :], EPS * P * P, osq[:, :, :],
                                           ALU.mult, ALU.add).then_inc(sem("out_mixed"), 1)
                elif g == 21:
                    dve.wait_ge(sem("out_rms"), it + 1)
                    V.reciprocal(osq[:, :, :], osq[:, :, :]).then_inc(sem("out_rsqrt"), 1)
                    dve.wait_ge(sem("out_rsqrt"), it + 1)
                    yy = y[:, sl(4 * it + 2, 2)]
                    V.scalar_tensor_tensor(yy, pb[4][:, :, :], col("ogain"), osq[:, :, :], ALU.mult, ALU.mult)\
                        .then_inc(sem("gdn_y"), 1)
                    dve.wait_ge(sem("gdn_y"), 2 * it + 1)
                    dve.wait_ge(sem("z_ready"), it + 1)
                    tt(yy, yy, zs[:, :], ALU.mult).then_inc(sem("gdn_y"), 1)

            def gdn_unit(it, fills=False):
                def react(j, i):
                    if (j, i) == (0, 0) and not (isinstance(it, int) and it == 0):
                        gdn(21, it - 1)
                    for s in (8 * j + 2 * i, 8 * j + 2 * i + 1):
                        if s in GDN_REACT:
                            gdn(GDN_REACT[s], it)
                    if fills and j == 3 and i > 0:
                        fill_y("y", i - 1)

                def evac(j):
                    if j < 3:
                        scale_to("gdn", it, 4, j, (zs, cy, cz)[j][:, :])
                        return
                    cs = sem("sc_scaled")
                    dve.wait_ge(evacuated, 4 * it + (UNIT0["gdn"] + 3))
                    tt(cz[:, :], cz[:, :], both(rr), ALU.mult).then_inc(cs, 1)
                    dve.wait_ge(cs, it + 1)
                    b = done("gdn", it, 4, j)
                    tt(cw[:, :], b[:, :, :], cz[:, :], ALU.mult).then_inc(evacuated, 1)

                def after(j):
                    if j == 3:
                        dve.wait_ge(sem("sc_tap0"), 2 * it + 2)
                        taps("sc_taps", cw, cv, lambda tap, t: col("sconv", 8 * (1 - tap) + (2 * it + t)), 2,
                             4 * it, shifted=True)
                        dve.wait_ge(sem("sc_taps"), 4 * it + 4)
                        tt(y[:, sl(4 * it, 2)], cv[:, :], cy[:, :], ALU.mult).then_inc(sem("sc_y"), 1)
                return react, evac, after

            react, evac, after = gdn_unit(0)
            units("gdn", 0, 4, evac, react, after=after)
            with dve.Fori(1, 3) as it:
                react, evac, after = gdn_unit(it)
                units("gdn", it, 4, evac, react, after=after)
            react, evac, after = gdn_unit(3, fills=True)
            units("gdn", 3, 4, evac, react, after=after)
            gdn(21, 3)

            def last_y(j, i):
                if (j, i) == (0, 0):
                    fill_y("y", 3)
                elif (j, i) == (0, 3):
                    dve.wait_ge(sem("x_again"), 16)
            phase("mixo", 8, lambda it, j: add_x("mixo", it, 2, j), last=lambda g: fill_x("xa", g),
                  react0=last_y)

            XSC = 512 ** -0.5

            def xa(a, h):
                if a == 0:
                    dve.wait_ge(sem("xa_scores"), h + 1)
                    V.tensor_reduce(smc(NMAX, 2), pb[0][:, :, :], AX.X, ALU.max, negate=True).then_inc(sem("xa_nmax"), 1)
                    dve.wait_ge(sem("xa_nmax"), 2 * h + 1)
                    V.tensor_scalar(smc(NMAX, 2), smc(NMAX, 2), XSC, None, ALU.mult).then_inc(sem("xa_nmax"), 1)
                    dve.wait_ge(sem("xa_exp"), 2 * h + 2)
                    V.reciprocal(smc(RINV, 2), smc(RSUM, 2)).then_inc(sem("xa_rinv"), 1)
                    dve.wait_ge(sem("xa_rinv"), h + 1)
                    for t in range(2):
                        V.tensor_scalar(pr[:, t], pr[:, t], smc(RINV + t), None, ALU.mult).then_inc(sem("xa_prob"), 1)
                elif a == 2:
                    dve.wait_ge(sem("xa_pv"), h + 1)
                    for q in range(2):
                        V.tensor_copy(y[:, sl(4 * h + 2 * q, 2)], pb[2 + q][:, :, :]).then_inc(sem("xa_o"), 1)

            def q_evac(it, j):
                if isinstance(it, int) and it == 0 and j == 0:
                    rsqrt("xa")
                scale_to("xq", it, 2, j, xq[:, 2 * j:2 * j + 2])
            units("xq", 0, 2, lambda j: q_evac(0, j))

            def xq_react(it):
                def react(j, i):
                    if (j, i) == (0, 0):
                        xa(0, it - 1)
                    elif (j, i) == (1, 0):
                        xa(2, it - 1)
                    elif isinstance(it, int) and j == 1:
                        fill_y("o", i - 1)
                return react
            with dve.Fori(1, 3) as it:
                units("xq", it, 2, lambda j: q_evac(it, j), xq_react(it))
            units("xq", 3, 2, lambda j: q_evac(3, j), xq_react(3))

            def last_head(j, i):
                if (j, i) == (0, 1):
                    xa(0, XH - 1)
                elif (j, i) == (0, 3):
                    xa(2, XH - 1)
                    fill_y("o", 3)
            phase("xo", 8, lambda it, j: add_x("xo", it, 2, j), react0=last_head,
                  last=lambda g: fill_x("ffn", g))
            tt(smc(GG_COL, KT), cols[:, COLS["fin"]:COLS["fin"] + KT], cols[:, COLS["pre"]:COLS["pre"] + KT],
               ALU.mult).then_inc(sem("gains_ready"), 1)
            dve.wait_ge(sem("gains_ready"), 1)
            tile0 = 0
            for s, nt in enumerate(SEGS):
                name = f"up{s}"
                g0 = sum(SEGS[:s]) // 2

                def evac(it, j):
                    b = scale_bank(name, it, 2, j)
                    dve.wait_ge(sem("up_tap0"), 4 * it + (4 * g0 + 2 * j + 2))
                    taps("up_taps", b, (cy, cw)[j],
                         lambda tap, t: col("fconv", 88 * (1 - tap) + 44 * j + tile0 + t + 2 * it), 2,
                         6 * it + (6 * g0 + 3 * j))
                    if j == 1:
                        dve.wait_ge(sem("gate_ready"), it + (g0 + 1))
                        dve.wait_ge(evacuated, 2 * it + (UNIT0[name] + 2))
                        tt(cv[:, :], cw[:, :], cz[:, :], ALU.mult).then_inc(sem("gated"), 1)

                def after(it, j):
                    if j == 1:
                        dve.wait_ge(sem("g_hi_ready"), it + (g0 + 1))
                        gt = sl(2 * it, 2)
                        tt(g_lo[:, gt], cv[:, :], g_hi[:, gt].bitcast(F32), ALU.subtract)\
                            .then_inc(sem("g_ready"), 1)
                phase(name, nt, evac, after=after, first=(lambda: rsqrt("ffn")) if s == 0 else None)
                tile0 += nt
                if nt == KT:
                    phase(f"down{s}", 8, lambda it, j: add_x(f"down{s}", it, 2, j))
                else:
                    phase(f"down{s}", 8, lambda it, j: add_x(f"down{s}", it, 4, j, K=nt), n=4, K=nt,
                          last=lambda g: fill_scaled("pre", 4 * g, 4 * g + 4, x, lambda k: smc(GG_COL + k)))

            pd = sem("pre_dve")
            m2 = smc(R2_COL, 2)

            def pre_norm():
                dve.wait_ge(sem("pre_rms"), 1)
                V.reciprocal(smc(RF_COL, 2), smc(RF_COL, 2))
                V.reciprocal(rf[:, :], rf[:, :]).then_inc(sem("pre_steps"), 1)
                dve.wait_ge(sem("pre_steps"), 1)
                tt(rr[:, :], pb[5][:, 1, :], rf[:, :], ALU.mult)
                tt(m2, pb[4][:, 0, 2:4], smc(RF_COL, 2), ALU.mult).then_inc(sem("pre_steps"), 1)
                dve.wait_ge(sem("pre_steps"), 2)
                tt(m2, m2, smc(RF_COL, 2), ALU.mult)
                tt(rr[:, :], rr[:, :], rf[:, :], ALU.mult).then_inc(pd, 1)
                dve.wait_ge(sem("rms_ready"), NORM["pre"])
                V.reciprocal(smc(R_COL, 2), smc(R_COL, 2))
                V.reciprocal(rr[:, :], rr[:, :]).then_inc(sem("rsqrt_ready"), 1)
                dve.wait_ge(sem("rsqrt_ready"), NORM["pre"])
                tt(smc(R_COL, 2), smc(R_COL, 2), smc(RF_COL, 2), ALU.mult)
                tt(rr[:, :], rr[:, :], rf[:, :], ALU.mult).then_inc(sem("pre_steps"), 1)
                dve.wait_ge(sem("pre_steps"), 3)

            rd = sem("rope_dve")

            def rope_angles():
                dve.wait_ge(sem("pos_in"), 16)
                V.tensor_copy(sinr[:, :], pos[:, :]).then_inc(rd, 1)
                dve.wait_ge(rd, 1)
                V.tensor_scalar(sinr[:, :], sinr[:, :], c1("invf"), None, ALU.mult).then_inc(rd, 1)
                dve.wait_ge(rd, 2)
                V.tensor_scalar(cosr[:, :], sinr[:, :], 1.0 / (2 * np.pi), MAGIC, ALU.mult, ALU.add).then_inc(rd, 1)
                dve.wait_ge(rd, 3)
                V.tensor_scalar(cosr[:, :], cosr[:, :], MAGIC, None, ALU.subtract).then_inc(rd, 1)
                for q in range(3):
                    dve.wait_ge(rd, 4 + q)
                    V.scalar_tensor_tensor(sinr[:, :], cosr[:, :], -TWO_PI[q], sinr[:, :], ALU.mult, ALU.add)\
                        .then_inc(rd, 1)
                dve.wait_ge(rd, 7)
                V.tensor_scalar(sinr[:, :], sinr[:, :], 3.1415925, -3.1415925, ALU.min, ALU.max).then_inc(rd, 1)

            def lat_react(it):
                def react(j, i):
                    if (it, j, i) == (0, 1, 2):
                        rope_angles()
                    elif it == 1:
                        if j == 0:
                            for k in range(4 * i, 4 * i + 4):
                                V.scalar_tensor_tensor(x[:, k], x[:, k], col("fin", k), rf[:, :], ALU.mult,
                                                       ALU.mult).then_inc(sem("x_final"), 1)
                        elif i == 0:
                            dve.wait_ge(sem("rope_act"), 3)
                            V.tensor_scalar(sinr[:, :], sinr[:, :], c1("sgn"), None, ALU.mult).then_inc(rd, 1)
                    elif (it, j) == (2, 0) and i in (1, 2):
                        dve.wait_ge(evacuated, UNIT0["lat"] + 3)
                        fill_scaled("gq", 4 * i - 4, min(4 * i, 6), lat, lambda k: col("gq", k), lh_hi, lh_lo)
                    elif (it, j, i) == (2, 1, 1):
                        dve.wait_ge(evacuated, UNIT0["lat"] + 5)
                        fill_scaled("gkv", 0, 4, lat[:, 6:10], lambda k: col("gkv", k), lh_hi, lh_lo, 6)
                return react

            def lat_evac(it, j):
                if (it, j) == (0, 0):
                    pre_norm()
                scale_to("lat", it, 2, j, lat[:, 4 * it + 2 * j:4 * it + 2 * j + 2])
            for it in range(3):
                units("lat", it, 2, lambda j: lat_evac(it, j), lat_react(it))
            def rope_key():
                dve.wait_ge(rd, 9)
                dve.wait_ge(evacuated, UNIT0["lat"] + 6)
                kd_ = sem("kr_dve")
                tt(kr[:, :], lat[:, 10], cosr[:, :], ALU.mult).then_inc(kd_, 1)
                dve.wait_ge(sem("kr_swap"), 2)
                tt(tn[:, 0], qm[:, :], sinr[:, :], ALU.mult).then_inc(kd_, 1)
                dve.wait_ge(kd_, 2)
                tt(kr[:, :], kr[:, :], tn[:, 0], ALU.add).then_inc(kd_, 1)

            fd = sem("forget_dve")

            def forget_first():
                dve.wait_ge(sem("forget_act"), 2)
                V.tensor_scalar(r[0:8, 2], r[0:8, 2], 1.0, None, ALU.add).then_inc(fd, 1)
                V.tensor_scalar(r[0:8, 3], lat[0:8, 11], col("bfor", 0, slice(0, 8)), 0.0, ALU.add, ALU.min)\
                    .then_inc(fd, 1)

            def forget_rest():
                dve.wait_ge(sem("forget_act"), 3)
                dve.wait_ge(fd, 2)
                tt(r[0:8, 3], r[0:8, 3], r[0:8, 2], ALU.subtract).then_inc(fd, 1)
                dve.wait_ge(fd, 3)
                V.tensor_tensor_scan(r[0:8, 0, 0:P], ones[0:8, :], r[0:8, 3, 0:P], 0.0, ALU.mult, ALU.add).then_inc(fd, 1)
                dve.wait_ge(fd, 4)
                V.tensor_copy(sm[0:8, EA_COL:EA_COL + 1], r[0:8, 0, P - 1:P]).then_inc(fd, 1)
                dve.wait_ge(fd, 5)
                V.tensor_tensor_scan(r[0:8, 0, P:S], ones[0:8, :], r[0:8, 3, P:S], sm[0:8, EA_COL:EA_COL + 1],
                                     ALU.mult, ALU.add).then_inc(fd, 1)

            def ca(a, kind, it):
                cd = sem("ca_logits")
                fox = kind == "fox"
                if a == -1:
                    for i in range(2):
                        if fox:
                            V.tensor_scalar(r[0:8, 2 + i], r[0:8, 0],
                                            cst[0:8, sl(CST["ident"] + i - 2 + 2 * it, 1)],
                                            None, ALU.mult).then_inc(sem("forget_rows"), 1)
                        else:
                            V.tensor_scalar(qmask[:, i], qrope[:, sl(it, 1)].rearrange("p a b -> p (a b)"),
                                            c1(f"head{i}"), None, ALU.mult).then_inc(sem("mla_q_masked"), 1)
                    return

                def n(k):
                    return 2 * k * it + (0 if fox else k)
                if a == 0:
                    if fox:
                        dve.wait_ge(sem("ca_scores"), n(1))
                        for i in range(2):
                            for t in range(2):
                                V.tensor_scalar(db[:, 2 * i + t], pb[2][:, i],
                                                smc(C_COL + 8 * t + i - 2 + 2 * it), -1.0,
                                                ALU.subtract, ALU.mult).then_inc(cd, 1)
                        dve.wait_ge(cd, 10 * it - 4)
                        for i in range(2):
                            tt(db[:, 2 * i:2 * i + 2], db[:, 2 * i:2 * i + 2], cmask, ALU.add).then_inc(cd, 1)
                        for i in range(2):
                            dve.wait_ge(cd, 10 * it + (i - 3))
                            V.scalar_tensor_tensor(db[:, 2 * i:2 * i + 2], pb[i][:, :, :], P ** -0.5,
                                                   db[:, 2 * i:2 * i + 2], ALU.mult, ALU.add).then_inc(cd, 1)
                        dve.wait_ge(cd, 10 * it)
                    else:
                        dve.wait_ge(sem("ca_scores"), n(1))
                        for i in range(2):
                            V.scalar_tensor_tensor(db[:, 2 * i:2 * i + 2], pb[i][:, :, :], 192 ** -0.5,
                                                   cmask, ALU.mult, ALU.add).then_inc(cd, 1)
                        dve.wait_ge(cd, 10 * it + 2)
                    V.tensor_reduce(smc(NMAX, 4), db[:, :, :], AX.X, ALU.max, negate=True).then_inc(sem("ca_nmax"), 1)
                    dve.wait_ge(sem("ca_exp"), n(4))
                    V.reciprocal(smc(RINV, 4), smc(RSUM, 4)).then_inc(sem("ca_rinv"), 1)
                    dve.wait_ge(sem("ca_rinv"), n(1))
                    for q in range(4):
                        V.tensor_scalar(pr2[:, q], pr2[:, q], smc(RINV + q), None, ALU.mult)\
                            .then_inc(sem("ca_prob"), 1)
                elif a == 1:
                    dve.wait_ge(sem("ca_turned"), n(1))
                    V.tensor_copy(pT2[:, 2:4], pb[4][:, :, :]).then_inc(sem("ca_prob_copied"), 1)
                else:
                    dve.wait_ge(sem("ca_pv"), n(1))
                    if fox:
                        dve.wait_ge(sem("fg_ready"), it)
                        tt(y[:, sl(2 * it - 2, 2)], pb[5][:, :, :], fg[:, :], ALU.mult).then_inc(sem("ca_o"), 1)
                    else:
                        V.tensor_scalar(y[:, sl(2 * it + 8, 2)], pb[5][:, :, :], 1.0, None, ALU.mult)\
                            .then_inc(sem("ca_o"), 1)

            rsqrt("gq", out=rq)

            def uq_evac(u):
                if u % 2:
                    dve.wait_ge(w_used, CHUNK0["uq"] + 6 * (u + 1) // BLK)
                else:
                    dve.wait_ge(sem("mid_chunk"), u // 2 + 1)
                to = qnope[:, 2 * u:2 * u + 2] if u < 4 else lat[:, 2 * u - 8:2 * u - 6]
                tt(to, bank[(UNIT0["uq"] + u) % 2][:, :, :], both(rq), ALU.mult).then_inc(evacuated, 1)
            u = 0
            for c in range(9):
                if c == 1:
                    rope_key()
                    forget_first()
                elif c == 2:
                    forget_rest()
                while u < 6 and (6 * (u + 1) - 1) // BLK == c:
                    uq_evac(u)
                    u += 1
                split(CHUNK0["uq"] + c + SLOTS)
            rsqrt("gkv", out=rkv, column=RKV_COL)
            qd_ = sem("qrope_ready")
            for u in range(8):
                if u in (2, 4):
                    for p in range(u - 2, u):
                        tt(qrope[:, p], lat[:, p], cosr[:, :], ALU.mult).then_inc(qd_, 1)
                        dve.wait_ge(sem("qr_swap"), 2 * p + 2)
                        tt(tn[:, p], tn[:, p], sinr[:, :], ALU.mult).then_inc(qd_, 1)
                        dve.wait_ge(qd_, 3 * p + 2)
                        tt(qrope[:, p], qrope[:, p], tn[:, p], ALU.add).then_inc(qd_, 1)
                dve.wait_ge(w_used, CHUNK0["ukv"] + u + 1)
                b = bank[(UNIT0["ukv"] + u) % 2]
                if u < 4:
                    tt(knope[:, 2 * u:2 * u + 2], b[:, :, :], both(rkv), ALU.mult).then_inc(evacuated, 1)
                else:
                    scale_tokens(b, vm[:, :, 256 * (u - 4):256 * (u - 3)], RKV_COL)
                split(CHUNK0["ukv"] + u + SLOTS)
            dve.wait_ge(sem("forget_cols"), 1)
            V.tensor_copy(smc(C_COL, 16), pb[2][:, 0, 0:16]).then_inc(fd, 1)
            dve.wait_ge(fd, 7)
            dve.wait_ge(qd_, 12)

            def fox_react(it, fox=True, mla=True):
                def react(j, i):
                    q = 4 * j + i
                    if q in CA_FOX and fox:
                        ca(CA_FOX[q], "fox", it)
                    elif q in CA_MLA and mla:
                        ca(CA_MLA[q], "mla", it)
                    elif not mla and j == 3 and i > 0:
                        fill_y("o2", i - 1)
                return react

            def fox_evac(it):
                def evac(j):
                    if j == 3:
                        scale_tokens(done("fox", it, 4, j), fv[:, :, :])
                    else:
                        scale_to("fox", it, 4, j, (fq, fk, fg)[j][:, :])
                return evac
            units("fox", 0, 4, fox_evac(0), fox_react(0, fox=False))
            with dve.Fori(1, 4) as it:
                units("fox", it, 4, fox_evac(it), fox_react(it))

            def gm_evac(j):
                if j >= 2:
                    dve.wait_ge(sem("o_gated"), j - 1)
                scale_to("gm", 0, 4, j, gg[:, j % 2])
                dve.wait_ge(sem("gate2_ready"), j + 1)
                yy = y[:, 8 + 2 * j:10 + 2 * j]
                tt(yy, yy, gg[:, j % 2], ALU.mult).then_inc(sem("o_gated"), 1)
            units("gm", 0, 4, gm_evac, fox_react(4, mla=False))
            fill_y("o2", 3)
            phase("out", 8, lambda it, j: copy_to("out", it, 2, j, y[:, sl(4 * it + 2 * j, 2)]), last=lambda g: None)
            dve.wait_ge(evacuated, UNIT0["out"] + 8)
            tt(acc2[:, :, :], y[:, 14:16], y[:, 14:16], ALU.mult).then_inc(sem("last_squares"), 1)
            rsqrt("post")
            od = sem("out_dve_steps")
            for j in range(6):
                if j < 5:
                    dve.wait_ge(sem("post_scaled"), j + 1)
                    yp = y[:, 2 * j:2 * j + 2]
                    tt(yp, yp, both(rr), ALU.mult).then_inc(od, 1)
                if j:
                    dve.wait_ge(od, j)
                    xp = x[:, 2 * j - 2:2 * j]
                    tt(xp, xp, y[:, 2 * j - 2:2 * j], ALU.add).then_inc(sem("out_dve"), 1)


def constants():
    c = np.zeros((P, N_CST), np.float32)
    i = np.arange(P)
    c[:, CST["ident"]:CST["ident"] + P] = np.eye(P)
    c[:, CST["ones"]:CST["ones"] + P] = 1
    c[:, CST["causT"]:CST["causT"] + P] = i[:, None] <= i[None, :]
    for l in range(NLEV):
        m = (i[:, None] >> l) + 1 == (i[None, :] >> l)
        m &= (i[None, :] >> l) % 2 == 1
        c[:, CST["levT"] + l * P:CST["levT"] + (l + 1) * P] = m
    for t in range(2):
        q, k = i[:, None] + t * P, np.arange(S)[None, :]
        c[:, CST["cmask"] + t * S:CST["cmask"] + (t + 1) * S] = np.where(k <= q, 0, NEG)
    c[:, CST["eps"]] = EPS
    c[:, CST["invf"]] = 10000.0 ** (-(i % 32) * 2.0 / 64)
    c[:, CST["sgn"]] = np.where(i < 64, -1, 1)
    c[:, CST["hpi"]] = np.pi / 2
    c[:, CST["epsq0"]] = EPS * EPS * P
    for h in range(2):
        c[:, CST[f"head{h}"]] = (i // 32) % 2 == h
    return c


def tiles(v):
    return np.asarray(v).reshape(-1, P).T


def feature_major(a):
    return np.ascontiguousarray(a.T.reshape(-1, P, a.shape[0]).transpose(1, 0, 2))


def stream_of(w):
    blocks = []

    def units(a, width=BW):
        k, n = a.shape
        blocks.append(a.reshape(k // P, P, n // width, width).transpose(2, 0, 1, 3).reshape(-1, P, width))

    def narrow(a):
        blocks.append(a.reshape(-1, 2, P, P).transpose(0, 2, 1, 3).reshape(-1, P, BW))

    def placed(n, parts):
        out = np.zeros((D, n), np.float32)
        for at_, a in parts:
            out[:, at_:at_ + a.shape[1]] = a
        return out

    mi, wi = w["w_mix_in"][0], w["w_in_2"][0]
    gw = 1024
    units(w["w_xk"][0])
    units(w["w_xv"][0])
    narrow(placed(P, [(0, mi[:, 4 * gw + 8:4 * gw + 16]), (32, mi[:, 4 * gw:4 * gw + 8])]))
    units(mi[:, :3 * gw])
    off = 4 * gw + 16
    for p in range(4):
        for base in (3 * gw, off, off + gw, off + 2 * gw):
            units(mi[:, base + p * BW:base + (p + 1) * BW])
    units(w["w_mix_out"][0].reshape(2, 4, BW, D)[::-1].transpose(1, 0, 2, 3).reshape(D, D))
    units(w["w_xq"][0])
    units(w["w_xo"][0])
    up, down = w["w_ffn_up"][0], w["w_ffn_down"][0]
    t0 = 0
    for nt in SEGS:
        for c in range(t0 * P, (t0 + nt) * P, BW):
            units(up[:, c:c + BW])
            units(up[:, FT * P + c:FT * P + c + BW])
        units(down[t0 * P:(t0 + nt) * P])
        t0 += nt
    units(wi[:, :1280])
    krope = wi[:, 1280:1344]
    f0 = 1344 + 4 * gw
    units(placed(BW, [(0, krope[:, :32]), (32, krope[:, :32]), (64, krope[:, 32:]), (96, krope[:, 32:]),
                      (P, wi[:, f0:f0 + 8])]))
    uq = w["w_uq_2"][0].reshape(768, 8, 192)
    units(np.ascontiguousarray(uq[:, :, :P]).reshape(768, -1))
    rope = uq[:, :, P:].reshape(768, 4, 2, 2, 32).transpose(0, 1, 3, 2, 4)
    units(np.ascontiguousarray(rope).reshape(768, -1))
    ukv = w["w_ukv_2"][0].reshape(512, 8, 256)
    units(np.ascontiguousarray(ukv[:, :, :P]).reshape(512, -1))
    units(np.ascontiguousarray(ukv[:, :, P:]).reshape(512, -1))
    for p in range(4):
        for base in (1344 + gw, 1344 + 2 * gw, f0 + 8, 1344 + 3 * gw):
            units(wi[:, base + p * BW:base + (p + 1) * BW])
    units(wi[:, 1344:1344 + gw])
    wo = w["w_out_2"][0]
    units(np.concatenate([wo[gw:], wo[:gw]]))
    b = np.concatenate(blocks)
    assert b.shape[0] == N_CHUNKS * BLK, (b.shape, N_CHUNKS)
    return np.ascontiguousarray(b.reshape(N_CHUNKS, BLK, P, BW).transpose(0, 2, 1, 3)).reshape(N_CHUNKS, P, BLK * BW)


def small_vectors(w):
    c = np.zeros((P, N_COLS), np.float32)

    def put(name, a):
        c[:a.shape[0], COLS[name]:COLS[name] + a.shape[1]] = a
    for name, key in (("mix", "mix_norm"), ("xa", "xattn_norm"), ("mem", "mem_norm"), ("ffn", "ffn_norm"),
                      ("pre", "g_pre_2"), ("post", "g_post_2"), ("gq", "g_q_latent_2"), ("gkv", "g_kv_latent_2"),
                      ("ogain", "gdn_out_norm"), ("gconv", "gdn_conv"), ("sconv", "sc_conv"), ("fconv", "ffn_conv")):
        put(name, tiles(np.asarray(w[key])[0].reshape(-1)))
    put("fin", tiles(w["final_norm"]))
    put("alog", np.asarray(w["gdn_a_log"])[0][:, None])
    put("dtb", np.asarray(w["gdn_dt_bias"])[0][:, None])
    put("bfor", np.asarray(w["b_forget_2"])[0][:, None])
    return c


def kernel(**inputs):
    from concourse import bacc
    from concourse.bass_utils import run_bass_kernel_spmd

    w = {k: np.asarray(v) for k, v in inputs.items()}
    arrays = {
        "weights": stream_of(w), "x_in": feature_major(w["x"][0]), "mem_in": feature_major(w["mem"][0]),
        "small_vectors": small_vectors(w), "constants": constants(),
        "positions": np.ascontiguousarray(w["positions_2"].reshape(1, S)),
    }
    nc = bacc.Bacc("TRN2", target_bir_lowering=False, num_devices=1)
    args = [nc.dram_tensor(n, a.shape, mybir.dt.from_np(a.dtype), kind="ExternalInput").ap()
            for n, a in arrays.items()]
    out = nc.dram_tensor("y_out", (P, KT, S), F32, kind="ExternalOutput").ap()
    build_program(nc, *args, out)
    r = run_bass_kernel_spmd(nc, [arrays], core_ids=[0])
    got = r.results[0]["y_out"]
    return np.ascontiguousarray(got.transpose(2, 1, 0)).reshape(1, S, D)
```
